# Optimizing a Trainium2 kernel written in Bass

```python
import jax, jax.numpy as jnp
from jax import lax
import numpy as np
import math

D_MODEL = 1024
BATCH = 1
SEQ = 512
DEPTH = 1

SSD_INNER = 2 * D_MODEL
SSD_HEAD_DIM = 64
SSD_HEADS = SSD_INNER // SSD_HEAD_DIM
SSD_GROUPS = 8
SSD_HEADS_PER_GROUP = SSD_HEADS // SSD_GROUPS
SSD_STATE = 128
SSD_CONV = 4
SSD_CHUNK = 128
SSD_CONV_DIM = SSD_INNER + 2 * SSD_GROUPS * SSD_STATE
SC_WIDTH = D_MODEL
SC_KERNEL = 3
N_EXPERTS = 64
TOP_K = 8
N_EXPERT_GROUPS = 8
TOPK_EXPERT_GROUPS = 4
D_EXPERT = 256
ROUTED_SCALE = 2.5
MOE_BLOCK = 128
LN_EPS = 1e-5
RMS_EPS = 1e-5
ALPHA = (2.0 * DEPTH) ** 0.25
BETA = (8.0 * DEPTH) ** -0.25
_IN_SIZES = (SSD_INNER, SSD_CONV_DIM, SSD_HEADS, SC_WIDTH, SC_WIDTH, SC_WIDTH, D_MODEL, D_MODEL)
IN_COLS = int(sum(_IN_SIZES))
IN_SPLITS = [int(v) for v in np.cumsum(_IN_SIZES)[:-1]]


def layer_norm(x):
    xf = x.astype(jnp.float32)
    mu = jnp.mean(xf, axis=-1, keepdims=True)
    xc = xf - mu
    var = jnp.mean(xc * xc, axis=-1, keepdims=True)
    return xc * lax.rsqrt(var + LN_EPS)

def causal_depthwise_conv(u, w):
    k = w.shape[0]
    return lax.conv_general_dilated(
        u, w[:, None, :].astype(u.dtype), window_strides=(1,), padding=[(k - 1, 0)],
        dimension_numbers=("NWC", "WIO", "NWC"), feature_group_count=u.shape[-1])

def gated_rmsnorm(y, z, w):
    g = y.astype(jnp.float32) * jax.nn.silu(z.astype(jnp.float32))
    g = g.reshape(*y.shape[:-1], SSD_GROUPS, -1)
    g = g * lax.rsqrt(jnp.mean(g * g, axis=-1, keepdims=True) + RMS_EPS)
    return g.reshape(y.shape) * w.astype(jnp.float32)

def ssd_chunked(xg, dt, A, Bg, Cg):
    b, s, g, r, p = xg.shape
    n = Bg.shape[-1]
    nc = s // SSD_CHUNK
    l = SSD_CHUNK
    X = (xg * dt[..., None]).reshape(b, nc, l, g, r, p)
    dA = (dt * A).reshape(b, nc, l, g, r).transpose(0, 1, 3, 4, 2)
    Bc = Bg.reshape(b, nc, l, g, n)
    Cc = Cg.reshape(b, nc, l, g, n)
    A_cs = jnp.cumsum(dA, axis=-1)
    seg = A_cs[..., :, None] - A_cs[..., None, :]
    causal = jnp.tril(jnp.ones((l, l), dtype=bool))
    Lmat = jnp.exp(jnp.where(causal, seg, -jnp.inf))
    CB = jnp.einsum("bclgn,bcsgn->bcgls", Cc, Bc)
    scores = CB[:, :, :, None] * Lmat
    y_diag = jnp.einsum("bcgrls,bcsgrp->bclgrp", scores, X)
    decay_states = jnp.exp(A_cs[..., -1:] - A_cs).transpose(0, 1, 4, 2, 3)
    states = jnp.einsum("bclgn,bclgrp->bcgrpn", Bc, X * decay_states[..., None])
    chunk_decay = jnp.exp(A_cs[..., -1])

    def step(h, inp):
        st, dec = inp
        return dec[..., None, None] * h + st, h

    h0 = jnp.zeros((b, g, r, p, n), jnp.float32)
    _, prev = lax.scan(step, h0, (states.transpose(1, 0, 2, 3, 4, 5).astype(jnp.float32),
                                  chunk_decay.transpose(1, 0, 2, 3)))
    prev = prev.transpose(1, 0, 2, 3, 4, 5)
    out_decay = jnp.exp(A_cs).transpose(0, 1, 4, 2, 3)
    y_off = jnp.einsum("bclgn,bcgrpn->bclgrp", Cc, prev) * out_decay[..., None]
    return (y_diag + y_off).reshape(b, s, g, r, p)

def hybrid_mixer(h, w_in, ssd_conv_w, ssd_conv_b, ssd_dt_bias, ssd_A_log, ssd_D, ssd_norm_w,
                 w_ssd_out, sc_conv_w, w_sc_out, w_o):
    b, s, _ = h.shape
    z, xbc, dt_raw, sc_b, sc_c, sc_h, gate_a, gate_b = jnp.split(h @ w_in, IN_SPLITS, axis=-1)
    xbc = jax.nn.silu(causal_depthwise_conv(xbc, ssd_conv_w) + ssd_conv_b)
    xs, Bm, Cm = jnp.split(xbc, [SSD_INNER, SSD_INNER + SSD_GROUPS * SSD_STATE], axis=-1)
    dt = jax.nn.softplus(dt_raw.astype(jnp.float32) + ssd_dt_bias.astype(jnp.float32))
    A = -jnp.exp(ssd_A_log.astype(jnp.float32))
    G, R = SSD_GROUPS, SSD_HEADS_PER_GROUP
    xg = xs.reshape(b, s, G, R, SSD_HEAD_DIM)
    y = ssd_chunked(xg, dt.reshape(b, s, G, R), A.reshape(G, R),
                    Bm.reshape(b, s, G, SSD_STATE), Cm.reshape(b, s, G, SSD_STATE))
    y = y + ssd_D.reshape(G, R)[:, :, None] * xg
    y = gated_rmsnorm(y.reshape(b, s, SSD_INNER), z, ssd_norm_w).astype(h.dtype)
    y_a = y @ w_ssd_out
    u = causal_depthwise_conv(sc_c * sc_h, sc_conv_w)
    y_b = (sc_b * u) @ w_sc_out
    merged = jax.nn.sigmoid(gate_a) * y_a + jax.nn.sigmoid(gate_b) * y_b
    return merged @ w_o

def moe_ffn(h, router_w, router_bias, w_gate, w_up, w_down, sh_gate, sh_up, sh_down):
    b, s, d = h.shape
    T = b * s
    hf = h.reshape(T, d)
    scores = jax.nn.sigmoid((hf @ router_w).astype(jnp.float32))
    biased = scores + router_bias.astype(jnp.float32)
    grp = biased.reshape(T, N_EXPERT_GROUPS, N_EXPERTS // N_EXPERT_GROUPS)
    grp_score = lax.top_k(grp, 2)[0].sum(-1)
    _, grp_idx = lax.top_k(grp_score, TOPK_EXPERT_GROUPS)
    grp_mask = jax.nn.one_hot(grp_idx, N_EXPERT_GROUPS, dtype=jnp.float32).sum(1) > 0
    expert_mask = jnp.repeat(grp_mask, N_EXPERTS // N_EXPERT_GROUPS, axis=1)
    _, e_idx = lax.top_k(jnp.where(expert_mask, biased, -jnp.inf), TOP_K)
    gate = jnp.take_along_axis(scores, e_idx, axis=1)
    gate = gate / jnp.sum(gate, axis=-1, keepdims=True) * ROUTED_SCALE
    n_assign = T * TOP_K
    nb = (n_assign + MOE_BLOCK - 1) // MOE_BLOCK + N_EXPERTS
    n_rows = nb * MOE_BLOCK
    e_flat = e_idx.reshape(-1)
    tok_flat = jnp.arange(n_assign, dtype=jnp.int32) // TOP_K
    order = jnp.argsort(e_flat)
    e_sorted = e_flat[order]
    tok_sorted = tok_flat[order]
    gate_sorted = gate.reshape(-1)[order]
    counts = jnp.bincount(e_flat, length=N_EXPERTS)
    padded = (counts + MOE_BLOCK - 1) // MOE_BLOCK * MOE_BLOCK
    start = jnp.cumsum(counts) - counts
    pend = jnp.cumsum(padded)
    pstart = pend - padded
    dest = pstart[e_sorted] + (jnp.arange(n_assign) - start[e_sorted])
    row_tok = jnp.full((n_rows,), T, jnp.int32).at[dest].set(tok_sorted)
    row_gate = jnp.zeros((n_rows,), jnp.float32).at[dest].set(gate_sorted)
    block_expert = jnp.minimum(
        jnp.searchsorted(pend, jnp.arange(nb) * MOE_BLOCK, side="right"), N_EXPERTS - 1)
    h_pad = jnp.concatenate([hf, jnp.zeros((1, d), hf.dtype)], axis=0)
    xin = h_pad[row_tok].reshape(nb, MOE_BLOCK, d)

    def expert_block(args):
        xb, e = args
        return (jax.nn.silu(xb @ w_gate[e]) * (xb @ w_up[e])) @ w_down[e]

    yb = lax.map(expert_block, (xin, block_expert)).reshape(n_rows, d)
    routed = jax.ops.segment_sum(yb * row_gate[:, None], row_tok, num_segments=T + 1)[:T]
    shared = (jax.nn.silu(hf @ sh_gate) * (hf @ sh_up)) @ sh_down
    return (routed + shared).reshape(b, s, d)

def first_inputs(seed: int = 0) -> dict:
    key = jax.random.key(seed)
    ks = jax.random.split(key, 32)
    L, D, E = DEPTH, D_MODEL, N_EXPERTS
    f32 = jnp.float32

    def nrm(k, shape, fan_in, scale=1.0):
        return jax.random.normal(k, shape, f32) * (scale * fan_in ** -0.5)

    u = jax.random.uniform(ks[5], (L, SSD_HEADS), f32)
    dt0 = jnp.exp(u * (np.log(0.1) - np.log(1e-3)) + np.log(1e-3))
    return {
        "x": jax.random.normal(ks[0], (BATCH, SEQ, D), f32),
        "c": jax.random.normal(ks[1], (BATCH, D), f32),
        "w_ada": nrm(ks[2], (L, D, 6 * D), D),
        "b_ada": 0.02 * jax.random.normal(ks[3], (L, 6 * D), f32),
        "w_in": nrm(ks[4], (L, D, IN_COLS), D),
        "ssd_conv_w": nrm(ks[6], (L, SSD_CONV, SSD_CONV_DIM), SSD_CONV),
        "ssd_conv_b": 0.02 * jax.random.normal(ks[7], (L, SSD_CONV_DIM), f32),
        "ssd_dt_bias": dt0 + jnp.log(-jnp.expm1(-dt0)),
        "ssd_A_log": jnp.log(jax.random.uniform(ks[8], (L, SSD_HEADS), f32, 1.0, 16.0)),
        "ssd_D": 1.0 + 0.1 * jax.random.normal(ks[9], (L, SSD_HEADS), f32),
        "ssd_norm_w": 1.0 + 0.1 * jax.random.normal(ks[10], (L, SSD_INNER), f32),
        "w_ssd_out": nrm(ks[11], (L, SSD_INNER, D), SSD_INNER, BETA),
        "sc_conv_w": nrm(ks[12], (L, SC_KERNEL, SC_WIDTH), SC_KERNEL),
        "w_sc_out": nrm(ks[13], (L, SC_WIDTH, D), SC_WIDTH, BETA),
        "w_o": nrm(ks[14], (L, D, D), D, BETA),
        "ln1_g": 1.0 + 0.1 * jax.random.normal(ks[15], (L, D), f32),
        "ln1_b": 0.02 * jax.random.normal(ks[16], (L, D), f32),
        "router_w": nrm(ks[17], (L, D, E), D),
        "router_bias": 0.01 * jax.random.normal(ks[18], (L, E), f32),
        "w_gate": nrm(ks[19], (L, E, D, D_EXPERT), D, BETA),
        "w_up": nrm(ks[20], (L, E, D, D_EXPERT), D, BETA),
        "w_down": nrm(ks[21], (L, E, D_EXPERT, D), D_EXPERT, BETA),
        "sh_gate": nrm(ks[22], (L, D, D_EXPERT), D, BETA),
        "sh_up": nrm(ks[23], (L, D, D_EXPERT), D, BETA),
        "sh_down": nrm(ks[24], (L, D_EXPERT, D), D_EXPERT, BETA),
        "ln2_g": 1.0 + 0.1 * jax.random.normal(ks[25], (L, D), f32),
        "ln2_b": 0.02 * jax.random.normal(ks[26], (L, D), f32),
    }

def first_block(x, c, w_ada, b_ada, w_in, ssd_conv_w, ssd_conv_b, ssd_dt_bias, ssd_A_log, ssd_D,
              ssd_norm_w, w_ssd_out, sc_conv_w, w_sc_out, w_o, ln1_g, ln1_b, router_w,
              router_bias, w_gate, w_up, w_down, sh_gate, sh_up, sh_down, ln2_g, ln2_b):
    dtype = x.dtype
    for l in range(DEPTH):
        mod = jax.nn.silu(c) @ w_ada[l] + b_ada[l]
        sh1, sc1, g1, sh2, sc2, g2 = jnp.split(mod[:, None, :], 6, axis=-1)
        h = (layer_norm(x) * (1.0 + sc1) + sh1).astype(dtype)
        mix = hybrid_mixer(h, w_in[l], ssd_conv_w[l], ssd_conv_b[l], ssd_dt_bias[l], ssd_A_log[l],
                           ssd_D[l], ssd_norm_w[l], w_ssd_out[l], sc_conv_w[l], w_sc_out[l], w_o[l])
        x = (layer_norm(ALPHA * x + g1 * mix) * ln1_g[l] + ln1_b[l]).astype(dtype)
        h = (layer_norm(x) * (1.0 + sc2) + sh2).astype(dtype)
        ffn = moe_ffn(h, router_w[l], router_bias[l], w_gate[l], w_up[l], w_down[l],
                      sh_gate[l], sh_up[l], sh_down[l])
        x = (layer_norm(ALPHA * x + g2 * ffn) * ln2_g[l] + ln2_b[l]).astype(dtype)
    return x


DEPTH_2 = 2

N_MIXERS = 2
N_A = (DEPTH_2 + 1) // 2
N_B = DEPTH_2 // 2
A_HEADS = 16
A_QK_DIM = 64
A_V_DIM = 64
A_KV_RANK = 256
IDX_HEADS = 8
IDX_DIM = 64
TOPK_MAX = 256
A_SPLITS = [A_HEADS * A_QK_DIM,
            A_HEADS * A_QK_DIM + A_KV_RANK,
            A_HEADS * A_QK_DIM + A_KV_RANK + IDX_HEADS * IDX_DIM,
            A_HEADS * A_QK_DIM + A_KV_RANK + IDX_HEADS * IDX_DIM + IDX_DIM]
A_IN = A_SPLITS[-1] + IDX_HEADS
B_HEADS = 8
B_HEAD_DIM = 64
B_QK = 2 * B_HEADS * B_HEAD_DIM
B_IN = 3 * B_QK
REL_BUCKETS = 32
REL_MAX_DIST = 128
BIAS_HEADS = A_HEADS
D_FF = 4 * D_MODEL
Q_BLOCK = 128
NEG = -1e30
DN_ALPHA = (2 * DEPTH_2) ** 0.25
DN_BETA = (8 * DEPTH_2) ** -0.25


def _layer_norm(x, g, b):
    xf = x.astype(jnp.float32)
    mu = jnp.mean(xf, -1, keepdims=True)
    var = jnp.mean(jnp.square(xf - mu), -1, keepdims=True)
    return ((xf - mu) * lax.rsqrt(var + LN_EPS)).astype(x.dtype) * g + b

def _rms_norm(x, g):
    xf = x.astype(jnp.float32)
    return (xf * lax.rsqrt(jnp.mean(xf * xf, -1, keepdims=True) + LN_EPS)).astype(x.dtype) * g

def _rel_bucket(dist):
    n = jnp.maximum(dist, 0)
    max_exact = REL_BUCKETS // 2
    nf = jnp.maximum(n, 1).astype(jnp.float32)
    large = max_exact + (jnp.log(nf / max_exact) / math.log(REL_MAX_DIST / max_exact)
                         * (REL_BUCKETS - max_exact)).astype(jnp.int32)
    large = jnp.minimum(large, REL_BUCKETS - 1)
    return jnp.where(n < max_exact, n, large)

def _to_blocks(a):
    B, S = a.shape[:2]
    return jnp.moveaxis(a.reshape(B, S // Q_BLOCK, Q_BLOCK, *a.shape[2:]), 1, 0)

def _from_blocks(a):
    nb, B, Q = a.shape[:3]
    return jnp.moveaxis(a, 0, 1).reshape(B, nb * Q, *a.shape[3:])

def _dsa_mixer(h, w_in, kv_norm, w_uk, w_uv, w_o, rel_bias):
    B, S, _ = h.shape
    topk = min(TOPK_MAX, S // 4)
    proj = h @ w_in
    q, ckv, iq, ik, iw = jnp.split(proj, A_SPLITS, axis=-1)
    q = q.reshape(B, S, A_HEADS, A_QK_DIM)
    ckv = _rms_norm(ckv, kv_norm)
    iq = iq.reshape(B, S, IDX_HEADS, IDX_DIM)
    iw = iw * (IDX_HEADS ** -0.5 * IDX_DIM ** -0.5)
    pos = jnp.arange(S, dtype=jnp.int32)

    def block(args):
        qb, iqb, iwb, tpos = args
        idx_logits = jnp.einsum('bqhd,bsd->bhqs', iqb, ik).astype(jnp.float32)
        score = jnp.einsum('bhqs,bqh->bqs', jax.nn.relu(idx_logits), iwb.astype(jnp.float32))
        causal = pos[None, :] <= tpos[:, None]
        score = jnp.where(causal[None], score, -jnp.inf)
        _, sel = lax.top_k(score, topk)
        valid = sel <= tpos[None, :, None]
        kv_sel = jax.vmap(lambda cb, ib: cb[ib])(ckv, sel)
        q_lat = jnp.einsum('bqhd,hdr->bqhr', qb, w_uk) * (A_QK_DIM ** -0.5)
        logits = jnp.einsum('bqhr,bqkr->bhqk', q_lat, kv_sel).astype(jnp.float32)
        bias = rel_bias[_rel_bucket(tpos[None, :, None] - sel)]
        logits = logits + jnp.transpose(bias, (0, 3, 1, 2))
        logits = jnp.where(valid[:, None], logits, NEG)
        p = jax.nn.softmax(logits, axis=-1).astype(h.dtype)
        o_lat = jnp.einsum('bhqk,bqkr->bqhr', p, kv_sel)
        return jnp.einsum('bqhr,hrd->bqhd', o_lat, w_uv)

    o = lax.map(block, (_to_blocks(q), _to_blocks(iq), _to_blocks(iw),
                        pos.reshape(S // Q_BLOCK, Q_BLOCK)))
    o = _from_blocks(o)
    return o.reshape(B, S, A_HEADS * A_V_DIM) @ w_o

def _diff_mixer(h, w_in, lam, subln_g, w_o, rel_bias, layer_idx):
    B, S, _ = h.shape
    lam_init = 0.8 - 0.6 * math.exp(-0.3 * layer_idx)
    proj = h @ w_in
    q, k, v = jnp.split(proj, 3, axis=-1)
    q = q.reshape(B, S, B_HEADS, 2, B_HEAD_DIM) * (B_HEAD_DIM ** -0.5)
    k = k.reshape(B, S, B_HEADS, 2, B_HEAD_DIM)
    v = v.reshape(B, S, B_HEADS, 2 * B_HEAD_DIM)
    lam_f = lam.astype(jnp.float32)
    lam_full = (jnp.exp(jnp.sum(lam_f[0] * lam_f[1])) - jnp.exp(jnp.sum(lam_f[2] * lam_f[3]))
                + lam_init)
    pos = jnp.arange(S, dtype=jnp.int32)

    def block(args):
        qb, tpos = args
        logits = jnp.einsum('bqhmd,bshmd->bhmqs', qb, k).astype(jnp.float32)
        bias = rel_bias[_rel_bucket(tpos[:, None] - pos[None, :])]
        bias = jnp.transpose(bias.reshape(Q_BLOCK, S, B_HEADS, 2), (2, 3, 0, 1))
        causal = pos[None, :] <= tpos[:, None]
        logits = jnp.where(causal, logits + bias, NEG)
        p = jax.nn.softmax(logits, axis=-1)
        a = p[:, :, 0] - lam_full * p[:, :, 1]
        return jnp.einsum('bhqs,bshe->bqhe', a.astype(h.dtype), v)

    o = _from_blocks(lax.map(block, (_to_blocks(q), pos.reshape(S // Q_BLOCK, Q_BLOCK))))
    o = _rms_norm(o, subln_g) * (1.0 - lam_init)
    return o.reshape(B, S, B_HEADS * 2 * B_HEAD_DIM) @ w_o

def _sqrelu_mlp(h, w1, w2):
    return jnp.square(jax.nn.relu(h @ w1)) @ w2

def second_inputs(seed: int = 0) -> dict:
    key = jax.random.key(seed)
    ks = jax.random.split(key, 20)
    nrm = lambda k, shape, s: jax.random.normal(k, shape, jnp.float32) * s
    D = D_MODEL
    b_w_in = nrm(ks[10], (N_B, D, B_IN), D ** -0.5)
    b_w_in = b_w_in.at[..., 2 * B_QK:].multiply(DN_BETA)
    return {
        'x': nrm(ks[0], (BATCH, SEQ, D), 1.0),
        'c': nrm(ks[1], (BATCH, D), 1.0),
        'rel_bias': nrm(ks[2], (REL_BUCKETS, BIAS_HEADS), 0.5),
        'ada_w': nrm(ks[3], (DEPTH_2, D, 6 * D), 0.1 * D ** -0.5),
        'ada_b': nrm(ks[4], (DEPTH_2, 6 * D), 0.01),
        'ln_g': 1.0 + nrm(ks[5], (DEPTH_2, 2, D), 0.02),
        'ln_b': nrm(ks[6], (DEPTH_2, 2, D), 0.02),
        'a_w_in': nrm(ks[7], (N_A, D, A_IN), D ** -0.5),
        'a_kv_norm': 1.0 + nrm(ks[8], (N_A, A_KV_RANK), 0.02),
        'a_w_uk': nrm(ks[9], (N_A, A_HEADS, A_QK_DIM, A_KV_RANK), A_KV_RANK ** -0.5),
        'a_w_uv': nrm(ks[11], (N_A, A_HEADS, A_KV_RANK, A_V_DIM), DN_BETA * A_KV_RANK ** -0.5),
        'a_w_o': nrm(ks[12], (N_A, A_HEADS * A_V_DIM, D), DN_BETA * (A_HEADS * A_V_DIM) ** -0.5),
        'b_w_in': b_w_in,
        'b_lambda': nrm(ks[13], (N_B, 4, B_HEAD_DIM), 0.1),
        'b_subln': 1.0 + nrm(ks[14], (N_B, 2 * B_HEAD_DIM), 0.02),
        'b_w_o': nrm(ks[15], (N_B, B_QK, D), DN_BETA * B_QK ** -0.5),
        'mlp_w1': nrm(ks[16], (DEPTH_2, D, D_FF), D ** -0.5),
        'mlp_w2': nrm(ks[17], (DEPTH_2, D_FF, D), DN_BETA * D_FF ** -0.5),
    }

def second_block(x, c, rel_bias, ada_w, ada_b, ln_g, ln_b,
              a_w_in, a_kv_norm, a_w_uk, a_w_uv, a_w_o,
              b_w_in, b_lambda, b_subln, b_w_o,
              mlp_w1, mlp_w2):
    mod = jnp.einsum('bd,lde->lbe', jax.nn.silu(c), ada_w) + ada_b[:, None]
    for i in range(DEPTH_2):
        sh_t, sc_t, g_t, sh_c, sc_c, g_c = [m[:, None] for m in jnp.split(mod[i], 6, axis=-1)]
        h = x * (1.0 + sc_t) + sh_t
        j = i // N_MIXERS
        if i % N_MIXERS == 0:
            y = _dsa_mixer(h, a_w_in[j], a_kv_norm[j], a_w_uk[j], a_w_uv[j], a_w_o[j], rel_bias)
        else:
            y = _diff_mixer(h, b_w_in[j], b_lambda[j], b_subln[j], b_w_o[j], rel_bias, i)
        x = _layer_norm(DN_ALPHA * x + (1.0 + g_t) * y, ln_g[i, 0], ln_b[i, 0])
        h = x * (1.0 + sc_c) + sh_c
        y = _sqrelu_mlp(h, mlp_w1[i], mlp_w2[i])
        x = _layer_norm(DN_ALPHA * x + (1.0 + g_c) * y, ln_g[i, 1], ln_b[i, 1])
    return x


def setup_inputs(seed=0):
    out = dict(first_inputs(seed))
    for name, value in second_inputs(seed + 1).items():
        if name != "x":
            out[name + "_2"] = value
    return out


def reference(
    x, c, w_ada, b_ada, w_in, ssd_conv_w, ssd_conv_b, ssd_dt_bias, ssd_A_log, ssd_D, ssd_norm_w,
    w_ssd_out, sc_conv_w, w_sc_out, w_o, ln1_g, ln1_b, router_w, router_bias, w_gate, w_up,
    w_down, sh_gate, sh_up, sh_down, ln2_g, ln2_b, c_2, rel_bias_2, ada_w_2, ada_b_2, ln_g_2,
    ln_b_2, a_w_in_2, a_kv_norm_2, a_w_uk_2, a_w_uv_2, a_w_o_2, b_w_in_2, b_lambda_2, b_subln_2,
    b_w_o_2, mlp_w1_2, mlp_w2_2,
):
    x = first_block(
        x, c, w_ada, b_ada, w_in, ssd_conv_w, ssd_conv_b, ssd_dt_bias, ssd_A_log, ssd_D,
        ssd_norm_w, w_ssd_out, sc_conv_w, w_sc_out, w_o, ln1_g, ln1_b, router_w, router_bias,
        w_gate, w_up, w_down, sh_gate, sh_up, sh_down, ln2_g, ln2_b,
    )
    return second_block(
        x, c_2, rel_bias_2, ada_w_2, ada_b_2, ln_g_2, ln_b_2, a_w_in_2, a_kv_norm_2, a_w_uk_2,
        a_w_uv_2, a_w_o_2, b_w_in_2, b_lambda_2, b_subln_2, b_w_o_2, mlp_w1_2, mlp_w2_2,
    )


_drawn_inputs = setup_inputs


def setup_inputs(seed=0):
    import zlib

    import numpy as np

    out = dict(_drawn_inputs(seed))
    spreads = {}
    factors = {'ssd_conv_b': 8.0,
     'ssd_D': 8.0,
     'ssd_norm_w': 3.74,
     'ada_b_2': 3.578,
     'a_kv_norm_2': 8.0,
     'b_subln_2': 8.0}
    for name, (base, spread) in spreads.items():
        noise = np.random.default_rng([zlib.crc32(name.encode()), seed]).standard_normal(out[name].shape)
        drawn = base * np.exp(spread * noise) if base else spread * noise
        out[name] = __import__('jax').numpy.asarray(drawn.astype(out[name].dtype))
    for name, factor in factors.items():
        out[name] = (out[name] * factor).astype(out[name].dtype)
    return out
```

```python
import math
from contextlib import ExitStack

import numpy as np

import concourse.bass as bass
from concourse import mybir

F32 = mybir.dt.float32
I32 = mybir.dt.int32
ALU = mybir.AluOpType
ACT = mybir.ActivationFunctionType
AX_X = mybir.AxisListType.X

P = 128
D = 1024
T = 512
KD = D // P
TT = T // P
NEG = -1e30
GONE = -3e38
FOUND = 1e30
NEWTON = 4

SSD_INNER = 2 * D
SSD_GROUPS = 8
SSD_HEADS = 32
HPG = SSD_HEADS // SSD_GROUPS
SSD_STATE = 128
HEAD = 64
GW = HPG * HEAD
Z0 = 0
XBC0 = SSD_INNER
B0 = XBC0 + SSD_INNER
C0 = B0 + SSD_GROUPS * SSD_STATE
DT0 = C0 + SSD_GROUPS * SSD_STATE
SCB0 = DT0 + SSD_HEADS
SCC0 = SCB0 + D
SCH0 = SCC0 + D
GA0 = SCH0 + D
GB0 = GA0 + D
N_EXPERTS = 64
D_EXPERT = 256
FE = D_EXPERT // P
ROUTED_SCALE = 2.5
EPS = 1e-5
ALPHA_1 = 2.0 ** 0.25
ALPHA_2 = 4.0 ** 0.25

KV_RANK = 256
Q0 = 0
CKV0 = 1024
IQ0 = 1280
IK0 = 1792
IW0 = 1856
IDX_HEADS = 8
IDX_DIM = 64
TOPK = 128
REL_BUCKETS = 32
REL_MAX_DIST = 128
HEADS = 16
D_FF = 4 * D
NVEC = T + P
LAM_INIT = 0.8 - 0.6 * math.exp(-0.3 * 1)


def bucket_onehot():
    dist = T - 1 - np.arange(NVEC)
    n = np.maximum(dist, 0)
    exact = REL_BUCKETS // 2
    nf = np.maximum(n, 1).astype(np.float32)
    large = exact + (np.log(nf / np.float32(exact)) / np.float32(math.log(REL_MAX_DIST / exact))
                     * np.float32(REL_BUCKETS - exact)).astype(np.int32)
    bucket = np.where(n < exact, n, np.minimum(large, REL_BUCKETS - 1))
    bucket = np.where(dist < 0, REL_BUCKETS, bucket)
    return (np.arange(REL_BUCKETS + 1)[:, None] == bucket[None, :]).astype(np.float32)


DSA_PAST = dict(pfree=24, proj=24, qkv=24, s_free=64, s=64, l=64, p=64, pn=64, tr=64 + 2, pT=64, pv=8,
                o_free=8, strip_free=8, strip_in=64)
NO_PAST = {name: 0 for name in DSA_PAST}


class Link:

    def __init__(self, eng, sem):
        self.eng, self.sem, self.base, self.k = eng, sem, 0, 0

    def mark(self, ins):
        self.k += 1
        ins.then_inc(self.sem, 1)

    def wait(self):
        self.eng.wait_ge(self.sem, self.base + self.k)

    def __call__(self, ins):
        self.mark(ins)
        self.wait()

    def enter(self, turn, each):
        self.start, self.each = self.base + self.k, each
        self.base, self.k = turn * each + self.start, 0

    def leave(self, turns):
        assert self.k == self.each, (self.k, self.each)
        self.base, self.k = self.start + turns * self.each, 0


class Slots:

    def __init__(self, stages, slots):
        self.at = {}
        fills, dmas = [0] * slots, [0] * slots
        for name, turns, units in stages:
            each_f, each_d = [0] * slots, [0] * slots
            entry = []
            for s, n in units:
                each_d[s] += n
                entry.append((s, fills[s] + each_f[s], dmas[s] + each_d[s]))
                each_f[s] += 1
            self.at[name] = [(s, f, each_f[s], d, each_d[s]) for s, f, d in entry]
            for s in range(slots):
                fills[s] += turns * each_f[s]
                dmas[s] += turns * each_d[s]

    def slot(self, name, u):
        return self.at[name][u][0]

    def free(self, name, u, turn):
        _, f, each, _, _ = self.at[name][u]
        return turn * each + (f + 1)

    def full(self, name, u, turn):
        _, _, _, d, each = self.at[name][u]
        return turn * (16 * each) + 16 * d


STAGES = [
    ("ada", 3, [(0, 1), (1, 1), (2, 1), (3, 1)]),
    ("short", 4, [(0, 3), (1, 3)]),
    ("ssd", 4, [(2, 3), (3, 1), (0, 3), (1, 1)]),
    ("merge", 4, [(2, 3), (3, 1), (0, 3), (1, 1)]),
    ("w_o", 1, [(2, 1), (3, 1)]),
    ("shared", 1, [(0, 2), (1, 1)]),
    ("moe", N_EXPERTS // 2, [(2, 2), (3, 1), (0, 2), (1, 1)]),
    ("index", 1, [(2, 4), (3, 1)]),
    ("dsa", 4, [(0, 4), (1, 4)]),
    ("a_w_o", 1, [(2, 1), (3, 1)]),
    ("up0", 2, [(0, 1), (1, 1), (2, 1), (3, 1)]),
    ("down0", 2, [(0, 1), (1, 1), (2, 1), (3, 1)]),
    ("diff", 4, [(0, 3), (1, 3)]),
    ("b_w_o", 1, [(2, 1), (3, 1)]),
    ("up1", 2, [(0, 1), (1, 1), (2, 1), (3, 1)]),
    ("down1", 2, [(0, 1), (1, 1), (2, 1), (3, 1)]),
]

INPUTS = [
    "x", "c", "w_ada", "b_ada", "w_in", "ssd_conv_w", "ssd_conv_b", "ssd_dt_bias", "ssd_A_log",
    "ssd_D", "ssd_norm_w", "w_ssd_out", "sc_conv_w", "w_sc_out", "w_o", "ln1_g", "ln1_b",
    "router_w", "router_bias", "w_gate", "w_up", "w_down", "sh_gate", "sh_up", "sh_down",
    "ln2_g", "ln2_b", "c_2", "rel_bias_2", "ada_w_2", "ada_b_2", "ln_g_2", "ln_b_2",
    "a_w_in_2", "a_kv_norm_2", "a_w_uk_2", "a_w_uv_2", "a_w_o_2", "b_w_in_2", "b_lambda_2",
    "b_subln_2", "b_w_o_2", "mlp_w1_2", "mlp_w2_2",
]


def program(nc, a, onehot, out):
    ctx = ExitStack()
    with ctx:
        def sb(name, shape):
            return ctx.enter_context(nc.sbuf_tensor(name, shape, F32))

        sems = {}

        def sem(name):
            if name not in sems:
                sems[name] = ctx.enter_context(nc.semaphore(name))
            return sems[name]

        w_in = a["w_in"][0].rearrange("(k p) n -> p k n", p=P)
        w_ada = a["w_ada"][0].rearrange("(k p) n -> p k n", p=P)
        w_ada_2 = a["ada_w_2"]
        w_ssd_out = a["w_ssd_out"][0].rearrange("(k p) n -> p k n", p=P)
        w_sc_out = a["w_sc_out"][0].rearrange("(k p) n -> p k n", p=P)
        w_o = a["w_o"][0].rearrange("(k p) n -> p k n", p=P)
        router_w = a["router_w"][0].rearrange("(k p) n -> p k n", p=P)
        w_gate = a["w_gate"][0].rearrange("e (k p) n -> e p k n", p=P)
        w_up = a["w_up"][0].rearrange("e (k p) n -> e p k n", p=P)
        w_down = a["w_down"][0].rearrange("e (k p) n -> e p k n", p=P)
        sh_gate = a["sh_gate"][0].rearrange("(k p) n -> p k n", p=P)
        sh_up = a["sh_up"][0].rearrange("(k p) n -> p k n", p=P)
        sh_down = a["sh_down"][0].rearrange("(k p) n -> p k n", p=P)
        a_w_in = a["a_w_in_2"][0].rearrange("(k p) n -> p k n", p=P)
        w_uk = a["a_w_uk_2"][0].rearrange("(j h) d r -> j (h d) r", h=2)
        w_uv = a["a_w_uv_2"][0].rearrange("h (k p) d -> p k h d", p=P)
        a_w_o = a["a_w_o_2"][0].rearrange("(k p) n -> p k n", p=P)
        b_w_in = a["b_w_in_2"][0].rearrange("(k p) n -> p k n", p=P)
        b_w_o = a["b_w_o_2"][0].rearrange("(k p) n -> p k n", p=P)
        mlp_w1 = [a["mlp_w1_2"][i].rearrange("(k p) n -> p k n", p=P) for i in range(2)]
        mlp_w2 = [a["mlp_w2_2"][i].rearrange("(k p) n -> p k n", p=P) for i in range(2)]
        x_in = a["x"][0].rearrange("(t p) d -> p t d", p=P)
        out_v = out[0].rearrange("(t p) d -> p t d", p=P)

        gates_dram = nc.dram_tensor("gates_dram", (N_EXPERTS, T), F32, kind="Internal").ap()
        bias_dram = nc.dram_tensor("bias_dram", (HEADS, NVEC), F32, kind="Internal").ap()

        strips_dram = nc.dram_tensor("strips_dram", (HEADS, P, T), F32, kind="Internal").ap()

        xr = sb("xr", [P, TT, D])
        hT = sb("hT", [P, KD, T])
        W = sb("W", [P, 4, 4096])
        R = sb("R", [P, 20736])
        ident = sb("ident", [P, P])
        tri = sb("tri", [P, P])
        cmask = sb("cmask", [P, P])
        ones = sb("ones", [P, P])
        prow = sb("prow", [P, 4, P])
        pcol = sb("pcol", [P, 4, P])
        mod = sb("mod", [P, 3 * 48])
        csil = sb("csil", [P, 16])
        lngb = sb("lngb", [P, 2, D])
        stats = sb("stats", [P, TT, 12])
        mv = sb("mv", [P, TT, 2])
        rstd = sb("rstd", [P, TT])
        rtmp = sb("rtmp", [P, 2, TT])
        ps = ctx.enter_context(nc.psum_tensor("ps", [P, 8, 512], F32))

        def rows(v):
            return v.rearrange("(j p) -> j p", p=P)

        small = [
            (prow[0:8, 0, :], rows(a["c"][0])),
            (prow[8:16, 0, :], rows(a["c_2"][0])),
            (prow[16:64, 0, :], rows(a["b_ada"][0])),
            (prow[0:96, 1, :], a["ada_b_2"].rearrange("l (j p) -> (l j) p", p=P)),
            (prow[0:128, 2, :], a["ssd_conv_w"][0].rearrange("k (j p) -> (k j) p", p=P)),
            (prow[0:32, 3, :], rows(a["ssd_conv_b"][0])),
            (prow[32:48, 3, :], rows(a["ssd_norm_w"][0])),
            (prow[48:72, 3, :], a["sc_conv_w"][0].rearrange("k (j p) -> (k j) p", p=P)),
            (prow[72:74, 3, :], rows(a["a_kv_norm_2"][0])),
            (prow[74:75, 3, :], rows(a["b_subln_2"][0])),
        ]
        PROWS = [64, 96, 128, 75]
        conv_w = pcol[:, 2, :].rearrange("p (k j) -> p k j", k=4)
        conv_b = pcol[:, 3, 0:32]
        norm_w = pcol[:, 3, 32:48]
        sc_w = pcol[:, 3, 48:72].rearrange("p (k j) -> p k j", k=3)
        kv_norm = pcol[:, 3, 72:74]
        subln = pcol[:, 3, 74:75]

        ring = Slots(STAGES, 4)
        landed = [sem(f"landed{i}") for i in range(4)]
        used = [sem(f"used{i}") for i in range(4)]

        def unit(name, u, at, *shape):
            n = int(np.prod(shape))
            v = W[:, ring.slot(name, u), at:at + n]
            if len(shape) == 2:
                return v.rearrange("p (a b) -> p a b", a=shape[0])
            if len(shape) == 3:
                return v.rearrange("p (a b c) -> p a b c", a=shape[0], b=shape[1])
            return v

        def view(base, at, *shape):
            n = int(np.prod(shape))
            v = base[:, at:at + n]
            if len(shape) == 2:
                return v.rearrange("p (a b) -> p a b", a=shape[0])
            if len(shape) == 3:
                return v.rearrange("p (a b c) -> p a b c", a=shape[0], b=shape[1])
            return v

        xflat = xr[:, :, :].rearrange("p t d -> p (t d)")
        lflat = lngb[:, :, :].rearrange("p a d -> p (a d)")

        xhat = view(R, 12288, TT, D)
        scuT = view(R, 0, KD, T)
        yT = view(R, 4096, 16, T)
        outT = view(R, 16384, KD, T)
        mixT = view(R, 4096, KD, T)
        mergedT = view(R, 12288, KD, T)
        sc_c = view(R, 12288, 2, T)
        sc_v = view(R, 13312, 2, T)
        sc_u = view(R, 14336, 2, T)
        mg = view(R, 16384, 2, 2, T)
        rw = view(R, 4096, KD, N_EXPERTS)
        rt = view(R, 4608, 6, TT, N_EXPERTS)
        r16 = view(R, 6144, 2, TT, 16)
        top = view(R, 6272, TT, 8 * 8)
        gateT = view(R, 6528, T)
        hexp = view(R, 0, 2 * FE, T)
        tg = view(R, 2048, FE, T)
        gateb = view(R, 3072, 2, T)
        adaw = view(R, 8192, KD, 384)
        h1T = view(R, 0, D_FF // P, T)
        oT = view(R, 0, KD, T)
        pT = view(R, 4096, 2, TT, T)
        qkv = [view(R, 8192 + 1536 * i, 3, T) for i in range(2)]
        lbuf = view(R, 11264, 4, T)
        strip = [view(R, 13312 + 1024 * i, 2, T) for i in range(2)]
        ckvT = view(R, 15360, 2, T)
        selm = view(R, 16384, TT, T)
        ukT = view(R, 18432, 2, P)
        onrm = view(R, 18688, TT, P)
        iqT = view(R, 4096, 4, T)
        ikT = view(R, 6144, T)
        rl = view(R, 6656, 2, T)
        ckvn = view(R, 8192, TT, KV_RANK)
        rbv = view(R, 4096, NVEC)
        oneh = view(R, 5120, NVEC)
        relb = view(R, 6144, HEADS)
        xsT = view(xflat, 0, 2, T)
        bcT = [view(xflat, 1024 + 1024 * i, 2, T) for i in range(2)]
        xtok = view(xflat, 3072, TT, GW)
        xdt = view(lflat, 0, TT, GW)
        wdt = view(lflat, 1024, KD, SSD_HEADS)
        acc = view(R, 12288, 2, T)
        th = view(R, 13312, 2, T)
        zs = [view(R, 14336 + 1024 * i, TT, GW) for i in range(2)]
        btok = view(R, 16384, TT, P)
        lm = [view(R, 16896 + 512 * i, HPG, P) for i in range(2)]
        xdd = view(R, 17920, TT, GW)
        y = view(R, 18944, TT, GW)
        state = view(R, 19968, GW)
        ytmp = view(R, 20224, GW)
        ysq = view(R, 20480, GW)
        cmaskq = sb("cmaskq", [P, P])
        lamb = sb("lamb", [P, 4, HEAD])
        lamv = sb("lamv", [P, 4])
        iws = sb("iws", [P, TT, IDX_HEADS])
        nmax = sb("nmax", [P, 8])
        rsum = sb("rsum", [P, 8])
        m8 = sb("m8", [P, 8])
        osq = sb("osq", [P, TT])
        ortmp = sb("ortmp", [P, 3, TT])
        dts = sb("dts", [P, 7, TT, SSD_HEADS])
        DT, DA, ACS, ODEC, DEC, CDEC, DSK = range(7)
        gs = [sb(f"gs{i}", [P, 7, TT, HPG]) for i in range(2)]
        dtw = sb("dtw", [P, 4, TT, SSD_HEADS])
        rowp = sb("rowp", [P, 3 * SSD_HEADS + N_EXPERTS])
        dtb, alog, dskip, rbias = (rowp[:, 0:32], rowp[:, 32:64], rowp[:, 64:96], rowp[:, 96:160])

        def spread(v, shape):
            return v.to_broadcast(shape)

        def slots(eng, proj, core, steps, links=None):
            def slot(pg, cg, par, turn):
                for k in range(steps):
                    if cg is not None:
                        core(k, cg, 1 - par)
                    if pg is not None:
                        proj(k, pg, par, turn)

            slot(0, None, 0, 0)
            with eng.Fori(0, 3) as i:
                if links:
                    links[0].enter(i, 2 * links[1])
                slot(i * 2 + 1, i * 2, 1, i)
                slot(i * 2 + 2, i * 2 + 1, 0, i + 1)
                if links:
                    links[0].leave(3)
            slot(7, 6, 1, 3)
            slot(None, 7, 0, 0)

        block = ctx.enter_context(nc.Block())

        @block.sync
        def _(sp):
            for i, (dst, src) in enumerate(small):
                sp.dma_start(dst, src).then_inc(sem("prow_in"), 16)
            sp.dma_start(xr[:, :, :], x_in).then_inc(sem("x_in"), 16)

            def fill(name, u, turn, *parts):
                s = ring.slot(name, u)
                sp.wait_ge(used[s], ring.free(name, u, turn))
                for dst, src in parts:
                    sp.dma_start(dst, src).then_inc(landed[s], 16)

            with sp.Fori(0, 3) as i:
                for u in range(4):
                    fill("ada", u, i, (unit("ada", u, 0, KD, 512),
                                       w_ada[:, :, bass.ds(i * 2048 + u * 512, 512)]))
            with sp.Fori(0, 4) as i:
                for u in range(2):
                    fill("short", u, i, *[
                        (unit("short", u, 1024 * n, KD, P), w_in[:, :, bass.ds(i * 256 + (c0 + u * P), P)])
                        for n, c0 in enumerate((SCB0, SCC0, SCH0))])
            with sp.Fori(0, 4) as i:
                for u in range(2):
                    w = unit("ssd", 2 * u, 0, KD, 512)
                    fill("ssd", 2 * u, i,
                         (w[:, :, 0:256], w_in[:, :, bass.ds(i * 512 + (XBC0 + u * GW), GW)]),
                         (w[:, :, 256:384], w_in[:, :, bass.ds(i * 256 + (B0 + u * P), P)]),
                         (w[:, :, 384:512], w_in[:, :, bass.ds(i * 256 + (C0 + u * P), P)]))
                    fill("ssd", 2 * u + 1, i,
                         (unit("ssd", 2 * u + 1, 0, KD, GW), w_in[:, :, bass.ds((i * 2 + u) * GW + Z0, GW)]))
            with sp.Fori(0, 4) as i:
                for u in range(2):
                    fill("merge", 2 * u, i,
                         (unit("merge", 2 * u, 0, KD, P), w_in[:, :, bass.ds(i * 256 + (GA0 + u * P), P)]),
                         (unit("merge", 2 * u, 1024, KD, P), w_in[:, :, bass.ds(i * 256 + (GB0 + u * P), P)]),
                         (unit("merge", 2 * u, 2048, KD, P), w_sc_out[:, :, bass.ds(i * 256 + u * P, P)]))
                    fill("merge", 2 * u + 1, i,
                         (unit("merge", 2 * u + 1, 0, 16, P), w_ssd_out[:, :, bass.ds(i * 256 + u * P, P)]))
            for u in range(2):
                fill("w_o", u, 0, (unit("w_o", u, 0, KD, 512), w_o[:, :, 512 * u:512 * u + 512]))
            sp.wait_ge(sem("ssd_y_T"), 2 * SSD_GROUPS)
            sp.dma_start(xr[:, :, :], x_in).then_inc(sem("x_in"), 16)
            fill("shared", 0, 0, (unit("shared", 0, 0, KD, D_EXPERT), sh_gate[:, :, :]),
                 (unit("shared", 0, 2048, KD, D_EXPERT), sh_up[:, :, :]))
            fill("shared", 1, 0, (unit("shared", 1, 0, FE, D), sh_down[:, :, :]))
            with sp.Fori(0, N_EXPERTS // 2) as i:
                sp.wait_ge(sem("adaw_used"), i + 1)
                src = bass.AP(w_ada_2.tensor, (i >> 4) * (D * 6 * D) + (i & 15) * 384,
                              [[6 * D, P], [P * 6 * D, KD], [1, 384]])
                sp.dma_start(adaw, src).then_inc(sem("adaw_in"), 16)
                for u in range(2):
                    e = i * 2 + u
                    fill("moe", 2 * u, i,
                         (unit("moe", 2 * u, 0, KD, D_EXPERT), w_gate[e]),
                         (unit("moe", 2 * u, 2048, KD, D_EXPERT), w_up[e]))
                    fill("moe", 2 * u + 1, i, (unit("moe", 2 * u + 1, 0, FE, D), w_down[e]))
                    sp.wait_ge(sem("gateb_free"), e + 1)
                    sp.dma_start(gateb[:, u, :], gates_dram[e].partition_broadcast(P)).then_inc(
                        sem(f"gateb_in{u}"), 16)
            fill("index", 0, 0,
                 (unit("index", 0, 0, KD, KV_RANK), a_w_in[:, :, CKV0:CKV0 + KV_RANK]),
                 (unit("index", 0, 2048, KD, IDX_HEADS), a_w_in[:, :, IW0:IW0 + IDX_HEADS]),
                 (unit("index", 0, 2112, KD, P)[:, :, 0:IDX_DIM], a_w_in[:, :, IK0:IK0 + IDX_DIM]),
                 (unit("index", 0, 2112, KD, P)[:, :, IDX_DIM:P], a_w_in[:, :, IK0:IK0 + IDX_DIM]))
            fill("index", 1, 0, (unit("index", 1, 0, KD, 512), a_w_in[:, :, IQ0:IQ0 + 512]))
            with sp.Fori(0, 4) as i:
                for u in range(2):
                    j = i * 2 + u
                    fill("dsa", u, i,
                         (unit("dsa", u, 0, KD, P), a_w_in[:, :, bass.ds(i * 256 + u * P, P)]),
                         (unit("dsa", u, 1024, KV_RANK), w_uk[j]),
                         *[(unit("dsa", u, 1280 + P * r, 2, HEAD), w_uv[:, r, bass.ds(j * 2, 2), :])
                           for r in range(2)])
            for u in range(2):
                fill("a_w_o", u, 0, (unit("a_w_o", u, 0, KD, 512), a_w_o[:, :, 512 * u:512 * u + 512]))

            def mlp(layer):
                with sp.Fori(0, 2) as i:
                    for u in range(4):
                        fill(f"up{layer}", u, i, (unit(f"up{layer}", u, 0, KD, 512),
                                                  mlp_w1[layer][:, :, bass.ds(i * 2048 + u * 512, 512)]))
                with sp.Fori(0, 2) as i:
                    for u in range(4):
                        fill(f"down{layer}", u, i, (unit(f"down{layer}", u, 0, D_FF // P, P),
                                                    mlp_w2[layer][:, :, bass.ds(i * 512 + u * P, P)]))

            mlp(0)
            with sp.Fori(0, 4) as i:
                for u in range(2):
                    fill("diff", u, i, *[
                        (unit("diff", u, 1024 * n, KD, P), b_w_in[:, :, bass.ds(i * 256 + (1024 * n + u * P), P)])
                        for n in range(3)])
            for u in range(2):
                fill("b_w_o", u, 0, (unit("b_w_o", u, 0, KD, 512), b_w_o[:, :, 512 * u:512 * u + 512]))
            mlp(1)
            for t in range(TT):
                sp.wait_ge(sem("res_x"), 5 * TT + t + 1)
                sp.dma_start(out_v[:, t, :], xr[:, t, :]).then_inc(sem("out_done"), 16)
            sp.wait_ge(sem("out_done"), 16 * TT)

        @block.gpsimd
        def _(pool):
            link = Link(pool, sem("pool_link"))
            link.mark(pool.memset(ident[:, :], 0.0))
            link.mark(pool.memset(tri[:, :], 1.0))
            link.mark(pool.memset(cmask[:, :], 0.0))
            link(pool.memset(ones[:, :], 1.0))
            pool.affine_select(out=ident[:, :], in_=ident[:, :], compare_op=ALU.not_equal, fill=1.0,
                               base=0, pattern=[[-1, P]], channel_multiplier=1).then_inc(sem("consts"), 1)
            pool.affine_select(out=tri[:, :], in_=tri[:, :], compare_op=ALU.is_ge, fill=0.0,
                               base=0, pattern=[[1, P]], channel_multiplier=-1).then_inc(sem("consts"), 1)
            pool.affine_select(out=cmask[:, :], in_=cmask[:, :], compare_op=ALU.is_ge, fill=NEG,
                               base=0, pattern=[[1, P]], channel_multiplier=-1).then_inc(sem("consts"), 1)
            pool.dma_start(wdt, w_in[:, :, DT0:DT0 + SSD_HEADS]).then_inc(sem("dt_in"), 16)
            for dst, src in ((dtb, a["ssd_dt_bias"]), (alog, a["ssd_A_log"]), (dskip, a["ssd_D"]),
                             (rbias, a["router_bias"])):
                pool.dma_start(dst, src[0].partition_broadcast(P)).then_inc(sem("dt_in"), 16)

            link(pool.memset(cmaskq[:, :], 0.0))
            pool.affine_select(out=cmaskq[:, :], in_=cmaskq[:, :], compare_op=ALU.is_ge, fill=NEG,
                               base=0, pattern=[[-1, P]], channel_multiplier=1).then_inc(sem("cmaskq"), 1)
            pool.dma_start(oneh[0:REL_BUCKETS + 1, :], onehot).then_inc(sem("bias_in"), 16)
            link(pool.memset(relb[0:64, :], NEG))
            pool.dma_start(relb[0:REL_BUCKETS, :], a["rel_bias_2"]).then_inc(sem("bias_in"), 16)
            pool.dma_start(lamb[:, :, :], a["b_lambda_2"][0].partition_broadcast(P)).then_inc(sem("lam_in"), 16)
            pool.wait_ge(sem("bias_v"), 2)
            pool.dma_start(bias_dram, rbv[0:HEADS, :]).then_inc(sem("bias_out"), 16)
            pool.wait_ge(sem("bias_out"), 16)
            for h in range(0, HEADS, 4):
                pool.dma_start(strips_dram[h:h + 4], bass.AP(bias_dram.tensor, h * NVEC + P - 1,
                                                             [[NVEC, 4], [-1, P], [1, T]])).then_inc(sem("strips_out"), 16)

            def gains(n, g, b, sem_name, count):
                pool.wait_ge(sem(sem_name), count)
                pool.dma_start(lngb[:, 0, :], g.partition_broadcast(P)).then_inc(sem("ln_in"), 16)
                pool.dma_start(lngb[:, 1, :], b.partition_broadcast(P)).then_inc(sem("ln_in"), 16)

            gains(0, a["ln1_g"][0], a["ln1_b"][0], "ssd_y_T", 2 * SSD_GROUPS)
            pool.wait_ge(sem("merge_y"), 8)
            pool.wait_ge(sem("res_b"), 1 * TT)
            pool.dma_start(rw, router_w).then_inc(sem("rw_in"), 16)
            pool.wait_ge(sem("gates_T"), 1)
            pool.dma_start(gates_dram, gateT[0:N_EXPERTS, :]).then_inc(sem("gates_out"), 16)
            pool.wait_ge(sem("gates_out"), 16)
            gains(1, a["ln2_g"][0], a["ln2_b"][0], "res_x", 1 * TT)
            pool.sem_inc(sem("gateb_free"), 2)
            with pool.Fori(0, N_EXPERTS // 2) as i:
                for u in range(2):
                    e = i * 2 + u
                    pool.wait_ge(sem(f"gateb_in{u}"), i * 16 + 16)
                    for f in range(FE):
                        pool.wait_ge(sem("moe_h"), e * 2 + (f + 1))
                        if f == 0 and u == 0:
                            pool.wait_ge(sem("hexp_free"), i + 1)
                        pool.tensor_tensor(hexp[:, FE * u + f, :], tg[:, f, :], gateb[:, u, :],
                                           ALU.mult).then_inc(sem("moe_hg"), 1)
                    pool.wait_ge(sem("moe_hg"), e * 2 + 4)
                    pool.sem_inc(sem("gateb_free"), 1)

            def strips(past):
                with pool.Fori(0, 4) as i:
                    for u in range(2):
                        c = i * 2 + u
                        pool.wait_ge(sem("att_strip_free"), c + 1 + past["strip_free"])
                        src = strips_dram[bass.ds(c * 2, 2)].rearrange("h q s -> q h s")
                        pool.dma_start(strip[u], src).then_inc(sem(f"strip_in{u}"), 16)

            gains(2, a["ln_g_2"][0, 0], a["ln_b_2"][0, 0], "res_x", 2 * TT)
            pool.wait_ge(sem("moe_out"), 1)
            pool.wait_ge(sem("strips_out"), 64)
            strips(NO_PAST)
            gains(3, a["ln_g_2"][0, 1], a["ln_b_2"][0, 1], "res_x", 3 * TT)
            gains(4, a["ln_g_2"][1, 0], a["ln_b_2"][1, 0], "res_x", 4 * TT)
            strips(DSA_PAST)
            gains(5, a["ln_g_2"][1, 1], a["ln_b_2"][1, 1], "res_x", 5 * TT)

        @block.tensor
        def _(pe):
            mm = nc.tensor.matmul
            for s in range(4):
                pe.sem_inc(used[s], 1)

            def have(name, u, turn=0):
                pe.wait_ge(landed[ring.slot(name, u)], ring.full(name, u, turn))

            def spent(ins, name, u):
                ins.then_inc(used[ring.slot(name, u)], 1)

            pe.wait_ge(sem("consts"), 3)
            pe.wait_ge(sem("prow_in"), 16 * len(small))
            for n, r in enumerate(PROWS):
                last = nc.tensor.transpose(ps[:, n, 0:r], prow[0:r, n, :], ident[0:r, 0:r])
            last.then_inc(sem("pcol_T"), 1)

            pe.wait_ge(sem("bias_in"), 32)
            mm(ps[0:HEADS, 5, :], relb[0:REL_BUCKETS + 1, :], oneh[0:REL_BUCKETS + 1, 0:512], start=True, stop=True)
            mm(ps[0:HEADS, 6, 0:P], relb[0:REL_BUCKETS + 1, :], oneh[0:REL_BUCKETS + 1, 512:NVEC],
               start=True, stop=True).then_inc(sem("bias_p"), 1)

            pe.wait_ge(sem("csil"), 1)
            with pe.Fori(0, 3) as i:
                pe.wait_ge(sem("ada_free"), i + 1)
                for u in range(4):
                    have("ada", u, i)
                    w = unit("ada", u, 0, KD, 512)
                    for j in range(4):
                        for k in range(KD):
                            last = mm(ps[:, 4, 4 * u + j:4 * u + j + 1], w[:, k, j * P:(j + 1) * P],
                                      csil[:, k:k + 1], start=(k == 0), stop=(k == KD - 1))
                    spent(last, "ada", u)

            def to_T(n, src, src_ready, base=0):
                for t in range(TT):
                    pe.wait_ge(sem(src_ready), base + t + 1)
                    for k in range(KD):
                        last = nc.tensor.transpose(ps[:, k, t * P:(t + 1) * P],
                                                   src[:, t, k * P:(k + 1) * P], ident[:, :])
                last.then_inc(sem("hT_turned"), 1)

            pe.wait_ge(sem("pcol_ready"), 1)
            pe.wait_ge(sem("ada_free"), 1 + 3)
            pe.wait_ge(sem("bias_v"), 2)
            to_T(0, xhat, "ln0_x")

            pe.wait_ge(sem("hT_ready"), 1 * KD)
            with pe.Fori(0, 4) as i:
                for u in range(2):
                    have("short", u, i)
                    pe.wait_ge(sem("short_free"), i * 2 + (u + 1))
                    for n in (1, 2, 0):
                        w = unit("short", u, 1024 * n, KD, P)
                        for k in range(KD):
                            last = mm(ps[:, 3 * u + n, :], w[:, k, :], hT[:, k, :],
                                      start=(k == 0), stop=(k == KD - 1))
                        if n:
                            last.then_inc(sem("short_p"), 1)
                    spent(last, "short", u)

            pe.wait_ge(sem("dt_in"), 80)
            for t in range(TT):
                for k in range(KD):
                    last = mm(ps[:, 6, t * SSD_HEADS:(t + 1) * SSD_HEADS], hT[:, k, t * P:(t + 1) * P],
                              wdt[:, k, :], start=(k == 0), stop=(k == KD - 1))
            last.then_inc(sem("dt_p"), 1)
            pe.wait_ge(sem("da_ready"), 1)
            for t in range(TT):
                mm(ps[:, 7, t * SSD_HEADS:(t + 1) * SSD_HEADS], tri[:, :], dts[:, DA, t, :], start=True, stop=True)
                last = mm(ps[:, 7, P + t * SSD_HEADS:P + (t + 1) * SSD_HEADS], ones[:, :], dts[:, DA, t, :],
                          start=True, stop=True)
            last.then_inc(sem("acs_p"), 1)
            pe.wait_ge(sem("dts_ready"), 1)
            pe.wait_ge(sem("short_free"), 2 + 8)

            def ssd_proj(k, g, par, turn):
                u = 2 * par
                if k == 0:
                    have("ssd", u, turn)
                if k == 4:
                    have("ssd", u + 1, turn)
                pe.wait_ge(sem("ssd_b01_free"), g * 6 + (k + 1))
                if k < 4:
                    w = unit("ssd", u, 0, KD, 512)
                    for kk in range(KD):
                        last = mm(ps[:, k % 2, :], w[:, kk, k * P:(k + 1) * P], hT[:, kk, :],
                                  start=(kk == 0), stop=(kk == KD - 1))
                else:
                    w = unit("ssd", u + 1, 0, KD, GW)
                    for h in range(2):
                        t = 2 * (k - 4) + h
                        for kk in range(KD):
                            last = mm(ps[:, k % 2, h * GW:(h + 1) * GW], hT[:, kk, t * P:(t + 1) * P],
                                      w[:, kk, :], start=(kk == 0), stop=(kk == KD - 1))
                last.then_inc(sem("ssd_proj"), 1)
                if k == 3:
                    pe.wait_ge(sem("ssd_proj"), g * 6 + 4)
                    pe.sem_inc(used[ring.slot("ssd", u)], 1)
                if k == 5:
                    pe.wait_ge(sem("ssd_proj"), g * 6 + 6)
                    pe.sem_inc(used[ring.slot("ssd", u + 1)], 1)

            def ssd_core(k, g, par):
                b, c = bcT[par][:, 0, :], bcT[par][:, 1, :]
                if k == 0:
                    pe.wait_ge(sem("ssd_silu"), g * 4 + 4)
                    pe.wait_ge(sem("ssd_b23_free"), g * 6 + 1)
                    for t in range(TT):
                        q = slice(t * P, (t + 1) * P)
                        nc.tensor.transpose(ps[:, 2, q], xsT[:, 0, q], ident[:, :])
                        nc.tensor.transpose(ps[:, 3, q], xsT[:, 1, q], ident[:, :])
                        last = nc.tensor.transpose(ps[:, 4, q], b[:, q], ident[:, :])
                    last.then_inc(sem("ssd_xb_T"), 1)
                    for t in range(TT):
                        q = slice(t * P, (t + 1) * P)
                        last = mm(ps[:, 5, q], b[:, q], c[:, q], start=True, stop=True)
                    last.then_inc(sem("ssd_cb"), 1)
                if 1 <= k <= 4:
                    t = k - 1
                    pe.wait_ge(sem("ssd_lm"), g * 4 + (t + 1))
                    pe.wait_ge(sem("ssd_x"), g * 2 + 2)
                    pe.wait_ge(sem("ssd_y_free"), g * 4 + (t + 1))
                    for h in range(HPG):
                        last = mm(ps[:, 6, h * HEAD:(h + 1) * HEAD], lm[t % 2][:, h, :],
                                  xdt[:, t, h * HEAD:(h + 1) * HEAD], start=True, stop=True)
                    if t > 0:
                        pe.wait_ge(sem("ssd_state"), g * 3 + t)
                        last = mm(ps[:, 6, GW:2 * GW], c[:, t * P:(t + 1) * P], state, start=True, stop=True)
                    if t < TT - 1:
                        last = mm(ps[:, 7, 0:GW], btok[:, t, :], xdd[:, t, :], start=True, stop=True)
                    last.then_inc(sem("ssd_y_p"), 1)
                if k <= 3:
                    t = k
                    pe.wait_ge(sem("ssd_gs"), g + 1)
                    pe.wait_ge(sem("ssd_b23_free"), g * 6 + (t + 2))
                    for h in range(HPG):
                        last = mm(ps[:, 2 + t % 2, h * P:(h + 1) * P],
                                  gs[par][:, DA, t, h:h + 1].to_broadcast([P, P]), tri[:, :],
                                  start=True, stop=True)
                    last.then_inc(sem("ssd_rowb"), 1)
                if k == 5:
                    pe.wait_ge(sem("ssd_yn"), g * 4 + 4)
                    pe.wait_ge(sem("ssd_b23_free"), g * 6 + 6)
                    for m in range(2):
                        for t in range(TT):
                            last = nc.tensor.transpose(ps[:, 2 + m, t * P:(t + 1) * P],
                                                       y[:, t, m * P:(m + 1) * P], ident[:, :])
                    last.then_inc(sem("ssd_y_p5"), 1)

            slots(pe, ssd_proj, ssd_core, 6)

            pe.wait_ge(sem("ssd_y_T"), 2 * SSD_GROUPS)
            pe.wait_ge(sem("ssd_b01_free"), 2 + 6 * SSD_GROUPS)
            with pe.Fori(0, 4) as i:
                for u in range(2):
                    have("merge", 2 * u, i)
                    pe.wait_ge(sem("merge_free"), i * 2 + (u + 1))
                    for n, rhs in enumerate((hT, hT, scuT)):
                        w = unit("merge", 2 * u, 1024 * n, KD, P)
                        for k in range(KD):
                            last = mm(ps[:, 4 * u + n, :], w[:, k, :], rhs[:, k, :],
                                      start=(k == 0), stop=(k == KD - 1))
                        if n < 2:
                            last.then_inc(sem("merge_g"), 1)
                    spent(last, "merge", 2 * u)
                    have("merge", 2 * u + 1, i)
                    w = unit("merge", 2 * u + 1, 0, 16, P)
                    for k in range(16):
                        last = mm(ps[:, 4 * u + 3, :], w[:, k, :], yT[:, k, :],
                                  start=(k == 0), stop=(k == 15))
                    last.then_inc(sem("merge_y"), 1)
                    pe.wait_ge(sem("merge_y"), i * 2 + (u + 1))
                    pe.sem_inc(used[ring.slot("merge", 2 * u + 1)], 1)

            def project(n, name, rhs, ready, count):
                pe.wait_ge(sem(ready), count)
                for u in range(2):
                    have(name, u)
                    w = unit(name, u, 0, KD, 512)
                    for j in range(4):
                        for k in range(KD):
                            last = mm(ps[:, 4 * u + j, :], w[:, k, j * P:(j + 1) * P], rhs[:, k, :],
                                      start=(k == 0), stop=(k == KD - 1))
                        if j < 3:
                            last.then_inc(sem("branch_p"), 1)
                    spent(last, name, u)

            def from_T(n, src):
                pe.wait_ge(sem("branch_ready"), (n + 1) * KD)
                for t in range(TT):
                    for k in range(KD):
                        last = nc.tensor.transpose(ps[:, 2 * t + k // 4, (k % 4) * P:(k % 4 + 1) * P],
                                                   src[:, k, t * P:(t + 1) * P], ident[:, :])
                    last.then_inc(sem("res_b"), 1)

            project(0, "w_o", mergedT, "merge_free", 2 + 8)
            from_T(0, mixT)
            pe.wait_ge(sem("res_x"), 1 * TT)
            to_T(1, xhat, "ln1_x")

            pe.wait_ge(sem("rw_in"), 16)
            pe.wait_ge(sem("hT_ready"), 2 * KD)
            for t in range(TT):
                for k in range(KD):
                    last = mm(ps[:, 0, t * N_EXPERTS:(t + 1) * N_EXPERTS], hT[:, k, t * P:(t + 1) * P],
                              rw[:, k, :], start=(k == 0), stop=(k == KD - 1))
            last.then_inc(sem("router_p"), 1)

            def gate_up(w, first, free, count, tag):
                for f in range(FE):
                    pe.wait_ge(sem(free), count(f))
                    for n in range(2):
                        for k in range(KD):
                            last = mm(ps[:, first + 2 * f + n, :], w[:, n, k, f * P:(f + 1) * P], hT[:, k, :],
                                      start=(k == 0), stop=(k == KD - 1))
                        if (f, n) != (FE - 1, 1):
                            last.then_inc(sem(tag + "_gu"), 1)
                return last

            have("shared", 0)
            last = gate_up(unit("shared", 0, 0, 2, KD, D_EXPERT), 4, "always", lambda f: 1, "sh")
            spent(last, "shared", 0)
            pe.wait_ge(sem("gates_ready"), 1)
            for t in range(TT):
                last = nc.tensor.transpose(ps[0:N_EXPERTS, 1, t * P:(t + 1) * P], rt[:, 5, t, :], ident[:, :])
            last.then_inc(sem("gates_p"), 1)
            have("shared", 1)
            pe.wait_ge(sem("sh_h"), FE)
            w = unit("shared", 1, 0, FE, D)
            for d in range(KD):
                pe.wait_ge(sem("sh_free"), 4 + d + 1)
                for k in range(FE):
                    last = mm(ps[:, 4 + d % 4, :], w[:, k, d * P:(d + 1) * P], hexp[:, k, :],
                              start=(k == 0), stop=(k == FE - 1))
                if d < KD - 1:
                    last.then_inc(sem("sh_d"), 1)
            spent(last, "shared", 1)

            pe.wait_ge(sem("gateb_free"), 1)
            pe.wait_ge(sem("sh_free"), 4 + 4 + KD)
            with pe.Fori(0, N_EXPERTS // 2) as i:
                pe.wait_ge(sem("adaw_in"), i * 16 + 16)
                pe.wait_ge(sem("moe_d_free"), i * 9 + 1)
                for j in range(3):
                    for k in range(KD):
                        last = mm(ps[:, 4, j:j + 1], adaw[:, k, j * P:(j + 1) * P], csil[:, 8 + k:9 + k],
                                  start=(k == 0), stop=(k == KD - 1))
                last.then_inc(sem("adaw_used"), 1)
                for u in range(2):
                    have("moe", 2 * u, i)
                    last = gate_up(unit("moe", 2 * u, 0, 2, KD, D_EXPERT), 0, "moe_gu_free",
                                   lambda f: i * 4 + (2 * u + f + 1), "moe")
                    spent(last, "moe", 2 * u)
                have("moe", 1, i)
                have("moe", 3, i)
                w = [unit("moe", 2 * u + 1, 0, FE, D) for u in range(2)]
                pe.wait_ge(sem("moe_hg"), i * 4 + 6)
                for d in range(KD):
                    pe.wait_ge(sem("moe_d_free"), i * 9 + (5 if d < 4 else d + 2))
                    for k in range(2 * FE):
                        last = mm(ps[:, 4 + d % 4, :], w[k // FE][:, k % FE, d * P:(d + 1) * P], hexp[:, k, :],
                                  start=(k == 0), stop=(k == 2 * FE - 1))
                        if d == KD - 1 and k == FE:
                            spent(last, "moe", 1)
                    if d < KD - 1:
                        last.then_inc(sem("moe_d"), 1)
                spent(last, "moe", 3)
            from_T(1, outT)
            pe.wait_ge(sem("res_x"), 2 * TT)
            to_T(2, xr, "res_x", TT)

            pe.wait_ge(sem("hT_ready"), 3 * KD)
            have("index", 0)
            w = unit("index", 0, 0, KD, KV_RANK)
            for t in range(TT):
                for k in range(KD):
                    last = mm(ps[:, t // 2, (t % 2) * KV_RANK:(t % 2 + 1) * KV_RANK], hT[:, k, t * P:(t + 1) * P],
                              w[:, k, :], start=(k == 0), stop=(k == KD - 1))
            last.then_inc(sem("ckv_p"), 1)
            w = unit("index", 0, 2048, KD, IDX_HEADS)
            for t in range(TT):
                for k in range(KD):
                    last = mm(ps[:, 2, t * IDX_HEADS:(t + 1) * IDX_HEADS], hT[:, k, t * P:(t + 1) * P],
                              w[:, k, :], start=(k == 0), stop=(k == KD - 1))
            last.then_inc(sem("iw_p"), 1)
            w = unit("index", 0, 2112, KD, P)
            for k in range(KD):
                last = mm(ps[:, 3, :], w[:, k, :], hT[:, k, :], start=(k == 0), stop=(k == KD - 1))
            spent(last, "index", 0)
            have("index", 1)
            w = unit("index", 1, 0, KD, 512)
            for j in range(4):
                for k in range(KD):
                    last = mm(ps[:, 4 + j, :], w[:, k, j * P:(j + 1) * P], hT[:, k, :],
                              start=(k == 0), stop=(k == KD - 1))
                if j < 3:
                    last.then_inc(sem("iq_p"), 1)
            spent(last, "index", 1)
            pe.wait_ge(sem("ckvn"), TT)
            for t in range(TT):
                for r in range(2):
                    last = nc.tensor.transpose(ps[:, r, t * P:(t + 1) * P], ckvn[:, t, r * P:(r + 1) * P],
                                               ident[:, :])
            last.then_inc(sem("ckv_T"), 1)
            pe.wait_ge(sem("iqk"), 5)
            n = 0
            for qb in range(1, TT):
                for h in range(IDX_HEADS):
                    half = slice(64 * (h % 2), 64 * (h % 2) + 64)
                    pe.wait_ge(sem("idx_free"), n + 1)
                    mm(ps[:, 4 + n % 4, 0:(qb + 1) * P], iqT[half, h // 2, qb * P:(qb + 1) * P],
                       ikT[half, 0:(qb + 1) * P], start=True, stop=True).then_inc(sem("idx_p"), 1)
                    n += 1
            pe.wait_ge(sem("idx_free"), 4 + n)
            pe.wait_ge(sem("ckvT_ready"), 2)

            def attention(tag):
                dsa = tag == "dsa"
                past = NO_PAST if dsa else DSA_PAST

                def proj(k, g, par, turn):
                    q_out, k_out, v_out = ps[:, 5, :], ps[:, 6, :], ps[:, 7, :]
                    if k == 0:
                        have(tag, par, turn)
                    if k not in (1, 4, 7, 10):
                        return
                    if k == 1:
                        pe.wait_ge(sem("att_pfree"), g * 3 + 1 + past["pfree"])
                        w = unit(tag, par, 0, KD, P)
                        for kk in range(KD):
                            last = mm(q_out, w[:, kk, :], hT[:, kk, :], start=(kk == 0), stop=(kk == KD - 1))
                        last.then_inc(sem("att_proj"), 1)
                    if k == 4 and dsa:
                        w = unit(tag, par, 1024, KV_RANK)
                        for r in range(2):
                            last = nc.tensor.transpose(k_out[:, r * P:(r + 1) * P], w[:, r * P:(r + 1) * P],
                                                       ident[:, :])
                        last.then_inc(sem("uk_p"), 1)
                    if k == 7:
                        if dsa:
                            pe.wait_ge(sem("uk_T"), g + 1)
                            for r in range(2):
                                last = mm(k_out, ukT[:, r, :], ckvT[:, r, :], start=(r == 0), stop=(r == 1))
                        else:
                            w = unit(tag, par, 1024, KD, P)
                            for kk in range(KD):
                                last = mm(k_out, w[:, kk, :], hT[:, kk, :], start=(kk == 0), stop=(kk == KD - 1))
                        last.then_inc(sem("att_proj"), 1)
                    if k == 10:
                        for t in range(TT):
                            q = slice(t * P, (t + 1) * P)
                            if dsa:
                                w = unit(tag, par, 1280, 2, P)
                                for r in range(2):
                                    last = mm(v_out[:, q], ckvT[:, r, q], w[:, r, :], start=(r == 0), stop=(r == 1))
                            else:
                                w = unit(tag, par, 2048, KD, P)
                                for kk in range(KD):
                                    last = mm(v_out[:, q], hT[:, kk, q], w[:, kk, :], start=(kk == 0),
                                              stop=(kk == KD - 1))
                        last.then_inc(sem("att_proj"), 1)
                        pe.wait_ge(sem("att_proj"), g * 3 + 3 + past["proj"])
                        pe.sem_inc(used[par], 1)

                def core(k, g, par):
                    q_in, k_in, v_in = (qkv[par][:, n, :] for n in range(3))
                    if k == 0:
                        pe.wait_ge(sem("att_qkv"), g * 3 + 3 + past["qkv"])
                    if k < 8:
                        qb, m = k // 2, k % 2
                        half = slice(64 * m, 64 * m + 64)
                        pe.wait_ge(sem("att_s_free"), g * 8 + (k + 1) + past["s_free"])
                        mm(ps[:, k % 2, 0:(qb + 1) * P], q_in[half, qb * P:(qb + 1) * P],
                           k_in[half, 0:(qb + 1) * P], start=True, stop=True).then_inc(sem("att_s"), 1)
                    if 2 <= k < 10 and (dsa or k % 2):
                        n = k - 2
                        qb = n // 2
                        b = 2 + (n if dsa else qb) % 2
                        if dsa:
                            pe.wait_ge(sem("att_pn"), g * 8 + (n + 1) + past["pn"])
                            pe.wait_ge(sem("att_pT"), g * 8 + (n + 1) + past["pT"])
                        else:
                            pe.wait_ge(sem("att_pn"), g * 4 + (qb + 1) + past["pn"])
                            pe.wait_ge(sem("att_pT"), g * 4 + (qb + 1) + past["pT"])
                        for sb_ in range(qb + 1):
                            last = nc.tensor.transpose(ps[:, b, sb_ * P:(sb_ + 1) * P],
                                                       lbuf[:, n % 4, sb_ * P:(sb_ + 1) * P], ident[:, :])
                        last.then_inc(sem("att_tr"), 1)
                    if k == 10:
                        pe.wait_ge(sem("att_pT"), g * (8 if dsa else 4) + ((8 if dsa else 4) + 2) + past["pT"])
                        pe.wait_ge(sem("att_o_free"), g + 1 + past["o_free"])
                        if dsa:
                            for m in range(2):
                                for s_ in range(TT):
                                    last = mm(ps[64 * m:64 * m + 64, 4, s_ * P:], v_in[:, s_ * P + 64 * m:s_ * P + 64 * m + 64],
                                              pT[:, m, s_, s_ * P:], start=(s_ == 0), stop=(s_ == TT - 1))
                        else:
                            for qb in range(TT):
                                for s_ in range(qb + 1):
                                    last = mm(ps[:, 4, qb * P:(qb + 1) * P], pT[:, 0, s_, qb * P:(qb + 1) * P],
                                              v_in[:, s_ * P:(s_ + 1) * P], start=(s_ == 0), stop=(s_ == qb))
                        last.then_inc(sem("att_pv"), 1)
                    if k == 11 and not dsa:
                        pe.wait_ge(sem("diff_on"), g * 4 + 4)
                        for qb in range(TT):
                            last = nc.tensor.transpose(ps[:, 4, qb * P:(qb + 1) * P], onrm[:, qb, :], ident[:, :])
                        last.then_inc(sem("diff_oT"), 1)

                slots(pe, proj, core, 12)

            attention("dsa")
            pe.wait_ge(sem("att_o_free"), 1 + 8)
            project(1, "a_w_o", oT, "att_o_free", 1 + 8)
            from_T(2, outT)

            def mlp(layer):
                pe.wait_ge(sem("res_x"), (3 + 2 * layer) * TT)
                to_T(3 + 2 * layer, xr, "res_x", (2 + 2 * layer) * TT)
                pe.wait_ge(sem("hT_ready"), KD * (4 + 2 * layer))
                name = f"up{layer}"
                with pe.Fori(0, 2) as i:
                    for u in range(4):
                        have(name, u, i)
                        w = unit(name, u, 0, KD, 512)
                        for j in range(4):
                            n = 4 * u + j
                            pe.wait_ge(sem("up_free"), i * 16 + (32 * layer + n + 1))
                            for k in range(KD):
                                last = mm(ps[:, n % 8, :], w[:, k, j * P:(j + 1) * P], hT[:, k, :],
                                          start=(k == 0), stop=(k == KD - 1))
                            if j < 3:
                                last.then_inc(sem("up_p"), 1)
                        spent(last, name, u)
                pe.wait_ge(sem("up_squared"), 32 * (layer + 1))
                name = f"down{layer}"
                n_out = 3 + 2 * layer
                with pe.Fori(0, 2) as i:
                    for u in range(4):
                        have(name, u, i)
                        w = unit(name, u, 0, D_FF // P, P)
                        pe.wait_ge(sem("branch_ready"), i * 4 + (n_out * KD + u - 3))
                        for k in range(D_FF // P):
                            last = mm(ps[:, u, :], w[:, k, :], h1T[:, k, :], start=(k == 0),
                                      stop=(k == D_FF // P - 1))
                        spent(last, name, u)
                from_T(n_out, outT)

            mlp(0)
            pe.wait_ge(sem("res_x"), 4 * TT)
            to_T(4, xr, "res_x", 3 * TT)
            pe.wait_ge(sem("hT_ready"), 5 * KD)
            attention("diff")
            project(2, "b_w_o", oT, "att_o_free", 1 + 16)
            from_T(4, outT)
            mlp(1)

        @block.scalar
        def _(act):
            A = nc.scalar.activation
            link = Link(act, sem("act_link"))
            act.wait_ge(sem("pcol_T"), 1)
            for n, r in enumerate(PROWS):
                link.mark(A(pcol[:, n, 0:r], ps[:, n, 0:r], ACT.Copy))
            link.wait()
            act.sem_inc(sem("pcol_ready"), 1)
            link(A(csil[:, :], pcol[:, 0, 0:16], ACT.Tanh, scale=0.5))
            act.sem_inc(sem("c_tanh"), 1)
            act.wait_ge(sem("bias_p"), 1)
            A(rbv[0:HEADS, 0:512], ps[0:HEADS, 5, :], ACT.Copy).then_inc(sem("bias_v"), 1)
            A(rbv[0:HEADS, 512:NVEC], ps[0:HEADS, 6, 0:P], ACT.Copy).then_inc(sem("bias_v"), 1)
            act.wait_ge(sem("lam_sum"), 1)
            A(lamv[:, 0:2], lamv[:, 0:2], ACT.Exp).then_inc(sem("lam_exp"), 1)

            def to_T(n, scale, bias):
                act.wait_ge(sem("hT_turned"), n + 1)
                for k in range(KD):
                    A(hT[:, k, :], ps[:, k, :], ACT.Identity, scale=scale[:, k:k + 1],
                      bias=bias[:, k:k + 1]).then_inc(sem("hT_ready"), 1)

            act.wait_ge(sem("mod_ready"), 1)
            to_T(0, mod[:, 8:16], mod[:, 0:8])

            with act.Fori(0, 4) as i:
                for u in range(2):
                    act.wait_ge(sem("short_p"), i * 4 + (2 * u + 1))
                    act.wait_ge(sem("short_v"), i * 2 + (u + 1))
                    A(sc_c[:, u, :], ps[:, 3 * u + 1, :], ACT.Copy).then_inc(sem("short_c"), 1)

            act.wait_ge(sem("dt_abs"), 1)
            A(dtw[:, 1, :, :], dtw[:, 1, :, :], ACT.Exp, scale=-1.0).then_inc(sem("dt_exp"), 1)
            A(alog, alog, ACT.Exp).then_inc(sem("dt_exp"), 1)
            act.wait_ge(sem("acs_p"), 1)
            act.wait_ge(sem("dec_arg"), 1)
            flat = lambda n: dts[:, n, :, :].rearrange("p t h -> p (t h)")
            A(flat(ODEC), ps[:, 7, 0:P], ACT.Exp).then_inc(sem("decays"), 1)
            A(flat(CDEC), ps[:, 7, P:2 * P], ACT.Exp).then_inc(sem("decays"), 1)
            A(flat(DEC), flat(DEC), ACT.Exp).then_inc(sem("decays"), 1)

            def ssd_proj(k, g, par, turn):
                if k < 4:
                    act.wait_ge(sem("ssd_conv"), g * 4 + (k + 1))
                    act.wait_ge(sem("ssd_th_free"), g * 4 + (k + 1))
                    A(th[:, k % 2, :], acc[:, k % 2, :], ACT.Tanh).then_inc(sem("ssd_tanh"), 1)
                else:
                    h = k - 4
                    flat2 = lambda v: v.rearrange("p t c -> p (t c)")
                    act.wait_ge(sem("ssd_proj"), g * 6 + (k + 1))
                    act.wait_ge(sem("ssd_silu"), g * 4 + (h + 3))
                    act.wait_ge(sem("ssd_zs_free"), g + 1)
                    A(th[:, h, :], ps[:, k % 2, :], ACT.Tanh, scale=0.5).then_inc(sem("ssd_ztanh"), 1)
                    link(A(flat2(zs[par][:, 2 * h:2 * h + 2, :]), ps[:, k % 2, :], ACT.Copy, scale=0.5))
                    act.sem_inc(sem("ssd_b01_free"), 1)
                    act.sem_inc(sem("ssd_zh"), 1)

            def ssd_core(k, g, par):
                if k == 0:
                    act.wait_ge(sem("ssd_xb_T"), g + 1)
                    act.wait_ge(sem("ssd_y_p"), g * 4 + 1)
                    for m in range(2):
                        link.mark(A(xtok[:, :, m * P:(m + 1) * P],
                                    ps[:, 2 + m, :].rearrange("p (t c) -> p t c", t=TT), ACT.Copy))
                    link(A(btok[:, :, :].rearrange("p t c -> p (t c)"), ps[:, 4, :], ACT.Copy))
                    act.sem_inc(sem("ssd_b23_free"), 1)
                    act.sem_inc(sem("ssd_xtok"), 1)
                if k <= 3:
                    act.wait_ge(sem("ssd_seg"), g * 4 + (k + 1))
                    v = lm[k % 2][:, :, :].rearrange("p h c -> p (h c)")
                    A(v, v, ACT.Exp).then_inc(sem("ssd_exp"), 1)
                if k == 4:
                    act.wait_ge(sem("ssd_gated"), g + 1)
                    for t in range(TT):
                        link(A(ysq, y[:, t, :], ACT.Square, accum_out=stats[:, t, 0:1]))
                    act.sem_inc(sem("ssd_sq"), 1)
                    act.wait_ge(sem("ssd_rstd"), g + 1)
                    for t in range(TT):
                        A(y[:, t, :], y[:, t, :], ACT.Copy, scale=rstd[:, t:t + 1]).then_inc(sem("ssd_yn"), 1)
                if k == 5:
                    act.wait_ge(sem("ssd_y_p5"), g + 1)
                    for m in range(2):
                        A(yT[:, bass.ds(g * 2 + m, 1), :], ps[:, 2 + m, :], ACT.Copy,
                          scale=norm_w[:, bass.ds(g * 2 + m, 1)]).then_inc(sem("ssd_y_T"), 1)
                    act.wait_ge(sem("ssd_y_T"), g * 2 + 2)
                    act.sem_inc(sem("ssd_b23_free"), 1)

            act.wait_ge(sem("bias_out"), 16)
            slots(act, ssd_proj, ssd_core, 6, (link, 9))

            with act.Fori(0, 4) as i:
                for u in range(2):
                    act.wait_ge(sem("merge_g"), i * 4 + (2 * u + 2))
                    act.wait_ge(sem("merge_used"), i * 2 + (u + 1))
                    for n in range(2):
                        A(mg[:, u, n, :], ps[:, 4 * u + n, :], ACT.Tanh, scale=0.5).then_inc(sem("merge_t"), 1)

            def evac(n, name, dst, scale):
                for k in range(KD):
                    u, j = k // 4, k % 4
                    if j < 3:
                        act.wait_ge(sem("branch_p"), 6 * n + 3 * u + j + 1)
                    else:
                        act.wait_ge(used[ring.slot(name, u)], ring.free(name, u, 0) + 1)
                    A(dst[:, k, :], ps[:, k, :], ACT.Copy, scale=scale[:, k:k + 1]).then_inc(sem("branch_ready"), 1)

            evac(0, "w_o", mixT, mod[:, 16:24])
            to_T(1, mod[:, 32:40], mod[:, 24:32])
            act.wait_ge(sem("router_p"), 1)
            link(A(rt[:, 0, :, :].rearrange("p t e -> p (t e)"), ps[:, 0, 0:TT * N_EXPERTS], ACT.Exp, scale=-1.0))
            act.sem_inc(sem("router_e"), 1)
            for f in range(FE):
                act.wait_ge(sem("sh_gu"), 2 * f + 1)
                A(tg[:, f, :], ps[:, 4 + 2 * f, :], ACT.Tanh, scale=0.5).then_inc(sem("sh_t"), 1)
            act.wait_ge(sem("gates_p"), 1)
            A(gateT[0:N_EXPERTS, :], ps[0:N_EXPERTS, 1, :], ACT.Copy).then_inc(sem("gates_T"), 1)
            with act.Fori(0, N_EXPERTS // 2) as i:
                for u in range(2):
                    for f in range(FE):
                        act.wait_ge(sem("moe_gu"), i * 6 + (3 * u + 2 * f + 1))
                        act.wait_ge(sem("moe_hg"), i * 4 + (2 * u + f + 1))
                        A(tg[:, f, :], ps[:, 2 * f, :], ACT.Tanh, scale=0.5).then_inc(sem("moe_t"), 1)
            act.wait_ge(sem("hexp_free"), 1 + N_EXPERTS // 2)
            for k in range(KD):
                A(outT[:, k, :], outT[:, k, :], ACT.Copy, scale=mod[:, 40 + k:41 + k]).then_inc(sem("branch_ready"), 1)
            to_T(2, mod[:, 56:64], mod[:, 48:56])

            act.wait_ge(sem("ckv_p"), 1)
            for t in range(TT):
                v = ps[:, t // 2, (t % 2) * KV_RANK:(t % 2 + 1) * KV_RANK]
                link(A(ckvn[:, t, :], v, ACT.Square, accum_out=stats[:, t, 0:1]))
            act.sem_inc(sem("ckv_sq"), 1)
            act.wait_ge(used[ring.slot("index", 0)], ring.free("index", 0, 0) + 1)
            A(ikT, ps[:, 3, :], ACT.Copy).then_inc(sem("iqk"), 1)
            for j in range(4):
                if j < 3:
                    act.wait_ge(sem("iq_p"), j + 1)
                else:
                    act.wait_ge(used[ring.slot("index", 1)], ring.free("index", 1, 0) + 1)
                A(iqT[:, j, :], ps[:, 4 + j, :], ACT.Copy).then_inc(sem("iqk"), 1)
            act.wait_ge(sem("ckv_rstd"), 1)
            for t in range(TT):
                v = ps[:, t // 2, (t % 2) * KV_RANK:(t % 2 + 1) * KV_RANK]
                A(ckvn[:, t, :], v, ACT.Copy, scale=rstd[:, t:t + 1]).then_inc(sem("ckvn"), 1)
            act.wait_ge(sem("ckv_T"), 1)
            for r in range(2):
                A(ckvT[:, r, :], ps[:, r, :], ACT.Copy, scale=kv_norm[:, r:r + 1]).then_inc(sem("ckvT_ready"), 1)
            n = 0
            for qb in range(1, TT):
                for h in range(IDX_HEADS):
                    act.wait_ge(sem("idx_p"), n + 1)
                    act.wait_ge(sem("idx_s"), n + 1)
                    A(rl[:, n % 2, 0:(qb + 1) * P], ps[:, 4 + n % 4, 0:(qb + 1) * P],
                      ACT.Relu).then_inc(sem("idx_free"), 1)
                    n += 1
            act.wait_ge(sem("idx_s"), 2 + n)

            def attention(tag):
                dsa = tag == "dsa"
                past = NO_PAST if dsa else DSA_PAST
                per = 8 if dsa else 4

                def proj(k, g, par, turn):
                    n = {2: 0, 8: 1, 11: 2}.get(k)
                    if k == 5 and dsa:
                        act.wait_ge(sem("uk_p"), g + 1)
                        A(ukT[:, :, :].rearrange("p r c -> p (r c)"), ps[:, 6, 0:KV_RANK],
                          ACT.Copy).then_inc(sem("uk_T"), 1)
                    if n is not None:
                        act.wait_ge(sem("att_proj"), g * 3 + (n + 1) + past["proj"])
                        A(qkv[par][:, n, :], ps[:, 5 + n, :], ACT.Copy).then_inc(sem("att_qkv"), 1)
                    if k == 11:
                        act.wait_ge(sem("att_qkv"), g * 3 + 3 + past["qkv"])
                        act.sem_inc(sem("att_pfree"), 3)

                def core(k, g, par):
                    if k < 8:
                        qb, m = k // 2, k % 2
                        v = lbuf[:, k % 4, 0:(qb + 1) * P]
                        act.wait_ge(sem("att_l"), g * 8 + (k + 1) + past["l"])
                        A(v, v, ACT.Exp, bias=nmax[:, k:k + 1],
                          accum_out=rsum[:, k:k + 1]).then_inc(sem("att_p"), 1)
                    if 3 <= k < 11 and (dsa or k % 2 == 0):
                        n = k - 3
                        qb, m = n // 2, (n % 2 if dsa else 0)
                        j = n if dsa else qb
                        act.wait_ge(sem("att_tr"), g * per + (j + 1 + (4 if dsa else 2)) + past["tr"])
                        if j == 0:
                            act.wait_ge(sem("att_pv"), g + 1 + past["pv"])
                        A(pT[:, m, 0:qb + 1, qb * P:(qb + 1) * P],
                          ps[:, 2 + j % 2, 0:(qb + 1) * P].rearrange("p (s q) -> p s q", s=qb + 1),
                          ACT.Copy).then_inc(sem("att_pT"), 1)
                    if k == 11:
                        act.wait_ge(sem("att_pv"), g + 2 + past["pv"])
                        if dsa:
                            A(oT[:, bass.ds(g, 1), :], ps[:, 4, :], ACT.Copy).then_inc(sem("att_o_free"), 1)
                        else:
                            for qb in range(TT):
                                link(A(onrm[:, qb, :], ps[:, 4, qb * P:(qb + 1) * P], ACT.Square,
                                       accum_out=osq[:, qb:qb + 1]))
                            act.sem_inc(sem("diff_osq"), 1)
                            act.wait_ge(sem("diff_rstd"), g + 1)
                            for qb in range(TT):
                                A(onrm[:, qb, :], ps[:, 4, qb * P:(qb + 1) * P], ACT.Copy,
                                  scale=ortmp[:, 2, qb:qb + 1]).then_inc(sem("diff_on"), 1)
                            act.wait_ge(sem("diff_oT"), g + 1)
                            A(oT[:, bass.ds(g, 1), :], ps[:, 4, :], ACT.Copy,
                              scale=subln).then_inc(sem("att_o_free"), 1)

                slots(act, proj, core, 12, (link, 0 if dsa else 4))

            attention("dsa")
            evac(1, "a_w_o", outT, mod[:, 64:72])

            def mlp(layer):
                m0 = 48 * (layer + 1)
                to_T(3 + 2 * layer, mod[:, m0 + 32:m0 + 40], mod[:, m0 + 24:m0 + 32])
                name = f"up{layer}"
                with act.Fori(0, 2) as i:
                    for n in range(16):
                        u, j = n // 4, n % 4
                        if j < 3:
                            act.wait_ge(sem("up_p"), i * 12 + (24 * layer + 3 * u + j + 1))
                        else:
                            act.wait_ge(used[u], ring.free(name, u, i) + 1)
                        A(h1T[:, bass.ds(i * 16 + n, 1), :], ps[:, n % 8, :], ACT.Relu).then_inc(sem("up_free"), 1)
                name = f"down{layer}"
                with act.Fori(0, 2) as i:
                    for u in range(4):
                        act.wait_ge(used[u], ring.free(name, u, i) + 1)
                        A(outT[:, bass.ds(i * 4 + u, 1), :], ps[:, u, :], ACT.Copy,
                          scale=mod[:, bass.ds(i * 4 + (m0 + 40 + u), 1)]).then_inc(sem("branch_ready"), 1)

            mlp(0)
            to_T(4, mod[:, 104:112], mod[:, 96:104])
            attention("diff")
            evac(2, "b_w_o", outT, mod[:, 112:120])
            mlp(1)

        @block.vector
        def _(dve):
            V = nc.vector
            link = Link(dve, sem("dve_link"))
            for name, n in (("ada_free", 1), ("short_free", 2), ("short_v", 2), ("ssd_b01_free", 2),
                            ("ssd_b23_free", 1), ("ssd_y_free", 1), ("ssd_y_p", 1), ("ssd_th_free", 2),
                            ("ssd_zs_free", 2), ("merge_free", 2), ("merge_used", 2), ("always", 1), ("sh_free", 4),
                            ("adaw_used", 1), ("moe_gu_free", 2), ("hexp_free", 1), ("moe_hg", 2), ("moe_d_free", 4),
                            ("idx_free", 4), ("idx_s", 2),
                            ("att_pfree", 1), ("att_s_free", 2), ("att_pT", 2), ("att_o_free", 1),
                            ("att_tr", 4), ("att_pv", 1), ("att_strip_free", 2),
                            ("up_free", 8)):
                dve.sem_inc(sem(name), n)

            def root(r, v, tmp):
                link(V.tensor_scalar(r.bitcast(I32), v.bitcast(I32), -0.5, float(0x5F3759DF), ALU.mult, ALU.add))
                for _ in range(NEWTON):
                    link(V.tensor_tensor(tmp, r, r, ALU.mult))
                    link(V.scalar_tensor_tensor(tmp, tmp, -0.5, v, ALU.mult, ALU.mult))
                    link(V.scalar_tensor_tensor(r, tmp, 1.5, r, ALU.add, ALU.mult))

            def layer_norm(t, src, dst):
                for h in range(2):
                    link.mark(V.bn_stats(stats[:, t, 6 * h:6 * h + 6], src[:, t, 512 * h:512 * h + 512]))
                link.wait()
                link(V.bn_aggr(mv[:, t, :], stats[:, t, :]))
                link(V.tensor_scalar(rtmp[:, 0, t:t + 1], mv[:, t, 1:2], EPS, None, ALU.add))
                root(rstd[:, t:t + 1], rtmp[:, 0, t:t + 1], rtmp[:, 1, t:t + 1])
                return V.tensor_scalar(dst[:, t, :], src[:, t, :], mv[:, t, 0:1], rstd[:, t:t + 1],
                                       ALU.subtract, ALU.mult)

            dve.wait_ge(sem("x_in"), 16)
            for t in range(TT):
                layer_norm(t, xr, xhat).then_inc(sem("ln0_x"), 1)

            dve.wait_ge(sem("pcol_ready"), 1)
            dve.wait_ge(sem("c_tanh"), 1)
            link(V.scalar_tensor_tensor(csil[:, :], csil[:, :], 1.0, pcol[:, 0, 0:16], ALU.add, ALU.mult))
            V.tensor_scalar(csil[:, :], csil[:, :], 0.5, None, ALU.mult).then_inc(sem("csil"), 1)
            link.mark(V.tensor_scalar(pcol[:, 2, :], pcol[:, 2, :], 0.5, None, ALU.mult))
            link(V.tensor_scalar(conv_b, conv_b, 0.5, None, ALU.mult))

            dve.wait_ge(sem("lam_in"), 16)
            for n in range(2):
                link(V.tensor_tensor(lamb[:, 2 * n, :], lamb[:, 2 * n, :], lamb[:, 2 * n + 1, :], ALU.mult))
                link(V.reduce_sum(lamv[:, n:n + 1], lamb[:, 2 * n, :], AX_X))
            dve.sem_inc(sem("lam_sum"), 1)
            dve.wait_ge(sem("lam_exp"), 1)
            link(V.tensor_tensor(lamv[:, 2:3], lamv[:, 1:2], lamv[:, 0:1], ALU.subtract))
            link.mark(V.tensor_scalar(lamv[:, 3:4], lamv[:, 2:3], -LAM_INIT, None, ALU.add))
            link(V.tensor_scalar(subln, subln, 1.0 - LAM_INIT, None, ALU.mult))

            with dve.Fori(0, 3) as i:
                link.enter(i, 1)
                dve.wait_ge(used[3], ring.free("ada", 3, i) + 1)
                link(V.tensor_tensor(mod[:, bass.ds(i * 16, 16)], ps[:, 4, 0:16],
                                     pcol[:, 0, bass.ds(i * 16 + 16, 16)], ALU.add))
                dve.sem_inc(sem("ada_free"), 1)
                link.leave(3)
            link.mark(V.tensor_scalar(mod[:, 8:16], mod[:, 8:16], 1.0, None, ALU.add))
            link(V.tensor_scalar(mod[:, 32:40], mod[:, 32:40], 1.0, None, ALU.add))
            link(V.tensor_scalar(mod[:, 16:24], mod[:, 16:24], 0.5, None, ALU.mult))
            dve.sem_inc(sem("mod_ready"), 1)

            with dve.Fori(0, 4) as i:
                link.enter(i, 8)
                for u in range(2):
                    j = i * 2 + u
                    w = [sc_w[:, n, bass.ds(j, 1)] for n in range(3)]
                    dve.wait_ge(sem("short_p"), i * 4 + (2 * u + 2))
                    dve.wait_ge(sem("short_c"), i * 2 + (u + 1))
                    link(V.tensor_tensor(sc_v[:, u, :], sc_c[:, u, :], ps[:, 3 * u + 2, :], ALU.mult))
                    dve.sem_inc(sem("short_v"), 1)
                    link(V.tensor_scalar(sc_u[:, u, :], sc_v[:, u, :], w[2], None, ALU.mult))
                    for n, s in ((1, 1), (0, 2)):
                        link(V.scalar_tensor_tensor(sc_u[:, u, s:], sc_v[:, u, :T - s], w[n],
                                                    sc_u[:, u, s:], ALU.mult, ALU.add))
                    dve.wait_ge(used[ring.slot("short", u)], ring.free("short", u, i) + 1)
                    V.tensor_tensor(scuT[:, bass.ds(j, 1), :], sc_u[:, u, :], ps[:, 3 * u, :],
                                    ALU.mult).then_inc(sem("short_free"), 1)
                link.leave(4)

            v4 = lambda n: dtw[:, n, :, :]
            f4 = lambda n: dtw[:, n, :, :].rearrange("p t h -> p (t h)")
            fd = lambda n: dts[:, n, :, :].rearrange("p t h -> p (t h)")
            row = lambda r: r.unsqueeze(1).to_broadcast([P, TT, SSD_HEADS])
            dve.wait_ge(sem("dt_p"), 1)
            link(V.tensor_tensor(v4(0), ps[:, 6, 0:P].rearrange("p (t h) -> p t h", t=TT), row(dtb), ALU.add))
            link(V.tensor_scalar(f4(2), f4(0), -1.0, None, ALU.mult))
            link(V.tensor_tensor(f4(1), f4(0), f4(2), ALU.max))
            dve.sem_inc(sem("dt_abs"), 1)
            dve.wait_ge(sem("dt_exp"), 2)
            link(V.tensor_scalar(f4(2), f4(1), 2.0, None, ALU.add))
            link(V.reciprocal(f4(2), f4(2)))
            link(V.tensor_tensor(f4(2), f4(2), f4(1), ALU.mult))
            link(V.tensor_tensor(f4(1), f4(2), f4(2), ALU.mult))
            link(V.tensor_scalar(f4(3), f4(1), 1.0 / 17, None, ALU.mult))
            for n in (15, 13, 11, 9, 7, 5, 3):
                link(V.scalar_tensor_tensor(f4(3), f4(3), 1.0 / n, f4(1), ALU.add, ALU.mult))
            link(V.scalar_tensor_tensor(f4(3), f4(3), 1.0, f4(2), ALU.add, ALU.mult))
            link(V.tensor_scalar(f4(0), f4(0), 0.0, None, ALU.max))
            link(V.scalar_tensor_tensor(fd(DT), f4(3), 2.0, f4(0), ALU.mult, ALU.add))
            link(V.scalar_tensor_tensor(dts[:, DA, :, :], dts[:, DT, :, :], -1.0, row(alog), ALU.mult, ALU.mult))
            dve.sem_inc(sem("da_ready"), 1)
            link(V.tensor_copy(dts[:, DSK, :, :], row(dskip)))
            dve.wait_ge(sem("acs_p"), 1)
            link(V.tensor_copy(fd(ACS), ps[:, 7, 0:P]))
            link(V.tensor_tensor(fd(DEC), ps[:, 7, P:2 * P], fd(ACS), ALU.subtract))
            dve.sem_inc(sem("dec_arg"), 1)
            dve.wait_ge(sem("decays"), 3)
            dve.sem_inc(sem("dts_ready"), 1)

            def ssd_silu(k, g, par):
                dst = xsT[:, k, :] if k < 2 else bcT[par][:, k - 2, :]
                dve.wait_ge(sem("ssd_tanh"), g * 4 + (k + 1))
                V.scalar_tensor_tensor(dst, th[:, k % 2, :], 1.0, acc[:, k % 2, :], ALU.add,
                                       ALU.mult).then_inc(sem("ssd_silu"), 1)

            def ssd_proj(k, g, par, turn):
                if k < 4:
                    j = (g * 2 + k) if k < 2 else (g + (16 + 8 * (k - 2)))
                    w = [conv_w[:, n, bass.ds(j, 1)] for n in range(4)]
                    dve.wait_ge(sem("ssd_proj"), g * 6 + (k + 1))
                    link(V.tensor_scalar(acc[:, k % 2, :], ps[:, k % 2, :], w[3], conv_b[:, bass.ds(j, 1)],
                                         ALU.mult, ALU.add))
                    for n, s in ((2, 1), (1, 2), (0, 3)):
                        link(V.scalar_tensor_tensor(acc[:, k % 2, s:], ps[:, k % 2, :T - s], w[n],
                                                    acc[:, k % 2, s:], ALU.mult, ALU.add))
                    dve.sem_inc(sem("ssd_b01_free"), 1)
                    dve.sem_inc(sem("ssd_conv"), 1)
                    ssd_silu(k, g, par)
                    dve.wait_ge(sem("ssd_silu"), g * 4 + (k + 1))
                    dve.sem_inc(sem("ssd_th_free"), 1)
                else:
                    h = k - 4
                    dve.wait_ge(sem("ssd_ztanh"), g * 2 + (h + 1))
                    dve.wait_ge(sem("ssd_zh"), g * 2 + (h + 1))
                    v = zs[par][:, 2 * h:2 * h + 2, :].rearrange("p t c -> p (t c)")
                    link(V.scalar_tensor_tensor(v, th[:, h, :], 1.0, v, ALU.add, ALU.mult))
                    dve.sem_inc(sem("ssd_zdone"), 1)

            def per_head(n, par, t=None):
                if t is None:
                    v = gs[par][:, n, :, :].rearrange("p t h -> p (t h)")
                    return v.unsqueeze(2).to_broadcast([P, TT * HPG, HEAD])
                return gs[par][:, n, t, :].unsqueeze(2).to_broadcast([P, HPG, HEAD])

            h16 = lambda v: v.rearrange("p t (h c) -> p (t h) c", c=HEAD)
            h4 = lambda v: v.rearrange("p (h c) -> p h c", c=HEAD)

            def ssd_core(k, g, par):
                if k == 0:
                    link(V.tensor_copy(gs[par][:, :, :, :].rearrange("p n t h -> p (n t) h"),
                                       dts[:, :, :, bass.ds(g * HPG, HPG)].rearrange("p n t h -> p (n t) h")))
                    dve.sem_inc(sem("ssd_gs"), 1)
                    dve.wait_ge(sem("ssd_xtok"), g + 1)
                    link(V.tensor_tensor(h16(xdt), h16(xtok), per_head(DT, par), ALU.mult))
                    dve.sem_inc(sem("ssd_x"), 1)
                    link.mark(V.tensor_tensor(h16(xdd), h16(xdt), per_head(DEC, par), ALU.mult))
                    link(V.tensor_tensor(h16(y), h16(xtok), per_head(DSK, par), ALU.mult))
                    dve.sem_inc(sem("ssd_x"), 1)
                if k <= 3:
                    t = k
                    dve.wait_ge(sem("ssd_rowb"), g * 4 + (t + 1))
                    for h in range(HPG):
                        link.mark(V.scalar_tensor_tensor(
                            lm[t % 2][:, h, :], ps[:, 2 + t % 2, h * P:(h + 1) * P],
                            gs[par][:, ACS, t, h:h + 1], cmask[:, :], ALU.subtract, ALU.min))
                    link.wait()
                    dve.sem_inc(sem("ssd_seg"), 1)
                    dve.sem_inc(sem("ssd_b23_free"), 1)
                if 1 <= k <= 4:
                    t = k - 1
                    dve.wait_ge(sem("ssd_y_p"), g * 4 + (t + 2))
                    yv = h4(y[:, t, :])
                    link(V.tensor_tensor(yv, yv, h4(ps[:, 6, 0:GW]), ALU.add))
                    if t > 0:
                        link(V.tensor_tensor(h4(ytmp), h4(ps[:, 6, GW:2 * GW]), per_head(ODEC, par, t), ALU.mult))
                        link(V.tensor_tensor(y[:, t, :], y[:, t, :], ytmp, ALU.add))
                    if t == 0:
                        link(V.tensor_copy(state, ps[:, 7, 0:GW]))
                    elif t < TT - 1:
                        link(V.tensor_tensor(h4(state), h4(state), per_head(CDEC, par, t), ALU.mult))
                        link(V.tensor_tensor(state, state, ps[:, 7, 0:GW], ALU.add))
                    if t < TT - 1:
                        dve.sem_inc(sem("ssd_state"), 1)
                    dve.sem_inc(sem("ssd_y_free"), 1)
                if k <= 3:
                    t = k
                    dve.wait_ge(sem("ssd_exp"), g * 4 + (t + 1))
                    dve.wait_ge(sem("ssd_cb"), g + 1)
                    V.tensor_tensor(lm[t % 2][:, :, :], lm[t % 2][:, :, :],
                                    ps[:, 5, t * P:(t + 1) * P].unsqueeze(1).to_broadcast([P, HPG, P]),
                                    ALU.mult).then_inc(sem("ssd_lm"), 1)
                if k == 4:
                    dve.wait_ge(sem("ssd_zdone"), g * 2 + 2)
                    flat2 = lambda v: v[:, :, :].rearrange("p t c -> p (t c)")
                    link(V.tensor_tensor(flat2(y), flat2(y), flat2(zs[par]), ALU.mult))
                    dve.sem_inc(sem("ssd_zs_free"), 1)
                    dve.sem_inc(sem("ssd_gated"), 1)
                    dve.wait_ge(sem("ssd_sq"), g + 1)
                    link(V.tensor_scalar(rtmp[:, 0, :], stats[:, 0:TT, 0], 1.0 / GW, EPS, ALU.mult, ALU.add))
                    root(rstd[:, :], rtmp[:, 0, :], rtmp[:, 1, :])
                    dve.sem_inc(sem("ssd_rstd"), 1)
                if k == 5:
                    dve.wait_ge(sem("ssd_y_p5"), g + 1)

            slots(dve, ssd_proj, ssd_core, 6, (link, 68))

            with dve.Fori(0, 4) as i:
                link.enter(i, 6)
                for u in range(2):
                    dve.wait_ge(sem("merge_t"), i * 4 + (2 * u + 2))
                    dve.wait_ge(used[ring.slot("merge", 2 * u)], ring.free("merge", 2 * u, i) + 1)
                    link(V.scalar_tensor_tensor(mg[:, u, 1, :], mg[:, u, 1, :], 1.0, ps[:, 4 * u + 2, :],
                                                ALU.add, ALU.mult))
                    dve.wait_ge(sem("merge_y"), i * 2 + (u + 1))
                    link(V.scalar_tensor_tensor(mg[:, u, 0, :], mg[:, u, 0, :], 1.0, ps[:, 4 * u + 3, :],
                                                ALU.add, ALU.mult))
                    link(V.tensor_tensor(mergedT[:, bass.ds(i * 2 + u, 1), :], mg[:, u, 0, :], mg[:, u, 1, :],
                                         ALU.add))
                    dve.sem_inc(sem("merge_used"), 1)
                    dve.sem_inc(sem("merge_free"), 1)
                link.leave(4)

            def residual(n, alpha):
                dve.wait_ge(sem("ln_in"), 32 * (n + 1))
                for t in range(TT):
                    dve.wait_ge(sem("res_b"), TT * n + t + 1)
                    link(V.scalar_tensor_tensor(xr[:, t, :], xr[:, t, :], alpha,
                                                ps[:, 2 * t:2 * t + 2, :].rearrange("p b c -> p (b c)"),
                                                ALU.mult, ALU.add))
                    link(layer_norm(t, xr, xr))
                    link(V.tensor_tensor(xr[:, t, :], xr[:, t, :], lngb[:, 0, :], ALU.mult))
                    V.tensor_tensor(xr[:, t, :], xr[:, t, :], lngb[:, 1, :], ALU.add).then_inc(sem("res_x"), 1)

            dve.wait_ge(sem("x_in"), 32)
            residual(0, ALPHA_1)
            for t in range(TT):
                dve.wait_ge(sem("res_x"), t + 1)
                layer_norm(t, xr, xhat).then_inc(sem("ln1_x"), 1)

            e3 = lambda n: rt[:, n, :, :]
            e2 = lambda n: rt[:, n, :, :].rearrange("p t e -> p (t e)")
            dve.wait_ge(sem("router_e"), 1)
            link(V.tensor_scalar(e2(0), e2(0), 1.0, None, ALU.add))
            link(V.reciprocal(e2(0), e2(0)))
            link(V.tensor_tensor(e3(1), e3(0), rbias.unsqueeze(1).to_broadcast([P, TT, N_EXPERTS]), ALU.add))
            for t in range(TT):
                for g in range(8):
                    link.mark(V.max(top[:, t, 8 * g:8 * g + 8], rt[:, 1, t, 8 * g:8 * g + 8]))
            link(V.memset(r16.rearrange("p a t e -> p (a t e)"), GONE))
            pair = top.rearrange("p t (g r) -> p t g r", r=8)
            for t in range(TT):
                link.mark(V.tensor_tensor(r16[:, 0, t, 0:8], pair[:, t, :, 0], pair[:, t, :, 1], ALU.add))
            link.wait()
            for t in range(TT):
                link(V.max(m8[:, :], r16[:, 0, t, 0:8]))
                link(V.tensor_copy(r16[:, 1, t, 0:4], m8[:, 0:4]))
                link(V.match_replace(r16[:, 0, t, :], r16[:, 1, t, 0:8], r16[:, 0, t, :], FOUND))
            for t in range(TT):
                link.mark(V.tensor_scalar(r16[:, 1, t, 8:16], r16[:, 0, t, 0:8], FOUND, NEG, ALU.not_equal, ALU.mult))
            link.wait()
            for t in range(TT):
                link.mark(V.tensor_tensor(rt[:, 2, t, :].rearrange("p (g e) -> p g e", e=8),
                                          rt[:, 1, t, :].rearrange("p (g e) -> p g e", e=8),
                                          r16[:, 1, t, 8:16].unsqueeze(2).to_broadcast([P, 8, 8]), ALU.add))
            link.wait()
            for t in range(TT):
                link(V.max(m8[:, :], rt[:, 2, t, :]))
                link(V.match_replace(rt[:, 3, t, :], m8[:, :], rt[:, 2, t, :], FOUND))
            link(V.scalar_tensor_tensor(e2(4), e2(3), FOUND, e2(0), ALU.is_equal, ALU.mult))
            for t in range(TT):
                link.mark(V.reduce_sum(mv[:, t, 0:1], rt[:, 4, t, :], AX_X))
            link.wait()
            link(V.reciprocal(mv[:, :, 1], mv[:, :, 0]))
            for t in range(TT):
                link(V.tensor_scalar(rt[:, 5, t, :], rt[:, 4, t, :], mv[:, t, 1:2], 0.5 * ROUTED_SCALE,
                                     ALU.mult, ALU.mult))
            dve.sem_inc(sem("gates_ready"), 1)

            for f in range(FE):
                dve.wait_ge(sem("sh_t"), f + 1)
                if f < FE - 1:
                    dve.wait_ge(sem("sh_gu"), 2 * f + 2)
                else:
                    dve.wait_ge(used[0], ring.free("shared", 0, 0) + 1)
                link(V.scalar_tensor_tensor(tg[:, f, :], tg[:, f, :], 1.0, ps[:, 4 + 2 * f, :], ALU.add, ALU.mult))
                link(V.scalar_tensor_tensor(hexp[:, f, :], tg[:, f, :], 0.5, ps[:, 5 + 2 * f, :], ALU.mult, ALU.mult))
                dve.sem_inc(sem("sh_h"), 1)
                dve.sem_inc(sem("sh_free"), 2)
            for d in range(KD):
                if d < KD - 1:
                    dve.wait_ge(sem("sh_d"), d + 1)
                else:
                    dve.wait_ge(used[1], ring.free("shared", 1, 0) + 1)
                V.tensor_copy(outT[:, d, :], ps[:, 4 + d % 4, :]).then_inc(sem("sh_free"), 1)
            dve.wait_ge(sem("sh_free"), 4 + 4 + KD)

            with dve.Fori(0, N_EXPERTS // 2) as i:
                link.enter(i, 8)
                dve.wait_ge(sem("adaw_used"), i + 2)
                V.tensor_tensor(mod[:, bass.ds(i * 3 + 48, 3)], ps[:, 4, 0:3], pcol[:, 1, bass.ds(i * 3, 3)],
                                ALU.add).then_inc(sem("moe_d_free"), 1)
                for u in range(2):
                    for f in range(FE):
                        dve.wait_ge(sem("moe_t"), i * 4 + (2 * u + f + 1))
                        link(V.scalar_tensor_tensor(tg[:, f, :], tg[:, f, :], 1.0, ps[:, 2 * f, :],
                                                    ALU.add, ALU.mult))
                        if f < FE - 1:
                            dve.wait_ge(sem("moe_gu"), i * 6 + (3 * u + 2))
                        else:
                            dve.wait_ge(used[ring.slot("moe", 2 * u)], ring.free("moe", 2 * u, i) + 1)
                        link(V.tensor_tensor(tg[:, f, :], tg[:, f, :], ps[:, 2 * f + 1, :], ALU.mult))
                        dve.sem_inc(sem("moe_h"), 1)
                        dve.sem_inc(sem("moe_gu_free"), 1)
                for d in range(KD):
                    if d < KD - 1:
                        dve.wait_ge(sem("moe_d"), i * 7 + (d + 1))
                    else:
                        dve.wait_ge(used[ring.slot("moe", 3)], ring.free("moe", 3, i) + 1)
                    if d == 0:
                        dve.wait_ge(sem("moe_d_free"), i * 9 + 5)
                    V.tensor_tensor(outT[:, d, :], outT[:, d, :], ps[:, 4 + d % 4, :],
                                    ALU.add).then_inc(sem("moe_d_free"), 1)
                dve.wait_ge(sem("moe_d_free"), i * 9 + 13)
                dve.sem_inc(sem("hexp_free"), 1)
                link.leave(N_EXPERTS // 2)
            for c in (56, 80, 104, 128):
                link.mark(V.tensor_scalar(mod[:, c:c + 16], mod[:, c:c + 16], 1.0, None, ALU.add))
            link.wait()
            dve.sem_inc(sem("moe_out"), 1)
            residual(1, ALPHA_1)

            dve.wait_ge(sem("iw_p"), 1)
            link(V.tensor_scalar(iws[:, :, :].rearrange("p t h -> p (t h)"), ps[:, 2, 0:TT * IDX_HEADS],
                                 IDX_HEADS ** -0.5 * IDX_DIM ** -0.5, None, ALU.mult))
            dve.wait_ge(sem("ckv_sq"), 1)
            link(V.tensor_scalar(rtmp[:, 0, :], stats[:, 0:TT, 0], 1.0 / KV_RANK, EPS, ALU.mult, ALU.add))
            root(rstd[:, :], rtmp[:, 0, :], rtmp[:, 1, :])
            dve.sem_inc(sem("ckv_rstd"), 1)
            link(V.memset(selm[:, 0, :], 0.0))
            n = 0
            dve.wait_ge(sem("cmaskq"), 1)
            for qb in range(1, TT):
                w = (qb + 1) * P
                score = selm[:, qb, 0:w]
                for h in range(IDX_HEADS):
                    dve.wait_ge(sem("idx_free"), 4 + n + 1)
                    if h == 0:
                        link(V.tensor_scalar(score, rl[:, n % 2, 0:w], iws[:, qb, h:h + 1], None, ALU.mult))
                    else:
                        link(V.scalar_tensor_tensor(score, rl[:, n % 2, 0:w], iws[:, qb, h:h + 1], score,
                                                    ALU.mult, ALU.add))
                    dve.sem_inc(sem("idx_s"), 1)
                    n += 1
            for qb in range(1, TT):
                w = (qb + 1) * P
                score = selm[:, qb, 0:w]
                link(V.tensor_tensor(score[:, qb * P:w], score[:, qb * P:w], cmaskq[:, :], ALU.add))
                for _ in range(TOPK // 8):
                    link(V.max(m8[:, :], score))
                    link(V.match_replace(score, m8[:, :], score, GONE))
                link(V.tensor_scalar(score, score, GONE, NEG, ALU.not_equal, ALU.mult))

            def attention(tag):
                dsa = tag == "dsa"
                past = NO_PAST if dsa else DSA_PAST

                def proj(k, g, par, turn):
                    pass

                def norm(n, g):
                    qb, m = n // 2, n % 2
                    v = lbuf[:, n % 4, 0:(qb + 1) * P]
                    dve.wait_ge(sem("att_p"), g * 8 + (n + 1) + past["p"])
                    link(V.reciprocal(rsum[:, n:n + 1], rsum[:, n:n + 1]))
                    if dsa:
                        V.tensor_scalar(v, v, rsum[:, n:n + 1], None, ALU.mult).then_inc(sem("att_pn"), 1)
                    elif m == 0:
                        link(V.tensor_scalar(v, v, rsum[:, n:n + 1], None, ALU.mult))
                    else:
                        link(V.tensor_scalar(rsum[:, n:n + 1], rsum[:, n:n + 1], lamv[:, 3:4], None, ALU.mult))
                        V.scalar_tensor_tensor(v, v, rsum[:, n:n + 1], lbuf[:, (n - 1) % 4, 0:(qb + 1) * P],
                                               ALU.mult, ALU.add).then_inc(sem("att_pn"), 1)

                def core(k, g, par):
                    if k < 8:
                        qb, m = k // 2, k % 2
                        w = (qb + 1) * P
                        v = lbuf[:, k % 4, 0:w]
                        dve.wait_ge(sem("att_s"), g * 8 + (k + 1) + past["s"])
                        if k == 0:
                            dve.wait_ge(sem(f"strip_in{par}"), (g >> 1) * 16 + 16 + past["strip_in"])
                        if dsa:
                            dve.wait_ge(sem("att_tr"), g * 8 + (k + 1) + past["tr"])
                        elif m:
                            dve.wait_ge(sem("att_tr"), g * 4 + (k + 1) // 2 + past["tr"])
                        link(V.scalar_tensor_tensor(v, ps[:, k % 2, 0:w], HEAD ** -0.5,
                                                    strip[par][:, m, T - w:T], ALU.mult, ALU.add))
                        dve.sem_inc(sem("att_s_free"), 1)
                        if dsa and qb:
                            link(V.tensor_tensor(v, v, selm[:, qb, 0:w], ALU.add))
                        V.tensor_reduce(nmax[:, k:k + 1], v, AX_X, ALU.max, negate=True).then_inc(sem("att_l"), 1)
                        if k == 7:
                            dve.sem_inc(sem("att_strip_free"), 1)
                    if 1 <= k < 9:
                        norm(k - 1, g)
                    if k == 11 and not dsa:
                        dve.wait_ge(sem("diff_osq"), g + 1)
                        link(V.tensor_scalar(ortmp[:, 0, :], osq[:, :], 1.0 / P, EPS, ALU.mult, ALU.add))
                        root(ortmp[:, 2, :], ortmp[:, 0, :], ortmp[:, 1, :])
                        dve.sem_inc(sem("diff_rstd"), 1)

                slots(dve, proj, core, 12, (link, 22 if dsa else 38))

            attention("dsa")
            residual(2, ALPHA_2)

            def mlp(layer):
                with dve.Fori(0, 2) as i:
                    for n in range(16):
                        dve.wait_ge(sem("up_free"), i * 16 + (32 * layer + n + 1 + 8))
                        v = h1T[:, bass.ds(i * 16 + n, 1), :]
                        V.tensor_tensor(v, v, v, ALU.mult).then_inc(sem("up_squared"), 1)
                residual(3 + 2 * layer, ALPHA_2)

            mlp(0)
            attention("diff")
            residual(4, ALPHA_2)
            mlp(1)


def kernel(**inputs):
    import concourse.bacc as bacc
    from concourse.bass_utils import run_bass_kernel_spmd

    nc = bacc.Bacc("TRN2", target_bir_lowering=False, num_devices=1)
    arrays, aps = {}, {}
    for name in INPUTS:
        v = np.ascontiguousarray(inputs[name])
        arrays["in_" + name] = v
        aps[name] = nc.dram_tensor("in_" + name, v.shape, F32, kind="ExternalInput").ap()
    arrays["bucket_onehot"] = bucket_onehot()
    onehot = nc.dram_tensor("bucket_onehot", arrays["bucket_onehot"].shape, F32, kind="ExternalInput").ap()
    out = nc.dram_tensor("out", (1, T, D), F32, kind="ExternalOutput").ap()
    program(nc, aps, onehot, out)
    r = run_bass_kernel_spmd(nc, [arrays], core_ids=[0])
    return r.results[0]["out"]
```

```python
import math
from contextlib import ExitStack

import numpy as np

import concourse.bass as bass
from concourse import mybir

F32 = mybir.dt.float32
I32 = mybir.dt.int32
ALU = mybir.AluOpType
ACT = mybir.ActivationFunctionType
AX_X = mybir.AxisListType.X

P = 128
D = 1024
T = 512
KD = D // P
TT = T // P
NEG = -1e30
GONE = -3e38
FOUND = 1e30
NEWTON = 3

SSD_INNER = 2 * D
SSD_GROUPS = 8
SSD_HEADS = 32
HPG = SSD_HEADS // SSD_GROUPS
SSD_STATE = 128
HEAD = 64
GW = HPG * HEAD
Z0 = 0
XBC0 = SSD_INNER
B0 = XBC0 + SSD_INNER
C0 = B0 + SSD_GROUPS * SSD_STATE
DT0 = C0 + SSD_GROUPS * SSD_STATE
SCB0 = DT0 + SSD_HEADS
SCC0 = SCB0 + D
SCH0 = SCC0 + D
GA0 = SCH0 + D
GB0 = GA0 + D
N_EXPERTS = 64
D_EXPERT = 256
FE = D_EXPERT // P
ROUTED_SCALE = 2.5
PER_TOKEN = 8
BLOCK = P
NBLK = 96
ADA_W = 256
ADA_N = 2 * 6 * D // ADA_W // 8
ADA_S = 2
ADA_C = ADA_N * ADA_W // P
EPS = 1e-5
ALPHA_1 = 2.0 ** 0.25
ALPHA_2 = 4.0 ** 0.25

KV_RANK = 256
Q0 = 0
CKV0 = 1024
IQ0 = 1280
IK0 = 1792
IW0 = 1856
IDX_HEADS = 8
IDX_DIM = 64
TOPK = 128
REL_BUCKETS = 32
REL_MAX_DIST = 128
HEADS = 16
D_FF = 4 * D
NVEC = T + P
LAM_INIT = 0.8 - 0.6 * math.exp(-0.3 * 1)


def bucket_onehot():
    dist = T - 1 - np.arange(NVEC)
    n = np.maximum(dist, 0)
    exact = REL_BUCKETS // 2
    nf = np.maximum(n, 1).astype(np.float32)
    large = exact + (np.log(nf / np.float32(exact)) / np.float32(math.log(REL_MAX_DIST / exact))
                     * np.float32(REL_BUCKETS - exact)).astype(np.int32)
    bucket = np.where(n < exact, n, np.minimum(large, REL_BUCKETS - 1))
    bucket = np.where(dist < 0, REL_BUCKETS, bucket)
    return (np.arange(REL_BUCKETS + 1)[:, None] == bucket[None, :]).astype(np.float32)


def counting_rows():
    tokens = np.arange(P)[:, None] + P * np.arange(TT)[None, :]
    blocks = np.broadcast_to(np.arange(NBLK)[None, :], (P, NBLK))
    return np.concatenate([tokens, blocks], axis=1).astype(np.float32)


INDEX_P = dict(ckv_p=1, iw_p=2, ckv_T=3)
START_P = dict(pcol_T=1, bias_p=2)
DECAY_P = dict(dt_p=1, acs_p=2)
DECAY_V = dict(dt_abs=1, da_ready=2, dec_arg=3, dts_ready=4)
ROUTE_P = dict(router_p=1, counts_p=2, g2_p=3, ends_p=4, blk_p=5, rows_p=6)
ROUTE_V = dict(chosen=1, ends=2, slots=3, past_e=4, blk_e=5, row_i=6)

ADA_SHORT = dict(sum=4 + 1, p=1, free=2, into=0)
ADA_MERGE = dict(sum=4 + 1 + 8 * ADA_S + 1, p=1 + 9, free=2 + 9, into=8 * 16)

YG_IN = ("yg_in0", "yg_in1", "yg_in2", "yg_in3")

DSA_PAST = dict(pfree=24, proj=24, qkv=24, s_free=64, s=64, l=64, p=64, pn=64, tr=64 + 2, pT=64, pv=8,
                o_free=8, strip_free=8, strip_in=64)
NO_PAST = {name: 0 for name in DSA_PAST}


class Link:

    def __init__(self, eng, sem):
        self.eng, self.sem, self.base, self.k = eng, sem, 0, 0

    def mark(self, ins):
        self.k += 1
        ins.then_inc(self.sem, 1)

    def wait(self):
        self.eng.wait_ge(self.sem, self.base + self.k)

    def __call__(self, ins):
        self.mark(ins)
        self.wait()

    def enter(self, turn, each):
        self.start, self.each = self.base + self.k, each
        self.base, self.k = turn * each + self.start, 0

    def leave(self, turns):
        assert self.k == self.each, (self.k, self.each)
        self.base, self.k = self.start + turns * self.each, 0


class Slots:

    def __init__(self, stages, slots):
        self.at = {}
        self.dmas = {name: [n for _, n in units] for name, _, units in stages}
        fills, dmas = [0] * slots, [0] * slots
        for name, turns, units in stages:
            each_f, each_d = [0] * slots, [0] * slots
            entry = []
            for s, n in units:
                each_d[s] += n
                entry.append((s, fills[s] + each_f[s], dmas[s] + each_d[s]))
                each_f[s] += 1
            self.at[name] = [(s, f, each_f[s], d, each_d[s]) for s, f, d in entry]
            for s in range(slots):
                fills[s] += turns * each_f[s]
                dmas[s] += turns * each_d[s]

    def slot(self, name, u):
        return self.at[name][u][0]

    def free(self, name, u, turn):
        _, f, each, _, _ = self.at[name][u]
        return turn * each + (f + 1)

    def before(self, name, u):
        _, _, _, d, each = self.at[name][u]
        return 16 * d - 16 * self.dmas[name][u]

    def full(self, name, u, turn):
        _, _, _, d, each = self.at[name][u]
        return turn * (16 * each) + 16 * d


STAGES = [
    ("ada", 1, [(0, 1), (1, 1), (2, 1), (3, 1)]),
    ("short", 4, [(0, 3), (1, 3)]),
    ("ssd", 4, [(2, 3), (3, 1), (0, 3), (1, 1)]),
    ("merge", 4, [(2, 3), (3, 1), (0, 3), (1, 1)]),
    ("w_o", 1, [(2, 1), (3, 1)]),
    ("shared", 1, [(0, 2), (1, 1)]),
    ("moe", NBLK // 2, [(2, 2), (3, 1), (0, 2), (1, 1)]),
    ("index", 1, [(2, 4), (3, 1)]),
    ("dsa", 4, [(0, 4), (1, 4)]),
    ("a_w_o", 1, [(2, 1), (3, 1)]),
    ("up0", 2, [(0, 1), (1, 1), (2, 1), (3, 1)]),
    ("down0", 2, [(0, 1), (1, 1), (2, 1), (3, 1)]),
    ("diff", 4, [(0, 3), (1, 3)]),
    ("b_w_o", 1, [(2, 1), (3, 1)]),
    ("up1", 2, [(0, 1), (1, 1), (2, 1), (3, 1)]),
    ("down1", 2, [(0, 1), (1, 1), (2, 1), (3, 1)]),
]

INPUTS = [
    "x", "c", "w_ada", "b_ada", "w_in", "ssd_conv_w", "ssd_conv_b", "ssd_dt_bias", "ssd_A_log",
    "ssd_D", "ssd_norm_w", "w_ssd_out", "sc_conv_w", "w_sc_out", "w_o", "ln1_g", "ln1_b",
    "router_w", "router_bias", "w_gate", "w_up", "w_down", "sh_gate", "sh_up", "sh_down",
    "ln2_g", "ln2_b", "c_2", "rel_bias_2", "ada_w_2", "ada_b_2", "ln_g_2", "ln_b_2",
    "a_w_in_2", "a_kv_norm_2", "a_w_uk_2", "a_w_uv_2", "a_w_o_2", "b_w_in_2", "b_lambda_2",
    "b_subln_2", "b_w_o_2", "mlp_w1_2", "mlp_w2_2",
]


def program(nc, a, onehot, counting, out):
    ctx = ExitStack()
    with ctx:
        def sb(name, shape):
            return ctx.enter_context(nc.sbuf_tensor(name, shape, F32))

        sems = {}

        def sem(name):
            if name not in sems:
                sems[name] = ctx.enter_context(nc.semaphore(name))
            return sems[name]

        w_in = a["w_in"][0].rearrange("(k p) n -> p k n", p=P)
        w_ada = a["w_ada"][0].rearrange("(k p) n -> p k n", p=P)
        w_ada_2 = a["ada_w_2"]
        w_ssd_out = a["w_ssd_out"][0].rearrange("(k p) n -> p k n", p=P)
        w_sc_out = a["w_sc_out"][0].rearrange("(k p) n -> p k n", p=P)
        w_o = a["w_o"][0].rearrange("(k p) n -> p k n", p=P)
        router_w = a["router_w"][0].rearrange("(k p) n -> p k n", p=P)
        w_gate = a["w_gate"][0].rearrange("e (k p) n -> e p k n", p=P)
        w_up = a["w_up"][0].rearrange("e (k p) n -> e p k n", p=P)
        w_down = a["w_down"][0].rearrange("e (k p) n -> e p k n", p=P)
        sh_gate = a["sh_gate"][0].rearrange("(k p) n -> p k n", p=P)
        sh_up = a["sh_up"][0].rearrange("(k p) n -> p k n", p=P)
        sh_down = a["sh_down"][0].rearrange("(k p) n -> p k n", p=P)
        a_w_in = a["a_w_in_2"][0].rearrange("(k p) n -> p k n", p=P)
        w_uk = a["a_w_uk_2"][0].rearrange("(j h) d r -> j (h d) r", h=2)
        w_uv = a["a_w_uv_2"][0].rearrange("h (k p) d -> p k h d", p=P)
        a_w_o = a["a_w_o_2"][0].rearrange("(k p) n -> p k n", p=P)
        b_w_in = a["b_w_in_2"][0].rearrange("(k p) n -> p k n", p=P)
        b_w_o = a["b_w_o_2"][0].rearrange("(k p) n -> p k n", p=P)
        mlp_w1 = [a["mlp_w1_2"][i].rearrange("(k p) n -> p k n", p=P) for i in range(2)]
        mlp_w2 = [a["mlp_w2_2"][i].rearrange("(k p) n -> p k n", p=P) for i in range(2)]
        x_in = a["x"][0].rearrange("(t p) d -> p t d", p=P)
        out_v = out[0].rearrange("(t p) d -> p t d", p=P)

        xhat_dram = nc.dram_tensor("xhat_dram", (T, D), F32, kind="Internal").ap()
        row_tok = nc.dram_tensor("row_tok", (NBLK * BLOCK, 1), F32, kind="Internal").ap()
        y_rows = nc.dram_tensor("y_rows", (NBLK * BLOCK, D), F32, kind="Internal").ap()
        g2_dram = nc.dram_tensor("g2_dram", (KD, P), F32, kind="Internal").ap()
        bias_dram = nc.dram_tensor("bias_dram", (HEADS, NVEC), F32, kind="Internal").ap()

        strips_dram = nc.dram_tensor("strips_dram", (HEADS, P, T), F32, kind="Internal").ap()

        xr = sb("xr", [P, TT, D])
        hT = sb("hT", [P, KD, T])
        W = sb("W", [P, 4, 4096])
        R = sb("R", [P, 20736])
        ident = sb("ident", [P, P])
        tri = sb("tri", [P, P])
        cmask = sb("cmask", [P, P])
        ones = sb("ones", [P, P])
        prow = sb("prow", [P, 4, P])
        pcol = sb("pcol", [P, 4, P])
        mod = sb("mod", [P, 3 * 48])
        csil = sb("csil", [P, 16])
        lngb = sb("lngb", [P, 2, D])
        stats = sb("stats", [P, TT, 12])
        mv = sb("mv", [P, TT, 2])
        rstd = sb("rstd", [P, TT])
        rtmp = sb("rtmp", [P, 2, TT])
        ps = ctx.enter_context(nc.psum_tensor("ps", [P, 8, 512], F32))

        def rows(v):
            return v.rearrange("(j p) -> j p", p=P)

        small = [
            (prow[0:8, 0, :], rows(a["c"][0])),
            (prow[8:16, 0, :], rows(a["c_2"][0])),
            (prow[16:64, 0, :], rows(a["b_ada"][0])),
            (prow[0:96, 1, :], a["ada_b_2"].rearrange("l (j p) -> (l j) p", p=P)),
            (prow[0:128, 2, :], a["ssd_conv_w"][0].rearrange("k (j p) -> (k j) p", p=P)),
            (prow[0:32, 3, :], rows(a["ssd_conv_b"][0])),
            (prow[32:48, 3, :], rows(a["ssd_norm_w"][0])),
            (prow[48:72, 3, :], a["sc_conv_w"][0].rearrange("k (j p) -> (k j) p", p=P)),
            (prow[72:74, 3, :], rows(a["a_kv_norm_2"][0])),
            (prow[74:75, 3, :], rows(a["b_subln_2"][0])),
        ]
        PROWS = [64, 96, 128, 75]
        conv_w = pcol[:, 2, :].rearrange("p (k j) -> p k j", k=4)
        conv_b = pcol[:, 3, 0:32]
        norm_w = pcol[:, 3, 32:48]
        sc_w = pcol[:, 3, 48:72].rearrange("p (k j) -> p k j", k=3)
        kv_norm = pcol[:, 3, 72:74]
        subln = pcol[:, 3, 74:75]

        ring = Slots(STAGES, 4)
        landed = [sem(f"landed{i}") for i in range(4)]
        used = [sem(f"used{i}") for i in range(4)]

        def unit(name, u, at, *shape):
            n = int(np.prod(shape))
            v = W[:, ring.slot(name, u), at:at + n]
            if len(shape) == 2:
                return v.rearrange("p (a b) -> p a b", a=shape[0])
            if len(shape) == 3:
                return v.rearrange("p (a b c) -> p a b c", a=shape[0], b=shape[1])
            return v

        def view(base, at, *shape):
            n = int(np.prod(shape))
            v = base[:, at:at + n]
            if len(shape) == 2:
                return v.rearrange("p (a b) -> p a b", a=shape[0])
            if len(shape) == 3:
                return v.rearrange("p (a b c) -> p a b c", a=shape[0], b=shape[1])
            return v

        xflat = xr[:, :, :].rearrange("p t d -> p (t d)")
        lflat = lngb[:, :, :].rearrange("p a d -> p (a d)")

        xhat = view(R, 12288, TT, D)
        scuT = view(R, 0, KD, T)
        yT = view(R, 4096, 16, T)
        outT = view(R, 16384, KD, T)
        mixT = view(R, 4096, KD, T)
        mergedT = view(R, 12288, KD, T)
        sc_c = view(R, 12288, 2, T)
        sc_v = view(R, 13312, 2, T)
        sc_u = view(R, 14336, 2, T)
        mg = view(R, 16384, 2, 2, T)
        rw = view(R, 4096, KD, N_EXPERTS)
        rt = view(R, 4608, 6, TT, N_EXPERTS)
        r16 = view(R, 6144, 2, TT, 16)
        top = view(R, 6272, TT, 8 * 8)
        hexp = view(R, 0, FE, T)
        tg = view(R, 2048, FE, T)
        scan = [view(R, 3072 + 96 * i, 96) for i in range(2)]
        nblk = view(R, 3264, N_EXPERTS)
        first = view(R, 3328, N_EXPERTS)
        past_e = view(R, 3392, NBLK)
        blk_e = view(R, 3488, NBLK)
        pendc = view(R, 3584, 1)
        spare = view(R, 3585, 1)
        idle_i = view(R, 3586, 1)
        g2r = view(R, 3600, P)
        key8 = view(R, 3728, TT, PER_TOKEN)
        mine = view(R, 6656, TT * PER_TOKEN, N_EXPERTS)
        xg = [view(R, 6656 + D * i, D) for i in range(2)]
        xT = view(R, 8704, KD, BLOCK)
        ybuf = [view(R, 9728 + D * i, D) for i in range(2)]
        row_i = view(R, 11776, NBLK)
        row_c = [view(R, 11872 + i, 1) for i in range(2)]
        rowt = view(R, 11904, BLOCK)
        slot_i = view(R, 12032, TT, PER_TOKEN)
        gate8 = view(R, 12064, TT, PER_TOKEN)
        count = view(R, 12096, TT + NBLK)
        tok_f, cnt_f = count[:, 0:TT], count[:, TT:TT + NBLK]
        tge = view(R, 14336, FE * BLOCK)
        he = [view(R, 14592 + 256 * i, FE, BLOCK) for i in range(2)]
        g2row = view(R, 15104, D)
        adaw = [view(xflat, 2048 * i, KD, ADA_W) for i in range(2)]
        adas = view(R, 18432, ADA_N, ADA_W)
        modx = view(R, 19968, 9 * ADA_C)
        yg = [view(R, D * i, D) for i in range(4)]
        routed = view(R, 4096, TT, D)
        ada0 = [view(R, 512 * i, 512) for i in range(4)]
        h1T = view(R, 0, D_FF // P, T)
        oT = view(R, 0, KD, T)
        pT = view(R, 4096, 2, TT, T)
        qkv = [view(R, 8192 + 1536 * i, 3, T) for i in range(2)]
        lbuf = view(R, 11264, 4, T)
        strip = [view(R, 13312 + 1024 * i, 2, T) for i in range(2)]
        ckvT = view(R, 15360, 2, T)
        selm = view(R, 16384, TT, T)
        ukT = view(R, 18432, 2, P)
        onrm = view(R, 18688, TT, P)
        iqT = view(R, 4096, 4, T)
        ikT = view(R, 6144, T)
        rl = view(R, 6656, 2, T)
        ckvn = view(R, 8192, TT, KV_RANK)
        rbv = view(R, 4096, NVEC)
        oneh = view(R, 5120, NVEC)
        relb = view(R, 6144, HEADS)
        xsT = view(xflat, 0, 2, T)
        bcT = [view(xflat, 1024 + 1024 * i, 2, T) for i in range(2)]
        xtok = view(xflat, 3072, TT, GW)
        xdt = view(lflat, 0, TT, GW)
        wdt = view(lflat, 1024, KD, SSD_HEADS)
        acc = view(R, 12288, 2, T)
        th = view(R, 13312, 2, T)
        zs = [view(R, 14336 + 1024 * i, TT, GW) for i in range(2)]
        btok = view(R, 16384, TT, P)
        lm = [view(R, 16896 + 512 * i, HPG, P) for i in range(2)]
        xdd = view(R, 17920, TT, GW)
        y = view(R, 18944, TT, GW)
        state = view(R, 19968, GW)
        ytmp = view(R, 20224, GW)
        ysq = view(R, 20480, GW)
        cmaskq = sb("cmaskq", [P, P])
        lamb = sb("lamb", [P, 4, HEAD])
        lamv = sb("lamv", [P, 4])
        iws = sb("iws", [P, TT, IDX_HEADS])
        nmax = sb("nmax", [P, 8])
        rsum = sb("rsum", [P, 8])
        m8 = sb("m8", [P, 8])
        osq = sb("osq", [P, TT])
        ortmp = sb("ortmp", [P, 3, TT])
        dts = sb("dts", [P, 7, TT, SSD_HEADS])
        DT, DA, ACS, ODEC, DEC, CDEC, DSK = range(7)
        gs = [sb(f"gs{i}", [P, 7, TT, HPG]) for i in range(2)]
        dtw = sb("dtw", [P, 4, TT, SSD_HEADS])
        rowp = sb("rowp", [P, 3 * SSD_HEADS + N_EXPERTS])
        dtb, alog, dskip, rbias = (rowp[:, 0:32], rowp[:, 32:64], rowp[:, 64:96], rowp[:, 96:160])

        LAST = NBLK // 2 - 1

        def turns_without_rows(eng):
            return eng.value_load(idle_i[0:1, 0:1].bitcast(I32), min_val=0, max_val=LAST)

        def spread(v, shape):
            return v.to_broadcast(shape)

        def slots(eng, proj, core, steps, links=None):
            def slot(pg, cg, par, turn):
                for k in range(steps):
                    if cg is not None:
                        core(k, cg, 1 - par)
                    if pg is not None:
                        proj(k, pg, par, turn)

            slot(0, None, 0, 0)
            with eng.Fori(0, 3) as i:
                if links:
                    links[0].enter(i, 2 * links[1])
                slot(i * 2 + 1, i * 2, 1, i)
                slot(i * 2 + 2, i * 2 + 1, 0, i + 1)
                if links:
                    links[0].leave(3)
            slot(7, 6, 1, 3)
            slot(None, 7, 0, 0)

        block = ctx.enter_context(nc.Block())

        @block.sync
        def _(sp):
            for i, (dst, src) in enumerate(small):
                sp.dma_start(dst, src).then_inc(sem("prow_in"), 16)
            sp.dma_start(xr[:, :, :], x_in).then_inc(sem("x_in"), 16)

            def fill(name, u, turn, *parts):
                s = ring.slot(name, u)
                sp.wait_ge(used[s], ring.free(name, u, turn))
                for dst, src in parts:
                    sp.dma_start(dst, src).then_inc(landed[s], 16)

            for u in range(4):
                fill("ada", u, 0, (unit("ada", u, 0, KD, 512), w_ada[:, :, u * 512:u * 512 + 512]))
            with sp.Fori(0, 4) as i:
                for u in range(2):
                    fill("short", u, i, *[
                        (unit("short", u, 1024 * n, KD, P), w_in[:, :, bass.ds(i * 256 + (c0 + u * P), P)])
                        for n, c0 in enumerate((SCB0, SCC0, SCH0))])
            with sp.Fori(0, 4) as i:
                for u in range(2):
                    w = unit("ssd", 2 * u, 0, KD, 512)
                    fill("ssd", 2 * u, i,
                         (w[:, :, 0:256], w_in[:, :, bass.ds(i * 512 + (XBC0 + u * GW), GW)]),
                         (w[:, :, 256:384], w_in[:, :, bass.ds(i * 256 + (B0 + u * P), P)]),
                         (w[:, :, 384:512], w_in[:, :, bass.ds(i * 256 + (C0 + u * P), P)]))
                    for n in range(2 * u, 2 * u + 2):
                        sp.dma_start(y_rows[bass.ds(i * (4 * T) + n * T, T), :].rearrange("(p n) d -> p (n d)", p=P),
                                     hT[:, :, :].rearrange("p k t -> p (k t)")).then_inc(sem("y_rows_set"), 16)
                    fill("ssd", 2 * u + 1, i,
                         (unit("ssd", 2 * u + 1, 0, KD, GW), w_in[:, :, bass.ds((i * 2 + u) * GW + Z0, GW)]))
            with sp.Fori(0, 4) as i:
                for u in range(2):
                    fill("merge", 2 * u, i,
                         (unit("merge", 2 * u, 0, KD, P), w_in[:, :, bass.ds(i * 256 + (GA0 + u * P), P)]),
                         (unit("merge", 2 * u, 1024, KD, P), w_in[:, :, bass.ds(i * 256 + (GB0 + u * P), P)]),
                         (unit("merge", 2 * u, 2048, KD, P), w_sc_out[:, :, bass.ds(i * 256 + u * P, P)]))
                    fill("merge", 2 * u + 1, i,
                         (unit("merge", 2 * u + 1, 0, 16, P), w_ssd_out[:, :, bass.ds(i * 256 + u * P, P)]))
            for u in range(2):
                fill("w_o", u, 0, (unit("w_o", u, 0, KD, 512), w_o[:, :, 512 * u:512 * u + 512]))
            sp.wait_ge(sem("ada_sum"), ADA_MERGE["sum"] + 8 * ADA_N)
            sp.dma_start(xr[:, :, :], x_in).then_inc(sem("x_in"), 16)
            fill("shared", 0, 0, (unit("shared", 0, 0, KD, D_EXPERT), sh_gate[:, :, :]),
                 (unit("shared", 0, 2048, KD, D_EXPERT), sh_up[:, :, :]))
            fill("shared", 1, 0, (unit("shared", 1, 0, FE, D), sh_down[:, :, :]))
            sp.wait_ge(sem("route_v"), ROUTE_V["blk_e"])

            def fill_gu(u, turn):
                e = sp.value_load(blk_e[0:1, bass.ds(turn * 2 + u, 1)].bitcast(I32), min_val=0,
                                  max_val=N_EXPERTS - 1)
                fill("moe", 2 * u, turn,
                     (unit("moe", 2 * u, 0, KD, D_EXPERT), w_gate[e]),
                     (unit("moe", 2 * u, 2048, KD, D_EXPERT), w_up[e]))

            def fill_down(u, turn):
                e = sp.value_load(blk_e[0:1, bass.ds(turn * 2 + u, 1)].bitcast(I32), min_val=0,
                                  max_val=N_EXPERTS - 1)
                fill("moe", 2 * u + 1, turn, (unit("moe", 2 * u + 1, 0, FE, D), w_down[e]))

            fill_gu(0, 0)
            sp.wait_ge(landed[ring.slot("moe", 0)], ring.full("moe", 0, 0))
            for n in range(1, 4):
                sp.wait_ge(landed[ring.slot("moe", n)], ring.before("moe", n))
            idle = turns_without_rows(sp)
            with sp.Fori(0, LAST) as i:
                with sp.If(i >= idle):
                    fill_down(0, i)
                    fill_gu(1, i)
                    fill_down(1, i)
                    fill_gu(0, i + 1)
                with sp.Else():
                    for n, turn in ((1, i), (2, i), (3, i), (0, i + 1)):
                        sp.wait_ge(used[ring.slot("moe", n)], ring.free("moe", n, turn))
                        sp.sem_inc(landed[ring.slot("moe", n)], 16 * ring.dmas["moe"][n])
            fill_down(0, LAST)
            fill_gu(1, LAST)
            fill_down(1, LAST)
            fill("index", 0, 0,
                 (unit("index", 0, 0, KD, KV_RANK), a_w_in[:, :, CKV0:CKV0 + KV_RANK]),
                 (unit("index", 0, 2048, KD, IDX_HEADS), a_w_in[:, :, IW0:IW0 + IDX_HEADS]),
                 (unit("index", 0, 2112, KD, P)[:, :, 0:IDX_DIM], a_w_in[:, :, IK0:IK0 + IDX_DIM]),
                 (unit("index", 0, 2112, KD, P)[:, :, IDX_DIM:P], a_w_in[:, :, IK0:IK0 + IDX_DIM]))
            fill("index", 1, 0, (unit("index", 1, 0, KD, 512), a_w_in[:, :, IQ0:IQ0 + 512]))
            with sp.Fori(0, 4) as i:
                for u in range(2):
                    j = i * 2 + u
                    fill("dsa", u, i,
                         (unit("dsa", u, 0, KD, P), a_w_in[:, :, bass.ds(i * 256 + u * P, P)]),
                         (unit("dsa", u, 1024, KV_RANK), w_uk[j]),
                         *[(unit("dsa", u, 1280 + P * r, 2, HEAD), w_uv[:, r, bass.ds(j * 2, 2), :])
                           for r in range(2)])
            for u in range(2):
                fill("a_w_o", u, 0, (unit("a_w_o", u, 0, KD, 512), a_w_o[:, :, 512 * u:512 * u + 512]))

            def mlp(layer):
                with sp.Fori(0, 2) as i:
                    for u in range(4):
                        fill(f"up{layer}", u, i, (unit(f"up{layer}", u, 0, KD, 512),
                                                  mlp_w1[layer][:, :, bass.ds(i * 2048 + u * 512, 512)]))
                with sp.Fori(0, 2) as i:
                    for u in range(4):
                        fill(f"down{layer}", u, i, (unit(f"down{layer}", u, 0, D_FF // P, P),
                                                    mlp_w2[layer][:, :, bass.ds(i * 512 + u * P, P)]))

            mlp(0)
            with sp.Fori(0, 4) as i:
                for u in range(2):
                    fill("diff", u, i, *[
                        (unit("diff", u, 1024 * n, KD, P), b_w_in[:, :, bass.ds(i * 256 + (1024 * n + u * P), P)])
                        for n in range(3)])
            for u in range(2):
                fill("b_w_o", u, 0, (unit("b_w_o", u, 0, KD, 512), b_w_o[:, :, 512 * u:512 * u + 512]))
            mlp(1)
            for t in range(TT):
                sp.wait_ge(sem("res_x"), 5 * TT + t + 1)
                sp.dma_start(out_v[:, t, :], xr[:, t, :]).then_inc(sem("out_done"), 16)
            sp.wait_ge(sem("out_done"), 16 * TT)

        @block.gpsimd
        def _(pool):
            link = Link(pool, sem("pool_link"))
            link.mark(pool.memset(ident[:, :], 0.0))
            link.mark(pool.memset(tri[:, :], 1.0))
            link.mark(pool.memset(cmask[:, :], 0.0))
            link(pool.memset(ones[:, :], 1.0))
            pool.affine_select(out=ident[:, :], in_=ident[:, :], compare_op=ALU.not_equal, fill=1.0,
                               base=0, pattern=[[-1, P]], channel_multiplier=1).then_inc(sem("consts"), 1)
            pool.affine_select(out=tri[:, :], in_=tri[:, :], compare_op=ALU.is_ge, fill=0.0,
                               base=0, pattern=[[1, P]], channel_multiplier=-1).then_inc(sem("consts"), 1)
            pool.affine_select(out=cmask[:, :], in_=cmask[:, :], compare_op=ALU.is_ge, fill=NEG,
                               base=0, pattern=[[1, P]], channel_multiplier=-1).then_inc(sem("consts"), 1)
            pool.dma_start(wdt, w_in[:, :, DT0:DT0 + SSD_HEADS]).then_inc(sem("dt_in"), 16)
            for dst, src in ((dtb, a["ssd_dt_bias"]), (alog, a["ssd_A_log"]), (dskip, a["ssd_D"]),
                             (rbias, a["router_bias"])):
                pool.dma_start(dst, src[0].partition_broadcast(P)).then_inc(sem("dt_in"), 16)

            link(pool.memset(cmaskq[:, :], 0.0))
            pool.affine_select(out=cmaskq[:, :], in_=cmaskq[:, :], compare_op=ALU.is_ge, fill=NEG,
                               base=0, pattern=[[-1, P]], channel_multiplier=1).then_inc(sem("cmaskq"), 1)
            pool.dma_start(oneh[0:REL_BUCKETS + 1, :], onehot).then_inc(sem("bias_in"), 16)
            link(pool.memset(relb[0:64, :], NEG))
            pool.dma_start(relb[0:REL_BUCKETS, :], a["rel_bias_2"]).then_inc(sem("bias_in"), 16)
            pool.dma_start(lamb[:, :, :], a["b_lambda_2"][0].partition_broadcast(P)).then_inc(sem("lam_in"), 16)
            pool.wait_ge(sem("bias_v"), 2)
            pool.dma_start(bias_dram, rbv[0:HEADS, :]).then_inc(sem("bias_out"), 16)
            pool.wait_ge(sem("bias_out"), 16)
            for h in range(0, HEADS, 4):
                pool.dma_start(strips_dram[h:h + 4], bass.AP(bias_dram.tensor, h * NVEC + P - 1,
                                                             [[NVEC, 4], [-1, P], [1, T]])).then_inc(sem("strips_out"), 16)

            pool.wait_ge(sem("ln0_x"), TT)
            with pool.Fori(0, 8) as i:
                for c in range(ADA_S):
                    pool.wait_ge(sem("ada_sum"), i * ADA_S + (ADA_SHORT["sum"] - 1 + c))
                    pool.dma_start(adaw[c % 2], w_ada[:, :, bass.ds(i * (ADA_S * ADA_W) + (2 * D + c * ADA_W), ADA_W)]
                                   ).then_inc(sem(f"adaw_in{c % 2}"), 16)

            def gains(n, g, b, sem_name, count):
                pool.wait_ge(sem(sem_name), count)
                pool.dma_start(lngb[:, 0, :], g.partition_broadcast(P)).then_inc(sem("ln_in"), 16)
                pool.dma_start(lngb[:, 1, :], b.partition_broadcast(P)).then_inc(sem("ln_in"), 16)

            gains(0, a["ln1_g"][0], a["ln1_b"][0], "ssd_y_T", 2 * SSD_GROUPS)
            with pool.Fori(0, 4) as i:
                for c in range(2 * ADA_N):
                    pool.wait_ge(sem("ada_sum"), i * (2 * ADA_N) + (ADA_MERGE["sum"] - 1 + c))
                    src = bass.AP(w_ada_2.tensor, (i >> 1) * (D * 6 * D) + (i & 1) * (2 * ADA_N * ADA_W) + c * ADA_W,
                                  [[6 * D, P], [P * 6 * D, KD], [1, ADA_W]])
                    pool.dma_start(adaw[c % 2], src).then_inc(sem(f"adaw_in{c % 2}"), 16)
            pool.wait_ge(sem("merge_y"), 8)
            pool.wait_ge(sem("res_b"), 1 * TT)
            pool.dma_start(rw, router_w).then_inc(sem("rw_in"), 16)
            pool.wait_ge(sem("ln1_x"), TT)
            pool.dma_start(xhat_dram.rearrange("(t p) d -> p t d", p=P), xhat).then_inc(sem("xhat_out"), 16)
            link(pool.memset(rowt, 0.0))
            pool.dma_start(row_tok.rearrange("(b r) o -> b (r o)", r=BLOCK), rowt[0:NBLK, :]).then_inc(
                sem("count_in"), 16)
            pool.dma_start(count, counting).then_inc(sem("count_in"), 16)
            pool.wait_ge(sem("g2_r"), 1)
            pool.dma_start(g2_dram, g2r[0:KD, :]).then_inc(sem("g2_moved"), 16)
            pool.wait_ge(sem("count_in"), 32)
            pool.wait_ge(sem("route_v"), ROUTE_V["slots"])
            for t in range(TT):
                for j in range(PER_TOKEN):
                    pool.indirect_dma_start(row_tok, bass.IndirectOffsetOnAxis(ap=slot_i[:, t, j:j + 1].bitcast(I32),
                                                                               axis=0),
                                            tok_f[:, t:t + 1], None).then_inc(sem("rows_out"), 16)
            pool.wait_ge(sem("rows_out"), 16 * TT * PER_TOKEN)
            pool.dma_start(rowt[0:NBLK, :], row_tok.rearrange("(b r) o -> b (r o)", r=BLOCK)).then_inc(
                sem("rows_out"), 16)
            pool.wait_ge(sem("g2_moved"), 16)
            pool.wait_ge(sem("xhat_out"), 16)
            pool.dma_start(g2row, g2_dram.rearrange("k p -> (k p)").partition_broadcast(P)).then_inc(
                sem("g2_moved"), 16)
            gains(1, a["ln2_g"][0], a["ln2_b"][0], "res_x", 1 * TT)
            pool.wait_ge(sem("route_v"), ROUTE_V["row_i"])

            def gather(u, turn, done):
                pool.wait_ge(sem("moe_x_p"), turn * 2 + (u + 1))
                pool.tensor_copy(row_c[u].bitcast(I32), row_i[:, bass.ds(turn * 2 + u, 1)].bitcast(I32)).then_inc(
                    sem("row_c"), 1)
                pool.wait_ge(sem("row_c"), done * 2 + 1)
                pool.sem_inc(sem("row_c"), 1)
                pool.indirect_dma_start(xg[u], None, xhat_dram,
                                        bass.IndirectOffsetOnAxis(ap=row_c[u].bitcast(I32), axis=0)
                                        ).then_inc(sem(f"xg_in{u}"), 16)

            gather(0, 0, 0)
            idle = turns_without_rows(pool)
            with pool.Fori(0, LAST) as i:
                with pool.If(i >= idle):
                    gather(1, i, ((i - idle) & 63) * 2 + 1)
                    gather(0, i + 1, ((i - idle) & 63) * 2 + 2)
            gather(1, LAST, ((LAST - idle) & 63) * 2 + 1)
            for u in range(2):
                pool.wait_ge(sem(f"y_out{u}"), 16 + 16 * (NBLK // 2))
            pool.wait_ge(sem("moe_x_p"), 2 + NBLK)
            for n in range(TT * PER_TOKEN):
                t, j = n // PER_TOKEN, n % PER_TOKEN
                if n >= 4:
                    pool.wait_ge(sem("summed"), n - 3)
                pool.indirect_dma_start(yg[n % 4], None, y_rows,
                                        bass.IndirectOffsetOnAxis(ap=slot_i[:, t, j:j + 1].bitcast(I32), axis=0)
                                        ).then_inc(sem(YG_IN[n % 4]), 16)

            def strips(past):
                with pool.Fori(0, 4) as i:
                    for u in range(2):
                        c = i * 2 + u
                        pool.wait_ge(sem("att_strip_free"), c + 1 + past["strip_free"])
                        src = strips_dram[bass.ds(c * 2, 2)].rearrange("h q s -> q h s")
                        pool.dma_start(strip[u], src).then_inc(sem(f"strip_in{u}"), 16)

            gains(2, a["ln_g_2"][0, 0], a["ln_b_2"][0, 0], "res_x", 2 * TT)
            pool.wait_ge(sem("moe_out"), 1)
            pool.wait_ge(sem("strips_out"), 64)
            strips(NO_PAST)
            gains(3, a["ln_g_2"][0, 1], a["ln_b_2"][0, 1], "res_x", 3 * TT)
            gains(4, a["ln_g_2"][1, 0], a["ln_b_2"][1, 0], "res_x", 4 * TT)
            strips(DSA_PAST)
            gains(5, a["ln_g_2"][1, 1], a["ln_b_2"][1, 1], "res_x", 5 * TT)

        @block.tensor
        def _(pe):
            mm = nc.tensor.matmul
            for s in range(4):
                pe.sem_inc(used[s], 1)

            def have(name, u, turn=0):
                pe.wait_ge(landed[ring.slot(name, u)], ring.full(name, u, turn))

            def spent(ins, name, u):
                ins.then_inc(used[ring.slot(name, u)], 1)

            pe.wait_ge(sem("consts"), 3)
            pe.wait_ge(sem("prow_in"), 16 * len(small))
            for n, r in enumerate(PROWS):
                last = nc.tensor.transpose(ps[:, n, 0:r], prow[0:r, n, :], ident[0:r, 0:r])
            last.then_inc(sem("start_p"), 1)

            pe.wait_ge(sem("bias_in"), 32)
            mm(ps[0:HEADS, 5, :], relb[0:REL_BUCKETS + 1, :], oneh[0:REL_BUCKETS + 1, 0:512], start=True, stop=True)
            mm(ps[0:HEADS, 6, 0:P], relb[0:REL_BUCKETS + 1, :], oneh[0:REL_BUCKETS + 1, 512:NVEC],
               start=True, stop=True).then_inc(sem("start_p"), 1)

            for u in range(4):
                pe.wait_ge(sem("ada_sum"), u + 1)
                for j in range(4):
                    last = mm(ps[:, 4, 4 * u + j:4 * u + j + 1], ada0[u][:, j * P:(j + 1) * P], ones[:, 0:1],
                              start=True, stop=True)
            last.then_inc(sem("ada_p"), 1)

            def ada_columns(past, chunks, step, bank):
                pe.wait_ge(sem("ada_sum"), step * chunks + past["sum"])
                for j in range(chunks * ADA_W // P):
                    last = mm(ps[:, bank, j:j + 1], adas[:, j // 2, (j % 2) * P:(j % 2 + 1) * P], ones[:, 0:1],
                              start=True, stop=True)
                last.then_inc(sem("ada_p"), 1)

            def to_T(n, src, src_ready, base=0):
                for t in range(TT):
                    pe.wait_ge(sem(src_ready), base + t + 1)
                    for k in range(KD):
                        last = nc.tensor.transpose(ps[:, k, t * P:(t + 1) * P],
                                                   src[:, t, k * P:(k + 1) * P], ident[:, :])
                last.then_inc(sem("hT_turned"), 1)

            pe.wait_ge(sem("pcol_ready"), 1)
            pe.wait_ge(sem("ada_free"), 1 + 1)
            pe.wait_ge(sem("bias_v"), 2)
            to_T(0, xhat, "ln0_x")

            pe.wait_ge(sem("hT_ready"), 1 * KD)
            with pe.Fori(0, 4) as i:
                for u in range(2):
                    have("short", u, i)
                    pe.wait_ge(sem("short_free"), i * 2 + (u + 1))
                    pe.wait_ge(sem("ada_free"), i * 2 + (u + ADA_SHORT["free"] - 1))
                    ada_columns(ADA_SHORT, ADA_S, i * 2 + u, 6 + u)
                    for n in (1, 2, 0):
                        w = unit("short", u, 1024 * n, KD, P)
                        for k in range(KD):
                            last = mm(ps[:, 3 * u + n, :], w[:, k, :], hT[:, k, :],
                                      start=(k == 0), stop=(k == KD - 1))
                        if n:
                            last.then_inc(sem("short_p"), 1)
                    spent(last, "short", u)

            pe.wait_ge(sem("ada_free"), ADA_SHORT["free"] + 7)
            ada_columns(ADA_SHORT, ADA_S, 8, 6)
            pe.wait_ge(sem("ada_free"), ADA_SHORT["free"] + 9)

            pe.wait_ge(sem("dt_in"), 80)
            for t in range(TT):
                for k in range(KD):
                    last = mm(ps[:, 6, t * SSD_HEADS:(t + 1) * SSD_HEADS], hT[:, k, t * P:(t + 1) * P],
                              wdt[:, k, :], start=(k == 0), stop=(k == KD - 1))
            last.then_inc(sem("decay_p"), 1)
            pe.wait_ge(sem("decay_v"), DECAY_V["da_ready"])
            for t in range(TT):
                mm(ps[:, 7, t * SSD_HEADS:(t + 1) * SSD_HEADS], tri[:, :], dts[:, DA, t, :], start=True, stop=True)
                last = mm(ps[:, 7, P + t * SSD_HEADS:P + (t + 1) * SSD_HEADS], ones[:, :], dts[:, DA, t, :],
                          start=True, stop=True)
            last.then_inc(sem("decay_p"), 1)
            pe.wait_ge(sem("decay_v"), DECAY_V["dts_ready"])
            pe.wait_ge(sem("short_free"), 2 + 8)

            def ssd_proj(k, g, par, turn):
                u = 2 * par
                if k == 0:
                    have("ssd", u, turn)
                if k == 4:
                    have("ssd", u + 1, turn)
                pe.wait_ge(sem("ssd_b01_free"), g * 6 + (k + 1))
                if k < 4:
                    w = unit("ssd", u, 0, KD, 512)
                    for kk in range(KD):
                        last = mm(ps[:, k % 2, :], w[:, kk, k * P:(k + 1) * P], hT[:, kk, :],
                                  start=(kk == 0), stop=(kk == KD - 1))
                else:
                    w = unit("ssd", u + 1, 0, KD, GW)
                    for h in range(2):
                        t = 2 * (k - 4) + h
                        for kk in range(KD):
                            last = mm(ps[:, k % 2, h * GW:(h + 1) * GW], hT[:, kk, t * P:(t + 1) * P],
                                      w[:, kk, :], start=(kk == 0), stop=(kk == KD - 1))
                last.then_inc(sem("ssd_proj"), 1)
                if k == 3:
                    pe.wait_ge(sem("ssd_proj"), g * 6 + 4)
                    pe.sem_inc(used[ring.slot("ssd", u)], 1)
                if k == 5:
                    pe.wait_ge(sem("ssd_proj"), g * 6 + 6)
                    pe.sem_inc(used[ring.slot("ssd", u + 1)], 1)

            def ssd_core(k, g, par):
                b, c = bcT[par][:, 0, :], bcT[par][:, 1, :]
                if k == 0:
                    pe.wait_ge(sem("ssd_silu"), g * 4 + 4)
                    pe.wait_ge(sem("ssd_b23_free"), g * 6 + 1)
                    for t in range(TT):
                        q = slice(t * P, (t + 1) * P)
                        nc.tensor.transpose(ps[:, 2, q], xsT[:, 0, q], ident[:, :])
                        nc.tensor.transpose(ps[:, 3, q], xsT[:, 1, q], ident[:, :])
                        last = nc.tensor.transpose(ps[:, 4, q], b[:, q], ident[:, :])
                    last.then_inc(sem("ssd_xb_T"), 1)
                    for t in range(TT):
                        q = slice(t * P, (t + 1) * P)
                        last = mm(ps[:, 5, q], b[:, q], c[:, q], start=True, stop=True)
                    last.then_inc(sem("ssd_cb"), 1)
                if 1 <= k <= 4:
                    t = k - 1
                    pe.wait_ge(sem("ssd_lm"), g * 4 + (t + 1))
                    pe.wait_ge(sem("ssd_x"), g * 2 + 2)
                    pe.wait_ge(sem("ssd_y_free"), g * 4 + (t + 1))
                    for h in range(HPG):
                        last = mm(ps[:, 6, h * HEAD:(h + 1) * HEAD], lm[t % 2][:, h, :],
                                  xdt[:, t, h * HEAD:(h + 1) * HEAD], start=True, stop=True)
                    if t > 0:
                        pe.wait_ge(sem("ssd_state"), g * 3 + t)
                        last = mm(ps[:, 6, GW:2 * GW], c[:, t * P:(t + 1) * P], state, start=True, stop=True)
                    if t < TT - 1:
                        last = mm(ps[:, 7, 0:GW], btok[:, t, :], xdd[:, t, :], start=True, stop=True)
                    last.then_inc(sem("ssd_y_p"), 1)
                if k <= 3:
                    t = k
                    pe.wait_ge(sem("ssd_gs"), g + 1)
                    pe.wait_ge(sem("ssd_b23_free"), g * 6 + (t + 2))
                    for h in range(HPG):
                        last = mm(ps[:, 2 + t % 2, h * P:(h + 1) * P],
                                  gs[par][:, DA, t, h:h + 1].to_broadcast([P, P]), tri[:, :],
                                  start=True, stop=True)
                    last.then_inc(sem("ssd_rowb"), 1)
                if k == 5:
                    pe.wait_ge(sem("ssd_yn"), g * 4 + 4)
                    pe.wait_ge(sem("ssd_b23_free"), g * 6 + 6)
                    for m in range(2):
                        for t in range(TT):
                            last = nc.tensor.transpose(ps[:, 2 + m, t * P:(t + 1) * P],
                                                       y[:, t, m * P:(m + 1) * P], ident[:, :])
                    last.then_inc(sem("ssd_y_p5"), 1)

            slots(pe, ssd_proj, ssd_core, 6)

            pe.wait_ge(sem("ssd_y_T"), 2 * SSD_GROUPS)
            pe.wait_ge(sem("ssd_b01_free"), 2 + 6 * SSD_GROUPS)
            with pe.Fori(0, 4) as i:
                for u in range(2):
                    have("merge", 2 * u, i)
                    pe.wait_ge(sem("merge_free"), i * 2 + (u + 1))
                    ada_columns(ADA_MERGE, ADA_N, i * 2 + u, 4 * u + 3)
                    for n, rhs in enumerate((hT, hT, scuT)):
                        w = unit("merge", 2 * u, 1024 * n, KD, P)
                        for k in range(KD):
                            last = mm(ps[:, 4 * u + n, :], w[:, k, :], rhs[:, k, :],
                                      start=(k == 0), stop=(k == KD - 1))
                        if n < 2:
                            last.then_inc(sem("merge_g"), 1)
                    spent(last, "merge", 2 * u)
                    have("merge", 2 * u + 1, i)
                    pe.wait_ge(sem("ada_free"), i * 2 + (u + ADA_MERGE["free"] + 1))
                    w = unit("merge", 2 * u + 1, 0, 16, P)
                    for k in range(16):
                        last = mm(ps[:, 4 * u + 3, :], w[:, k, :], yT[:, k, :],
                                  start=(k == 0), stop=(k == 15))
                    last.then_inc(sem("merge_y"), 1)
                    pe.wait_ge(sem("merge_y"), i * 2 + (u + 1))
                    pe.sem_inc(used[ring.slot("merge", 2 * u + 1)], 1)

            pe.wait_ge(sem("merge_free"), 2 + 7)
            ada_columns(ADA_MERGE, ADA_N, 8, 3)
            pe.wait_ge(sem("ada_free"), ADA_MERGE["free"] + 9)

            def project(n, name, rhs, ready, count):
                pe.wait_ge(sem(ready), count)
                for u in range(2):
                    have(name, u)
                    w = unit(name, u, 0, KD, 512)
                    for j in range(4):
                        for k in range(KD):
                            last = mm(ps[:, 4 * u + j, :], w[:, k, j * P:(j + 1) * P], rhs[:, k, :],
                                      start=(k == 0), stop=(k == KD - 1))
                        if j < 3:
                            last.then_inc(sem("branch_p"), 1)
                    spent(last, name, u)

            def from_T(n, src):
                pe.wait_ge(sem("branch_ready"), (n + 1) * KD)
                for t in range(TT):
                    for k in range(KD):
                        last = nc.tensor.transpose(ps[:, 2 * t + k // 4, (k % 4) * P:(k % 4 + 1) * P],
                                                   src[:, k, t * P:(t + 1) * P], ident[:, :])
                    last.then_inc(sem("res_b"), 1)

            project(0, "w_o", mergedT, "merge_free", 2 + 8)
            from_T(0, mixT)
            pe.wait_ge(sem("res_read"), 1)
            to_T(1, xhat, "ln1_x")

            pe.wait_ge(sem("rw_in"), 16)
            pe.wait_ge(sem("hT_ready"), 2 * KD)
            for t in range(TT):
                for k in range(KD):
                    last = mm(ps[:, 0, t * N_EXPERTS:(t + 1) * N_EXPERTS], hT[:, k, t * P:(t + 1) * P],
                              rw[:, k, :], start=(k == 0), stop=(k == KD - 1))
            last.then_inc(sem("route_p"), 1)

            have("shared", 0)
            w = unit("shared", 0, 0, 2, KD, D_EXPERT)
            for f in range(FE):
                for n in range(2):
                    for k in range(KD):
                        last = mm(ps[:, 4 + 2 * f + n, :], w[:, n, k, f * P:(f + 1) * P], hT[:, k, :],
                                  start=(k == 0), stop=(k == KD - 1))
                    if (f, n) != (FE - 1, 1):
                        last.then_inc(sem("sh_gu"), 1)
            spent(last, "shared", 0)
            pe.wait_ge(sem("route_v"), ROUTE_V["chosen"])
            for t in range(TT + 1):
                for m in range(min(t + 1, TT)):
                    last = mm(ps[:, 1, t * N_EXPERTS:(t + 1) * N_EXPERTS], tri[:, :] if m == t else ones[:, :],
                              rt[:, 2, m, :], start=(m == 0), stop=(m == min(t, TT - 1)))
            last.then_inc(sem("route_p"), 1)
            nc.tensor.transpose(ps[0:KD, 3, 0:P], mod[:, 40:48], ident[:, :]).then_inc(sem("route_p"), 1)
            have("shared", 1)
            pe.wait_ge(sem("sh_h"), FE)
            w = unit("shared", 1, 0, FE, D)
            for d in range(KD):
                if d >= 4:
                    pe.wait_ge(sem("sh_free"), d - 3)
                for k in range(FE):
                    last = mm(ps[:, 4 + d % 4, :], w[:, k, d * P:(d + 1) * P], hexp[:, k, :],
                              start=(k == 0), stop=(k == FE - 1))
                if d < KD - 1:
                    last.then_inc(sem("sh_d"), 1)
            spent(last, "shared", 1)

            pe.wait_ge(sem("route_v"), ROUTE_V["ends"])
            nc.tensor.transpose(ps[0:N_EXPERTS, 2, 0:P], scan[0][:, 32:96], ident[:, :]).then_inc(sem("route_p"), 1)
            pe.wait_ge(sem("route_v"), ROUTE_V["past_e"])
            mm(ps[:, 2, 0:NBLK], ones[0:N_EXPERTS, :], past_e[0:N_EXPERTS, :], start=True, stop=True).then_inc(sem("route_p"), 1)
            pe.wait_ge(sem("rows_out"), 16 * TT * PER_TOKEN + 16)
            pe.wait_ge(sem("route_v"), ROUTE_V["blk_e"])
            nc.tensor.transpose(ps[:, 2, 0:NBLK], rowt[0:NBLK, :], ident[0:NBLK, 0:NBLK]).then_inc(sem("route_p"), 1)

            def turn_rows(u, done):
                pe.wait_ge(sem(f"xg_in{u}"), done * 16 + 16)
                for k in range(KD):
                    last = nc.tensor.transpose(ps[:, k // 4, (k % 4) * P:(k % 4 + 1) * P], xg[u][:, k * P:(k + 1) * P],
                                               ident[:, :])
                last.then_inc(sem("moe_x_p"), 1)

            def block_gu(u, turn):
                b = turn * 2 + u
                if not (isinstance(b, int) and b == 0):
                    pe.wait_ge(sem("moe_h"), b)
                have("moe", 2 * u, turn)
                pe.wait_ge(sem("moe_x"), turn * (2 * KD) + KD * (u + 1))
                w = unit("moe", 2 * u, 0, 2, KD, D_EXPERT)
                for n in range(2):
                    for f in range(FE):
                        for k in range(KD):
                            last = mm(ps[:, 2 + n, f * BLOCK:(f + 1) * BLOCK], w[:, n, k, f * P:(f + 1) * P],
                                      xT[:, k, :], start=(k == 0), stop=(k == KD - 1))
                    if n == 0:
                        last.then_inc(sem("moe_g"), 1)
                spent(last, "moe", 2 * u)

            def block_down(u, turn):
                have("moe", 2 * u + 1, turn)
                pe.wait_ge(sem("moe_h"), turn * 2 + (u + 1))
                for n in range(2):
                    pe.wait_ge(sem(f"moe_y{n}"), turn * 2 + (u + 1))
                w = unit("moe", 2 * u + 1, 0, FE, D)
                for n in range(2):
                    for f in range(FE):
                        last = mm(ps[:, 4 + 2 * u + n, :], he[u][:, f, :], w[:, f, 512 * n:512 * n + 512],
                                  start=(f == 0), stop=(f == FE - 1))
                spent(last, "moe", 2 * u + 1)

            pe.wait_ge(sem("sh_free"), KD)
            turn_rows(0, 0)
            block_gu(0, 0)
            idle = turns_without_rows(pe)
            with pe.Fori(0, LAST) as i:
                with pe.If(i >= idle):
                    turn_rows(1, (i - idle) & 63)
                    block_down(0, i)
                    block_gu(1, i)
                    turn_rows(0, ((i - idle) & 63) + 1)
                    block_down(1, i)
                    block_gu(0, i + 1)
                with pe.Else():
                    pe.wait_ge(sem("moe_x"), i * (2 * KD) + KD)
                    pe.sem_inc(sem("moe_x_p"), 2)
                    pe.wait_ge(sem("moe_h"), i * 2 + 1)
                    pe.sem_inc(sem("moe_g"), 2)
                    for n in range(4):
                        pe.sem_inc(used[ring.slot("moe", n)], 1)
            turn_rows(1, (LAST - idle) & 63)
            block_down(0, LAST)
            block_gu(1, LAST)
            block_down(1, LAST)
            for n in range(2):
                pe.wait_ge(sem(f"moe_y{n}"), 2 + NBLK)
            pe.wait_ge(sem("moe_h"), NBLK)
            from_T(1, outT)
            pe.wait_ge(sem("res_read"), 2)
            to_T(2, xr, "res_x", TT)

            pe.wait_ge(sem("hT_ready"), 3 * KD)
            have("index", 0)
            w = unit("index", 0, 0, KD, KV_RANK)
            for t in range(TT):
                for k in range(KD):
                    last = mm(ps[:, t // 2, (t % 2) * KV_RANK:(t % 2 + 1) * KV_RANK], hT[:, k, t * P:(t + 1) * P],
                              w[:, k, :], start=(k == 0), stop=(k == KD - 1))
            last.then_inc(sem("index_p"), 1)
            w = unit("index", 0, 2048, KD, IDX_HEADS)
            for t in range(TT):
                for k in range(KD):
                    last = mm(ps[:, 2, t * IDX_HEADS:(t + 1) * IDX_HEADS], hT[:, k, t * P:(t + 1) * P],
                              w[:, k, :], start=(k == 0), stop=(k == KD - 1))
            last.then_inc(sem("index_p"), 1)
            w = unit("index", 0, 2112, KD, P)
            for k in range(KD):
                last = mm(ps[:, 3, :], w[:, k, :], hT[:, k, :], start=(k == 0), stop=(k == KD - 1))
            spent(last, "index", 0)
            have("index", 1)
            w = unit("index", 1, 0, KD, 512)
            for j in range(4):
                for k in range(KD):
                    last = mm(ps[:, 4 + j, :], w[:, k, j * P:(j + 1) * P], hT[:, k, :],
                              start=(k == 0), stop=(k == KD - 1))
                if j < 3:
                    last.then_inc(sem("iq_p"), 1)
            spent(last, "index", 1)
            pe.wait_ge(sem("ckvn"), TT)
            for t in range(TT):
                for r in range(2):
                    last = nc.tensor.transpose(ps[:, r, t * P:(t + 1) * P], ckvn[:, t, r * P:(r + 1) * P],
                                               ident[:, :])
            last.then_inc(sem("index_p"), 1)
            pe.wait_ge(sem("iqk"), 5)
            n = 0
            for qb in range(1, TT):
                for h in range(IDX_HEADS):
                    half = slice(64 * (h % 2), 64 * (h % 2) + 64)
                    pe.wait_ge(sem("idx_free"), n + 1)
                    mm(ps[:, 4 + n % 4, 0:(qb + 1) * P], iqT[half, h // 2, qb * P:(qb + 1) * P],
                       ikT[half, 0:(qb + 1) * P], start=True, stop=True).then_inc(sem("idx_p"), 1)
                    n += 1
            pe.wait_ge(sem("idx_free"), 4 + n)
            pe.wait_ge(sem("ckvT_ready"), 2)

            def attention(tag):
                dsa = tag == "dsa"
                past = NO_PAST if dsa else DSA_PAST

                def proj(k, g, par, turn):
                    q_out, k_out, v_out = ps[:, 5, :], ps[:, 6, :], ps[:, 7, :]
                    if k == 0:
                        have(tag, par, turn)
                    if k not in (1, 4, 7, 10):
                        return
                    if k == 1:
                        pe.wait_ge(sem("att_pfree"), g * 3 + 1 + past["pfree"])
                        w = unit(tag, par, 0, KD, P)
                        for kk in range(KD):
                            last = mm(q_out, w[:, kk, :], hT[:, kk, :], start=(kk == 0), stop=(kk == KD - 1))
                        last.then_inc(sem("att_proj"), 1)
                    if k == 4 and dsa:
                        w = unit(tag, par, 1024, KV_RANK)
                        for r in range(2):
                            last = nc.tensor.transpose(k_out[:, r * P:(r + 1) * P], w[:, r * P:(r + 1) * P],
                                                       ident[:, :])
                        last.then_inc(sem("uk_p"), 1)
                    if k == 7:
                        if dsa:
                            pe.wait_ge(sem("uk_T"), g + 1)
                            for r in range(2):
                                last = mm(k_out, ukT[:, r, :], ckvT[:, r, :], start=(r == 0), stop=(r == 1))
                        else:
                            w = unit(tag, par, 1024, KD, P)
                            for kk in range(KD):
                                last = mm(k_out, w[:, kk, :], hT[:, kk, :], start=(kk == 0), stop=(kk == KD - 1))
                        last.then_inc(sem("att_proj"), 1)
                    if k == 10:
                        for t in range(TT):
                            q = slice(t * P, (t + 1) * P)
                            if dsa:
                                w = unit(tag, par, 1280, 2, P)
                                for r in range(2):
                                    last = mm(v_out[:, q], ckvT[:, r, q], w[:, r, :], start=(r == 0), stop=(r == 1))
                            else:
                                w = unit(tag, par, 2048, KD, P)
                                for kk in range(KD):
                                    last = mm(v_out[:, q], hT[:, kk, q], w[:, kk, :], start=(kk == 0),
                                              stop=(kk == KD - 1))
                        last.then_inc(sem("att_proj"), 1)
                        pe.wait_ge(sem("att_proj"), g * 3 + 3 + past["proj"])
                        pe.sem_inc(used[par], 1)

                def core(k, g, par):
                    q_in, k_in, v_in = (qkv[par][:, n, :] for n in range(3))
                    if k == 0:
                        pe.wait_ge(sem("att_qkv"), g * 3 + 3 + past["qkv"])
                    if k < 8:
                        qb, m = k // 2, k % 2
                        half = slice(64 * m, 64 * m + 64)
                        pe.wait_ge(sem("att_s_free"), g * 8 + (k + 1) + past["s_free"])
                        mm(ps[:, k % 2, 0:(qb + 1) * P], q_in[half, qb * P:(qb + 1) * P],
                           k_in[half, 0:(qb + 1) * P], start=True, stop=True).then_inc(sem("att_s"), 1)
                    if 2 <= k < 10 and (dsa or k % 2):
                        n = k - 2
                        qb = n // 2
                        b = 2 + (n if dsa else qb) % 2
                        if dsa:
                            pe.wait_ge(sem("att_pn"), g * 8 + (n + 1) + past["pn"])
                            pe.wait_ge(sem("att_pT"), g * 8 + (n + 1) + past["pT"])
                        else:
                            pe.wait_ge(sem("att_pn"), g * 4 + (qb + 1) + past["pn"])
                            pe.wait_ge(sem("att_pT"), g * 4 + (qb + 1) + past["pT"])
                        for sb_ in range(qb + 1):
                            last = nc.tensor.transpose(ps[:, b, sb_ * P:(sb_ + 1) * P],
                                                       lbuf[:, n % 4, sb_ * P:(sb_ + 1) * P], ident[:, :])
                        last.then_inc(sem("att_tr"), 1)
                    if k == 10:
                        pe.wait_ge(sem("att_pT"), g * (8 if dsa else 4) + ((8 if dsa else 4) + 2) + past["pT"])
                        pe.wait_ge(sem("att_o_free"), g + 1 + past["o_free"])
                        if dsa:
                            for m in range(2):
                                for s_ in range(TT):
                                    last = mm(ps[64 * m:64 * m + 64, 4, s_ * P:], v_in[:, s_ * P + 64 * m:s_ * P + 64 * m + 64],
                                              pT[:, m, s_, s_ * P:], start=(s_ == 0), stop=(s_ == TT - 1))
                        else:
                            for qb in range(TT):
                                for s_ in range(qb + 1):
                                    last = mm(ps[:, 4, qb * P:(qb + 1) * P], pT[:, 0, s_, qb * P:(qb + 1) * P],
                                              v_in[:, s_ * P:(s_ + 1) * P], start=(s_ == 0), stop=(s_ == qb))
                        last.then_inc(sem("att_pv"), 1)
                    if k == 11 and not dsa:
                        pe.wait_ge(sem("diff_on"), g * 4 + 4)
                        for qb in range(TT):
                            last = nc.tensor.transpose(ps[:, 4, qb * P:(qb + 1) * P], onrm[:, qb, :], ident[:, :])
                        last.then_inc(sem("diff_oT"), 1)

                slots(pe, proj, core, 12)

            attention("dsa")
            pe.wait_ge(sem("att_o_free"), 1 + 8)
            project(1, "a_w_o", oT, "att_o_free", 1 + 8)
            from_T(2, outT)

            def mlp(layer):
                pe.wait_ge(sem("res_read"), 3 + 2 * layer)
                to_T(3 + 2 * layer, xr, "res_x", (2 + 2 * layer) * TT)
                pe.wait_ge(sem("hT_ready"), KD * (4 + 2 * layer))
                name = f"up{layer}"
                with pe.Fori(0, 2) as i:
                    for u in range(4):
                        have(name, u, i)
                        w = unit(name, u, 0, KD, 512)
                        for j in range(4):
                            n = 4 * u + j
                            pe.wait_ge(sem("up_free"), i * 16 + (32 * layer + n + 1))
                            for k in range(KD):
                                last = mm(ps[:, n % 8, :], w[:, k, j * P:(j + 1) * P], hT[:, k, :],
                                          start=(k == 0), stop=(k == KD - 1))
                            if j < 3:
                                last.then_inc(sem("up_p"), 1)
                        spent(last, name, u)
                pe.wait_ge(sem("up_squared"), 32 * (layer + 1))
                name = f"down{layer}"
                n_out = 3 + 2 * layer
                with pe.Fori(0, 2) as i:
                    for u in range(4):
                        have(name, u, i)
                        w = unit(name, u, 0, D_FF // P, P)
                        pe.wait_ge(sem("branch_ready"), i * 4 + (n_out * KD + u - 3))
                        for k in range(D_FF // P):
                            last = mm(ps[:, u, :], w[:, k, :], h1T[:, k, :], start=(k == 0),
                                      stop=(k == D_FF // P - 1))
                        spent(last, name, u)
                from_T(n_out, outT)

            mlp(0)
            pe.wait_ge(sem("res_read"), 4)
            to_T(4, xr, "res_x", 3 * TT)
            pe.wait_ge(sem("hT_ready"), 5 * KD)
            attention("diff")
            project(2, "b_w_o", oT, "att_o_free", 1 + 16)
            from_T(4, outT)
            mlp(1)

        @block.scalar
        def _(act):
            A = nc.scalar.activation
            link = Link(act, sem("act_link"))
            act.wait_ge(sem("start_p"), START_P["pcol_T"])
            for n, r in enumerate(PROWS):
                link.mark(A(pcol[:, n, 0:r], ps[:, n, 0:r], ACT.Copy))
            link.wait()
            act.sem_inc(sem("pcol_ready"), 1)
            link(A(csil[:, :], pcol[:, 0, 0:16], ACT.Tanh, scale=0.5))
            act.sem_inc(sem("c_tanh"), 1)
            act.wait_ge(sem("start_p"), START_P["bias_p"])
            A(rbv[0:HEADS, 0:512], ps[0:HEADS, 5, :], ACT.Copy).then_inc(sem("bias_v"), 1)
            A(rbv[0:HEADS, 512:NVEC], ps[0:HEADS, 6, 0:P], ACT.Copy).then_inc(sem("bias_v"), 1)
            act.wait_ge(sem("lam_sum"), 1)
            A(lamv[:, 0:2], lamv[:, 0:2], ACT.Exp).then_inc(sem("lam_exp"), 1)

            def to_T(n, scale, bias):
                act.wait_ge(sem("hT_turned"), n + 1)
                for k in range(KD):
                    A(hT[:, k, :], ps[:, k, :], ACT.Identity, scale=scale[:, k:k + 1],
                      bias=bias[:, k:k + 1]).then_inc(sem("hT_ready"), 1)

            act.wait_ge(sem("mod_ready"), 1)
            to_T(0, mod[:, 8:16], mod[:, 0:8])

            with act.Fori(0, 4) as i:
                for u in range(2):
                    act.wait_ge(sem("short_p"), i * 4 + (2 * u + 1))
                    act.wait_ge(sem("short_v"), i * 2 + (u + 1))
                    A(sc_c[:, u, :], ps[:, 3 * u + 1, :], ACT.Copy).then_inc(sem("short_c"), 1)

            act.wait_ge(sem("decay_v"), DECAY_V["dt_abs"])
            A(dtw[:, 1, :, :], dtw[:, 1, :, :], ACT.Exp, scale=-1.0).then_inc(sem("dt_exp"), 1)
            A(alog, alog, ACT.Exp).then_inc(sem("dt_exp"), 1)
            act.wait_ge(sem("decay_p"), DECAY_P["acs_p"])
            act.wait_ge(sem("decay_v"), DECAY_V["dec_arg"])
            flat = lambda n: dts[:, n, :, :].rearrange("p t h -> p (t h)")
            A(flat(ODEC), ps[:, 7, 0:P], ACT.Exp).then_inc(sem("decays"), 1)
            A(flat(CDEC), ps[:, 7, P:2 * P], ACT.Exp).then_inc(sem("decays"), 1)
            A(flat(DEC), flat(DEC), ACT.Exp).then_inc(sem("decays"), 1)

            def ssd_proj(k, g, par, turn):
                if k < 4:
                    act.wait_ge(sem("ssd_conv"), g * 4 + (k + 1))
                    act.wait_ge(sem("ssd_th_free"), g * 4 + (k + 1))
                    A(th[:, k % 2, :], acc[:, k % 2, :], ACT.Tanh).then_inc(sem("ssd_tanh"), 1)
                else:
                    h = k - 4
                    flat2 = lambda v: v.rearrange("p t c -> p (t c)")
                    act.wait_ge(sem("ssd_proj"), g * 6 + (k + 1))
                    act.wait_ge(sem("ssd_silu"), g * 4 + (h + 3))
                    act.wait_ge(sem("ssd_zs_free"), g + 1)
                    A(th[:, h, :], ps[:, k % 2, :], ACT.Tanh, scale=0.5).then_inc(sem("ssd_ztanh"), 1)
                    link(A(flat2(zs[par][:, 2 * h:2 * h + 2, :]), ps[:, k % 2, :], ACT.Copy, scale=0.5))
                    act.sem_inc(sem("ssd_b01_free"), 1)
                    act.sem_inc(sem("ssd_zh"), 1)

            def ssd_core(k, g, par):
                if k == 0:
                    act.wait_ge(sem("ssd_xb_T"), g + 1)
                    act.wait_ge(sem("ssd_y_p"), g * 4 + 1)
                    for m in range(2):
                        link.mark(A(xtok[:, :, m * P:(m + 1) * P],
                                    ps[:, 2 + m, :].rearrange("p (t c) -> p t c", t=TT), ACT.Copy))
                    link(A(btok[:, :, :].rearrange("p t c -> p (t c)"), ps[:, 4, :], ACT.Copy))
                    act.sem_inc(sem("ssd_b23_free"), 1)
                    act.sem_inc(sem("ssd_xtok"), 1)
                if k <= 3:
                    act.wait_ge(sem("ssd_seg"), g * 4 + (k + 1))
                    v = lm[k % 2][:, :, :].rearrange("p h c -> p (h c)")
                    A(v, v, ACT.Exp).then_inc(sem("ssd_exp"), 1)
                if k == 4:
                    act.wait_ge(sem("ssd_gated"), g + 1)
                    for t in range(TT):
                        link(A(ysq, y[:, t, :], ACT.Square, accum_out=stats[:, t, 0:1]))
                    act.sem_inc(sem("ssd_sq"), 1)
                    act.wait_ge(sem("ssd_rstd"), g + 1)
                    for t in range(TT):
                        A(y[:, t, :], y[:, t, :], ACT.Copy, scale=rstd[:, t:t + 1]).then_inc(sem("ssd_yn"), 1)
                if k == 5:
                    act.wait_ge(sem("ssd_y_p5"), g + 1)
                    for m in range(2):
                        A(yT[:, bass.ds(g * 2 + m, 1), :], ps[:, 2 + m, :], ACT.Copy,
                          scale=norm_w[:, bass.ds(g * 2 + m, 1)]).then_inc(sem("ssd_y_T"), 1)
                    act.wait_ge(sem("ssd_y_T"), g * 2 + 2)
                    act.sem_inc(sem("ssd_b23_free"), 1)

            act.wait_ge(sem("bias_out"), 16)
            slots(act, ssd_proj, ssd_core, 6, (link, 9))

            with act.Fori(0, 4) as i:
                for u in range(2):
                    act.wait_ge(sem("merge_g"), i * 4 + (2 * u + 2))
                    act.wait_ge(sem("merge_used"), i * 2 + (u + 1))
                    for n in range(2):
                        A(mg[:, u, n, :], ps[:, 4 * u + n, :], ACT.Tanh, scale=0.5).then_inc(sem("merge_t"), 1)

            def evac(n, name, dst, scale):
                for k in range(KD):
                    u, j = k // 4, k % 4
                    if j < 3:
                        act.wait_ge(sem("branch_p"), 6 * n + 3 * u + j + 1)
                    else:
                        act.wait_ge(used[ring.slot(name, u)], ring.free(name, u, 0) + 1)
                    A(dst[:, k, :], ps[:, k, :], ACT.Copy, scale=scale[:, k:k + 1]).then_inc(sem("branch_ready"), 1)

            def normalize(n):
                for t in range(TT):
                    act.wait_ge(sem("res_stats"), TT * n + t + 1)
                    A(xr[:, t, :], xr[:, t, :], ACT.Identity, scale=rstd[:, t:t + 1],
                      bias=rtmp[:, 1, t:t + 1]).then_inc(sem("res_norm"), 1)

            evac(0, "w_o", mixT, mod[:, 16:24])
            normalize(0)
            to_T(1, mod[:, 32:40], mod[:, 24:32])
            act.wait_ge(sem("route_p"), ROUTE_P["router_p"])
            link(A(rt[:, 0, :, :].rearrange("p t e -> p (t e)"), ps[:, 0, 0:TT * N_EXPERTS], ACT.Exp, scale=-1.0))
            act.sem_inc(sem("router_e"), 1)
            for f in range(FE):
                act.wait_ge(sem("sh_gu"), 2 * f + 1)
                A(tg[:, f, :], ps[:, 4 + 2 * f, :], ACT.Tanh, scale=0.5).then_inc(sem("sh_t"), 1)
            act.wait_ge(sem("route_p"), ROUTE_P["g2_p"])
            A(g2r[0:KD, :], ps[0:KD, 3, 0:P], ACT.Copy).then_inc(sem("g2_r"), 1)
            for d in range(KD):
                if d < KD - 1:
                    act.wait_ge(sem("sh_d"), d + 1)
                else:
                    act.wait_ge(used[1], ring.free("shared", 1, 0) + 1)
                A(outT[:, d, :], ps[:, 4 + d % 4, :], ACT.Copy, scale=mod[:, 40 + d:41 + d]).then_inc(sem("sh_free"), 1)

            def block_x(u, turn):
                act.wait_ge(sem("moe_x_p"), turn * 2 + (u + 3))
                for k in range(KD):
                    A(xT[:, k, :], ps[:, k // 4, (k % 4) * P:(k % 4 + 1) * P], ACT.Identity,
                      scale=mod[:, 32 + k:33 + k], bias=mod[:, 24 + k:25 + k]).then_inc(sem("moe_x"), 1)

            def block_tanh(u, turn):
                act.wait_ge(sem("moe_g"), turn * 2 + (u + 1))
                A(tge, ps[:, 2, 0:FE * BLOCK], ACT.Tanh, scale=0.5).then_inc(sem("moe_t"), 1)

            def block_y(u, turn):
                act.wait_ge(sem(f"y_out{u}"), turn * 16 + 16)
                act.wait_ge(used[ring.slot("moe", 2 * u + 1)], ring.free("moe", 2 * u + 1, turn) + 1)
                A(ybuf[u][:, 0:512], ps[:, 4 + 2 * u, :], ACT.Copy).then_inc(sem("moe_y0"), 1)
                for n in range(2):
                    act.wait_ge(sem(f"moe_y{n}"), turn * 2 + (u + 3))
                act.dma_start(y_rows[bass.ds(turn * (2 * BLOCK) + u * BLOCK, BLOCK), :], ybuf[u]).then_inc(
                    sem(f"y_out{u}"), 16)

            act.wait_ge(sem("y_rows_set"), 16 * 16)
            block_x(0, 0)
            block_tanh(0, 0)
            idle = turns_without_rows(act)
            with act.Fori(0, LAST) as i:
                with act.If(i >= idle):
                    block_x(1, i)
                    block_y(0, i)
                    block_tanh(1, i)
                    block_x(0, i + 1)
                    block_y(1, i)
                    block_tanh(0, i + 1)
                with act.Else():
                    act.wait_ge(sem("moe_x_p"), i * 2 + 5)
                    act.sem_inc(sem("moe_x"), 2 * KD)
                    act.wait_ge(sem("moe_g"), i * 2 + 3)
                    act.sem_inc(sem("moe_t"), 2)
                    act.sem_inc(sem("moe_y0"), 2)
                    for u in range(2):
                        act.sem_inc(sem(f"y_out{u}"), 16)
            block_x(1, LAST)
            block_y(0, LAST)
            block_tanh(1, LAST)
            block_y(1, LAST)
            act.wait_ge(sem("sh_free"), KD)
            act.sem_inc(sem("branch_ready"), KD)
            normalize(1)
            to_T(2, mod[:, 56:64], mod[:, 48:56])

            act.wait_ge(sem("index_p"), INDEX_P["ckv_p"])
            for t in range(TT):
                v = ps[:, t // 2, (t % 2) * KV_RANK:(t % 2 + 1) * KV_RANK]
                link(A(ckvn[:, t, :], v, ACT.Square, accum_out=stats[:, t, 0:1]))
            act.sem_inc(sem("ckv_sq"), 1)
            act.wait_ge(used[ring.slot("index", 0)], ring.free("index", 0, 0) + 1)
            A(ikT, ps[:, 3, :], ACT.Copy).then_inc(sem("iqk"), 1)
            for j in range(4):
                if j < 3:
                    act.wait_ge(sem("iq_p"), j + 1)
                else:
                    act.wait_ge(used[ring.slot("index", 1)], ring.free("index", 1, 0) + 1)
                A(iqT[:, j, :], ps[:, 4 + j, :], ACT.Copy).then_inc(sem("iqk"), 1)
            act.wait_ge(sem("ckv_rstd"), 1)
            for t in range(TT):
                v = ps[:, t // 2, (t % 2) * KV_RANK:(t % 2 + 1) * KV_RANK]
                A(ckvn[:, t, :], v, ACT.Copy, scale=rstd[:, t:t + 1]).then_inc(sem("ckvn"), 1)
            act.wait_ge(sem("index_p"), INDEX_P["ckv_T"])
            for r in range(2):
                A(ckvT[:, r, :], ps[:, r, :], ACT.Copy, scale=kv_norm[:, r:r + 1]).then_inc(sem("ckvT_ready"), 1)
            n = 0
            for qb in range(1, TT):
                for h in range(IDX_HEADS):
                    act.wait_ge(sem("idx_p"), n + 1)
                    act.wait_ge(sem("idx_s"), n + 1)
                    A(rl[:, n % 2, 0:(qb + 1) * P], ps[:, 4 + n % 4, 0:(qb + 1) * P],
                      ACT.Relu).then_inc(sem("idx_free"), 1)
                    n += 1
            act.wait_ge(sem("idx_s"), 2 + n)

            def attention(tag):
                dsa = tag == "dsa"
                past = NO_PAST if dsa else DSA_PAST
                per = 8 if dsa else 4

                def proj(k, g, par, turn):
                    n = {2: 0, 8: 1, 11: 2}.get(k)
                    if k == 5 and dsa:
                        act.wait_ge(sem("uk_p"), g + 1)
                        A(ukT[:, :, :].rearrange("p r c -> p (r c)"), ps[:, 6, 0:KV_RANK],
                          ACT.Copy).then_inc(sem("uk_T"), 1)
                    if n is not None:
                        act.wait_ge(sem("att_proj"), g * 3 + (n + 1) + past["proj"])
                        A(qkv[par][:, n, :], ps[:, 5 + n, :], ACT.Copy).then_inc(sem("att_qkv"), 1)
                    if k == 11:
                        act.wait_ge(sem("att_qkv"), g * 3 + 3 + past["qkv"])
                        act.sem_inc(sem("att_pfree"), 3)

                def core(k, g, par):
                    if k < 8:
                        qb, m = k // 2, k % 2
                        v = lbuf[:, k % 4, 0:(qb + 1) * P]
                        act.wait_ge(sem("att_l"), g * 8 + (k + 1) + past["l"])
                        A(v, v, ACT.Exp, bias=nmax[:, k:k + 1],
                          accum_out=rsum[:, k:k + 1]).then_inc(sem("att_p"), 1)
                    if 3 <= k < 11 and (dsa or k % 2 == 0):
                        n = k - 3
                        qb, m = n // 2, (n % 2 if dsa else 0)
                        j = n if dsa else qb
                        act.wait_ge(sem("att_tr"), g * per + (j + 1 + (4 if dsa else 2)) + past["tr"])
                        if j == 0:
                            act.wait_ge(sem("att_pv"), g + 1 + past["pv"])
                        A(pT[:, m, 0:qb + 1, qb * P:(qb + 1) * P],
                          ps[:, 2 + j % 2, 0:(qb + 1) * P].rearrange("p (s q) -> p s q", s=qb + 1),
                          ACT.Copy).then_inc(sem("att_pT"), 1)
                    if k == 11:
                        act.wait_ge(sem("att_pv"), g + 2 + past["pv"])
                        if dsa:
                            A(oT[:, bass.ds(g, 1), :], ps[:, 4, :], ACT.Copy).then_inc(sem("att_o_free"), 1)
                        else:
                            for qb in range(TT):
                                link(A(onrm[:, qb, :], ps[:, 4, qb * P:(qb + 1) * P], ACT.Square,
                                       accum_out=osq[:, qb:qb + 1]))
                            act.sem_inc(sem("diff_osq"), 1)
                            act.wait_ge(sem("diff_rstd"), g + 1)
                            for qb in range(TT):
                                A(onrm[:, qb, :], ps[:, 4, qb * P:(qb + 1) * P], ACT.Copy,
                                  scale=ortmp[:, 2, qb:qb + 1]).then_inc(sem("diff_on"), 1)
                            act.wait_ge(sem("diff_oT"), g + 1)
                            A(oT[:, bass.ds(g, 1), :], ps[:, 4, :], ACT.Copy,
                              scale=subln).then_inc(sem("att_o_free"), 1)

                slots(act, proj, core, 12, (link, 0 if dsa else 4))

            attention("dsa")
            evac(1, "a_w_o", outT, mod[:, 64:72])
            normalize(2)

            def mlp(layer):
                m0 = 48 * (layer + 1)
                to_T(3 + 2 * layer, mod[:, m0 + 32:m0 + 40], mod[:, m0 + 24:m0 + 32])
                name = f"up{layer}"
                with act.Fori(0, 2) as i:
                    for n in range(16):
                        u, j = n // 4, n % 4
                        if j < 3:
                            act.wait_ge(sem("up_p"), i * 12 + (24 * layer + 3 * u + j + 1))
                        else:
                            act.wait_ge(used[u], ring.free(name, u, i) + 1)
                        A(h1T[:, bass.ds(i * 16 + n, 1), :], ps[:, n % 8, :], ACT.Relu).then_inc(sem("up_free"), 1)
                name = f"down{layer}"
                with act.Fori(0, 2) as i:
                    for u in range(4):
                        act.wait_ge(used[u], ring.free(name, u, i) + 1)
                        A(outT[:, bass.ds(i * 4 + u, 1), :], ps[:, u, :], ACT.Copy,
                          scale=mod[:, bass.ds(i * 4 + (m0 + 40 + u), 1)]).then_inc(sem("branch_ready"), 1)
                normalize(3 + 2 * layer)

            mlp(0)
            to_T(4, mod[:, 104:112], mod[:, 96:104])
            attention("diff")
            evac(2, "b_w_o", outT, mod[:, 112:120])
            normalize(4)
            mlp(1)

        @block.vector
        def _(dve):
            V = nc.vector
            link = Link(dve, sem("dve_link"))
            for name, n in (("ada_free", 1), ("short_free", 2), ("short_v", 2), ("ssd_b01_free", 2),
                            ("ssd_b23_free", 1), ("ssd_y_free", 1), ("ssd_y_p", 1), ("ssd_th_free", 2),
                            ("ssd_zs_free", 2), ("merge_free", 2), ("merge_used", 2),
                            ("moe_x_p", 2), ("moe_y0", 2), ("moe_y1", 2), ("y_out0", 16), ("y_out1", 16),
                            ("idx_free", 4), ("idx_s", 2),
                            ("att_pfree", 1), ("att_s_free", 2), ("att_pT", 2), ("att_o_free", 1),
                            ("att_tr", 4), ("att_pv", 1), ("att_strip_free", 2),
                            ("up_free", 8)):
                dve.sem_inc(sem(name), n)

            def root(r, v, tmp):
                link(V.tensor_scalar(r.bitcast(I32), v.bitcast(I32), -0.5, float(0x5F3759DF), ALU.mult, ALU.add))
                for _ in range(NEWTON):
                    link(V.tensor_tensor(tmp, r, r, ALU.mult))
                    link(V.scalar_tensor_tensor(tmp, tmp, -0.5, v, ALU.mult, ALU.mult))
                    link(V.scalar_tensor_tensor(r, tmp, 1.5, r, ALU.add, ALU.mult))

            def moments(t, src):
                for h in range(2):
                    link.mark(V.bn_stats(stats[:, t, 6 * h:6 * h + 6], src[:, t, 512 * h:512 * h + 512]))
                link.wait()
                link(V.bn_aggr(mv[:, t, :], stats[:, t, :]))
                link(V.tensor_scalar(rtmp[:, 0, t:t + 1], mv[:, t, 1:2], EPS, None, ALU.add))
                root(rstd[:, t:t + 1], rtmp[:, 0, t:t + 1], rtmp[:, 1, t:t + 1])

            def layer_norm(t, src, dst):
                moments(t, src)
                return V.tensor_scalar(dst[:, t, :], src[:, t, :], mv[:, t, 0:1], rstd[:, t:t + 1],
                                       ALU.subtract, ALU.mult)

            dve.wait_ge(sem("x_in"), 16)
            for t in range(TT):
                layer_norm(t, xr, xhat).then_inc(sem("ln0_x"), 1)

            dve.wait_ge(sem("pcol_ready"), 1)
            dve.wait_ge(sem("c_tanh"), 1)
            link(V.scalar_tensor_tensor(csil[:, :], csil[:, :], 1.0, pcol[:, 0, 0:16], ALU.add, ALU.mult))
            link(V.tensor_scalar(csil[:, :], csil[:, :], 0.5, None, ALU.mult))
            link.mark(V.tensor_scalar(pcol[:, 2, :], pcol[:, 2, :], 0.5, None, ALU.mult))
            link(V.tensor_scalar(conv_b, conv_b, 0.5, None, ALU.mult))

            dve.wait_ge(sem("lam_in"), 16)
            for n in range(2):
                link(V.tensor_tensor(lamb[:, 2 * n, :], lamb[:, 2 * n, :], lamb[:, 2 * n + 1, :], ALU.mult))
                link(V.reduce_sum(lamv[:, n:n + 1], lamb[:, 2 * n, :], AX_X))
            dve.sem_inc(sem("lam_sum"), 1)
            dve.wait_ge(sem("lam_exp"), 1)
            link(V.tensor_tensor(lamv[:, 2:3], lamv[:, 1:2], lamv[:, 0:1], ALU.subtract))
            link.mark(V.tensor_scalar(lamv[:, 3:4], lamv[:, 2:3], -LAM_INIT, None, ALU.add))
            link(V.tensor_scalar(subln, subln, 1.0 - LAM_INIT, None, ALU.mult))

            def weigh(dst, w, c):
                for k in range(KD):
                    if k == 0:
                        ins = V.tensor_scalar(dst, w[:, k, :], c[:, k:k + 1], None, ALU.mult)
                    else:
                        ins = V.scalar_tensor_tensor(dst, w[:, k, :], c[:, k:k + 1], dst, ALU.mult, ALU.add)
                    link(ins)
                dve.sem_inc(sem("ada_sum"), 1)

            for u in range(4):
                dve.wait_ge(landed[ring.slot("ada", u)], ring.full("ada", u, 0))
                weigh(ada0[u], unit("ada", u, 0, KD, 512), csil[:, 0:KD])
                dve.sem_inc(used[ring.slot("ada", u)], 1)
            dve.wait_ge(sem("ada_p"), 1)
            link(V.tensor_tensor(mod[:, 0:16], ps[:, 4, 0:16], pcol[:, 0, 16:32], ALU.add))
            dve.sem_inc(sem("ada_free"), 1)
            link(V.tensor_scalar(mod[:, 8:16], mod[:, 8:16], 1.0, None, ALU.add))
            dve.sem_inc(sem("mod_ready"), 1)

            def take_columns(past, chunks, step, bank):
                n = chunks * ADA_W // P
                dve.wait_ge(sem("ada_p"), step + (past["p"] + 1))
                link(V.tensor_copy(modx[:, bass.ds(step * n, n)], ps[:, bank, 0:n]))
                dve.sem_inc(sem("ada_free"), 1)

            def weigh_chunks(past, chunks, i, u):
                for c in range(chunks):
                    dve.wait_ge(sem(f"adaw_in{c % 2}"),
                                i * (16 * chunks) + (past["into"] + 8 * chunks * u + 16 * (c // 2 + 1)))
                    weigh(adas[:, c, :], adaw[c % 2], csil[:, 0:KD] if past is ADA_SHORT else csil[:, KD:2 * KD])

            V.memset(adas, 0.0).then_inc(sem("ada_sum"), 1)

            with dve.Fori(0, 4) as i:
                link.enter(i, 8 + 2 + 2 * ADA_S * KD)
                for u in range(2):
                    take_columns(ADA_SHORT, ADA_S, i * 2 + u, 6 + u)
                    weigh_chunks(ADA_SHORT, ADA_S, i, u)
                    j = i * 2 + u
                    w = [sc_w[:, n, bass.ds(j, 1)] for n in range(3)]
                    dve.wait_ge(sem("short_p"), i * 4 + (2 * u + 2))
                    dve.wait_ge(sem("short_c"), i * 2 + (u + 1))
                    link(V.tensor_tensor(sc_v[:, u, :], sc_c[:, u, :], ps[:, 3 * u + 2, :], ALU.mult))
                    dve.sem_inc(sem("short_v"), 1)
                    link(V.tensor_scalar(sc_u[:, u, :], sc_v[:, u, :], w[2], None, ALU.mult))
                    for n, s in ((1, 1), (0, 2)):
                        link(V.scalar_tensor_tensor(sc_u[:, u, s:], sc_v[:, u, :T - s], w[n],
                                                    sc_u[:, u, s:], ALU.mult, ALU.add))
                    dve.wait_ge(used[ring.slot("short", u)], ring.free("short", u, i) + 1)
                    V.tensor_tensor(scuT[:, bass.ds(j, 1), :], sc_u[:, u, :], ps[:, 3 * u, :],
                                    ALU.mult).then_inc(sem("short_free"), 1)
                link.leave(4)
            take_columns(ADA_SHORT, ADA_S, 8, 6)
            link(V.tensor_tensor(mod[:, 16:48], modx[:, 4:36], pcol[:, 0, 32:64], ALU.add))
            link.mark(V.tensor_scalar(mod[:, 32:40], mod[:, 32:40], 1.0, None, ALU.add))
            link(V.tensor_scalar(mod[:, 16:24], mod[:, 16:24], 0.5, None, ALU.mult))

            v4 = lambda n: dtw[:, n, :, :]
            f4 = lambda n: dtw[:, n, :, :].rearrange("p t h -> p (t h)")
            fd = lambda n: dts[:, n, :, :].rearrange("p t h -> p (t h)")
            row = lambda r: r.unsqueeze(1).to_broadcast([P, TT, SSD_HEADS])
            dve.wait_ge(sem("decay_p"), DECAY_P["dt_p"])
            link(V.tensor_tensor(v4(0), ps[:, 6, 0:P].rearrange("p (t h) -> p t h", t=TT), row(dtb), ALU.add))
            link(V.tensor_scalar(f4(2), f4(0), -1.0, None, ALU.mult))
            link(V.tensor_tensor(f4(1), f4(0), f4(2), ALU.max))
            dve.sem_inc(sem("decay_v"), 1)
            dve.wait_ge(sem("dt_exp"), 2)
            link(V.tensor_scalar(f4(2), f4(1), 2.0, None, ALU.add))
            link(V.reciprocal(f4(2), f4(2)))
            link(V.tensor_tensor(f4(2), f4(2), f4(1), ALU.mult))
            link(V.tensor_tensor(f4(1), f4(2), f4(2), ALU.mult))
            link(V.tensor_scalar(f4(3), f4(1), 1.0 / 17, None, ALU.mult))
            for n in (15, 13, 11, 9, 7, 5, 3):
                link(V.scalar_tensor_tensor(f4(3), f4(3), 1.0 / n, f4(1), ALU.add, ALU.mult))
            link(V.scalar_tensor_tensor(f4(3), f4(3), 1.0, f4(2), ALU.add, ALU.mult))
            link(V.tensor_scalar(f4(0), f4(0), 0.0, None, ALU.max))
            link(V.scalar_tensor_tensor(fd(DT), f4(3), 2.0, f4(0), ALU.mult, ALU.add))
            link(V.scalar_tensor_tensor(dts[:, DA, :, :], dts[:, DT, :, :], -1.0, row(alog), ALU.mult, ALU.mult))
            dve.sem_inc(sem("decay_v"), 1)
            link(V.tensor_copy(dts[:, DSK, :, :], row(dskip)))
            dve.wait_ge(sem("decay_p"), DECAY_P["acs_p"])
            link(V.tensor_copy(fd(ACS), ps[:, 7, 0:P]))
            link(V.tensor_tensor(fd(DEC), ps[:, 7, P:2 * P], fd(ACS), ALU.subtract))
            dve.sem_inc(sem("decay_v"), 1)
            dve.wait_ge(sem("decays"), 3)
            dve.sem_inc(sem("decay_v"), 1)

            def ssd_silu(k, g, par):
                dst = xsT[:, k, :] if k < 2 else bcT[par][:, k - 2, :]
                dve.wait_ge(sem("ssd_tanh"), g * 4 + (k + 1))
                V.scalar_tensor_tensor(dst, th[:, k % 2, :], 1.0, acc[:, k % 2, :], ALU.add,
                                       ALU.mult).then_inc(sem("ssd_silu"), 1)

            def ssd_proj(k, g, par, turn):
                if k < 4:
                    j = (g * 2 + k) if k < 2 else (g + (16 + 8 * (k - 2)))
                    w = [conv_w[:, n, bass.ds(j, 1)] for n in range(4)]
                    dve.wait_ge(sem("ssd_proj"), g * 6 + (k + 1))
                    link(V.tensor_scalar(acc[:, k % 2, :], ps[:, k % 2, :], w[3], conv_b[:, bass.ds(j, 1)],
                                         ALU.mult, ALU.add))
                    for n, s in ((2, 1), (1, 2), (0, 3)):
                        link(V.scalar_tensor_tensor(acc[:, k % 2, s:], ps[:, k % 2, :T - s], w[n],
                                                    acc[:, k % 2, s:], ALU.mult, ALU.add))
                    dve.sem_inc(sem("ssd_b01_free"), 1)
                    dve.sem_inc(sem("ssd_conv"), 1)
                    ssd_silu(k, g, par)
                    dve.wait_ge(sem("ssd_silu"), g * 4 + (k + 1))
                    dve.sem_inc(sem("ssd_th_free"), 1)
                else:
                    h = k - 4
                    dve.wait_ge(sem("ssd_ztanh"), g * 2 + (h + 1))
                    dve.wait_ge(sem("ssd_zh"), g * 2 + (h + 1))
                    v = zs[par][:, 2 * h:2 * h + 2, :].rearrange("p t c -> p (t c)")
                    link(V.scalar_tensor_tensor(v, th[:, h, :], 1.0, v, ALU.add, ALU.mult))
                    dve.sem_inc(sem("ssd_zdone"), 1)

            def per_head(n, par, t=None):
                if t is None:
                    v = gs[par][:, n, :, :].rearrange("p t h -> p (t h)")
                    return v.unsqueeze(2).to_broadcast([P, TT * HPG, HEAD])
                return gs[par][:, n, t, :].unsqueeze(2).to_broadcast([P, HPG, HEAD])

            h16 = lambda v: v.rearrange("p t (h c) -> p (t h) c", c=HEAD)
            h4 = lambda v: v.rearrange("p (h c) -> p h c", c=HEAD)

            def ssd_core(k, g, par):
                if k == 0:
                    link(V.tensor_copy(gs[par][:, :, :, :].rearrange("p n t h -> p (n t) h"),
                                       dts[:, :, :, bass.ds(g * HPG, HPG)].rearrange("p n t h -> p (n t) h")))
                    dve.sem_inc(sem("ssd_gs"), 1)
                    dve.wait_ge(sem("ssd_xtok"), g + 1)
                    link(V.tensor_tensor(h16(xdt), h16(xtok), per_head(DT, par), ALU.mult))
                    dve.sem_inc(sem("ssd_x"), 1)
                    link.mark(V.tensor_tensor(h16(xdd), h16(xdt), per_head(DEC, par), ALU.mult))
                    link(V.tensor_tensor(h16(y), h16(xtok), per_head(DSK, par), ALU.mult))
                    dve.sem_inc(sem("ssd_x"), 1)
                if k <= 3:
                    t = k
                    dve.wait_ge(sem("ssd_rowb"), g * 4 + (t + 1))
                    for h in range(HPG):
                        link.mark(V.scalar_tensor_tensor(
                            lm[t % 2][:, h, :], ps[:, 2 + t % 2, h * P:(h + 1) * P],
                            gs[par][:, ACS, t, h:h + 1], cmask[:, :], ALU.subtract, ALU.min))
                    link.wait()
                    dve.sem_inc(sem("ssd_seg"), 1)
                    dve.sem_inc(sem("ssd_b23_free"), 1)
                if 1 <= k <= 4:
                    t = k - 1
                    dve.wait_ge(sem("ssd_y_p"), g * 4 + (t + 2))
                    yv = h4(y[:, t, :])
                    link(V.tensor_tensor(yv, yv, h4(ps[:, 6, 0:GW]), ALU.add))
                    if t > 0:
                        link(V.tensor_tensor(h4(ytmp), h4(ps[:, 6, GW:2 * GW]), per_head(ODEC, par, t), ALU.mult))
                        link(V.tensor_tensor(y[:, t, :], y[:, t, :], ytmp, ALU.add))
                    if t == 0:
                        link(V.tensor_copy(state, ps[:, 7, 0:GW]))
                    elif t < TT - 1:
                        link(V.tensor_tensor(h4(state), h4(state), per_head(CDEC, par, t), ALU.mult))
                        link(V.tensor_tensor(state, state, ps[:, 7, 0:GW], ALU.add))
                    if t < TT - 1:
                        dve.sem_inc(sem("ssd_state"), 1)
                    dve.sem_inc(sem("ssd_y_free"), 1)
                if k <= 3:
                    t = k
                    dve.wait_ge(sem("ssd_exp"), g * 4 + (t + 1))
                    dve.wait_ge(sem("ssd_cb"), g + 1)
                    V.tensor_tensor(lm[t % 2][:, :, :], lm[t % 2][:, :, :],
                                    ps[:, 5, t * P:(t + 1) * P].unsqueeze(1).to_broadcast([P, HPG, P]),
                                    ALU.mult).then_inc(sem("ssd_lm"), 1)
                if k == 4:
                    dve.wait_ge(sem("ssd_zdone"), g * 2 + 2)
                    flat2 = lambda v: v[:, :, :].rearrange("p t c -> p (t c)")
                    link(V.tensor_tensor(flat2(y), flat2(y), flat2(zs[par]), ALU.mult))
                    dve.sem_inc(sem("ssd_zs_free"), 1)
                    dve.sem_inc(sem("ssd_gated"), 1)
                    dve.wait_ge(sem("ssd_sq"), g + 1)
                    link(V.tensor_scalar(rtmp[:, 0, :], stats[:, 0:TT, 0], 1.0 / GW, EPS, ALU.mult, ALU.add))
                    root(rstd[:, :], rtmp[:, 0, :], rtmp[:, 1, :])
                    dve.sem_inc(sem("ssd_rstd"), 1)
                if k == 5:
                    dve.wait_ge(sem("ssd_y_p5"), g + 1)

            slots(dve, ssd_proj, ssd_core, 6, (link, 65))

            dve.wait_ge(sem("ssd_y_T"), 2 * SSD_GROUPS)
            V.memset(adas, 0.0).then_inc(sem("ada_sum"), 1)
            with dve.Fori(0, 4) as i:
                link.enter(i, 6 + 2 + 2 * ADA_N * KD)
                for u in range(2):
                    take_columns(ADA_MERGE, ADA_N, i * 2 + u, 4 * u + 3)
                    weigh_chunks(ADA_MERGE, ADA_N, i, u)
                    dve.wait_ge(sem("merge_t"), i * 4 + (2 * u + 2))
                    dve.wait_ge(used[ring.slot("merge", 2 * u)], ring.free("merge", 2 * u, i) + 1)
                    link(V.scalar_tensor_tensor(mg[:, u, 1, :], mg[:, u, 1, :], 1.0, ps[:, 4 * u + 2, :],
                                                ALU.add, ALU.mult))
                    dve.wait_ge(sem("merge_y"), i * 2 + (u + 1))
                    link(V.scalar_tensor_tensor(mg[:, u, 0, :], mg[:, u, 0, :], 1.0, ps[:, 4 * u + 3, :],
                                                ALU.add, ALU.mult))
                    link(V.tensor_tensor(mergedT[:, bass.ds(i * 2 + u, 1), :], mg[:, u, 0, :], mg[:, u, 1, :],
                                         ALU.add))
                    dve.sem_inc(sem("merge_used"), 1)
                    dve.sem_inc(sem("merge_free"), 1)
                link.leave(4)
            take_columns(ADA_MERGE, ADA_N, 8, 3)
            link(V.tensor_tensor(mod[:, 48:144], modx[:, ADA_C:9 * ADA_C], pcol[:, 1, 0:96], ALU.add))
            for c in (56, 80, 104, 128):
                link.mark(V.tensor_scalar(mod[:, c:c + 16], mod[:, c:c + 16], 1.0, None, ALU.add))
            link.wait()

            def residual(n, alpha, more=None, then=None):
                dve.wait_ge(sem("ln_in"), 32 * (n + 1))
                for t in range(TT):
                    dve.wait_ge(sem("res_b"), TT * n + t + 1)
                    link.mark(V.scalar_tensor_tensor(xr[:, t, :], xr[:, t, :], alpha,
                                                     ps[:, 2 * t:2 * t + 2, :].rearrange("p b c -> p (b c)"),
                                                     ALU.mult, ALU.add))
                link.wait()
                dve.sem_inc(sem("res_read"), 1)
                for t in range(TT + 1):
                    if t < TT:
                        if more is not None:
                            link(V.tensor_tensor(xr[:, t, :], xr[:, t, :], more(t), ALU.add))
                        moments(t, xr)
                        link(V.scalar_tensor_tensor(rtmp[:, 1, t:t + 1], mv[:, t, 0:1], -1.0, rstd[:, t:t + 1],
                                                    ALU.mult, ALU.mult))
                        dve.sem_inc(sem("res_stats"), 1)
                    if t > 0:
                        dve.wait_ge(sem("res_norm"), TT * n + t)
                        link(V.tensor_tensor(xr[:, t - 1, :], xr[:, t - 1, :], lngb[:, 0, :], ALU.mult))
                        V.tensor_tensor(xr[:, t - 1, :], xr[:, t - 1, :], lngb[:, 1, :],
                                        ALU.add).then_inc(sem("res_x"), 1)
                        if then is not None:
                            then(t - 1)

            def second_norm(t):
                dve.wait_ge(sem("res_x"), t + 1)
                layer_norm(t, xr, xhat).then_inc(sem("ln1_x"), 1)

            dve.wait_ge(sem("x_in"), 32)
            residual(0, ALPHA_1, then=second_norm)

            e3 = lambda n: rt[:, n, :, :]
            e2 = lambda n: rt[:, n, :, :].rearrange("p t e -> p (t e)")
            dve.wait_ge(sem("router_e"), 1)
            link(V.tensor_scalar(e2(0), e2(0), 1.0, None, ALU.add))
            link(V.reciprocal(e2(0), e2(0)))
            link(V.tensor_tensor(e3(1), e3(0), rbias.unsqueeze(1).to_broadcast([P, TT, N_EXPERTS]), ALU.add))
            for t in range(TT):
                for g in range(8):
                    link.mark(V.max(top[:, t, 8 * g:8 * g + 8], rt[:, 1, t, 8 * g:8 * g + 8]))
            link(V.memset(r16.rearrange("p a t e -> p (a t e)"), GONE))
            pair = top.rearrange("p t (g r) -> p t g r", r=8)
            for t in range(TT):
                link.mark(V.tensor_tensor(r16[:, 0, t, 0:8], pair[:, t, :, 0], pair[:, t, :, 1], ALU.add))
            link.wait()
            for t in range(TT):
                link(V.max(m8[:, :], r16[:, 0, t, 0:8]))
                link(V.tensor_copy(r16[:, 1, t, 0:4], m8[:, 0:4]))
                link(V.match_replace(r16[:, 0, t, :], r16[:, 1, t, 0:8], r16[:, 0, t, :], FOUND))
            for t in range(TT):
                link.mark(V.tensor_scalar(r16[:, 1, t, 8:16], r16[:, 0, t, 0:8], FOUND, NEG, ALU.not_equal, ALU.mult))
            link.wait()
            for t in range(TT):
                link.mark(V.tensor_tensor(rt[:, 2, t, :].rearrange("p (g e) -> p g e", e=8),
                                          rt[:, 1, t, :].rearrange("p (g e) -> p g e", e=8),
                                          r16[:, 1, t, 8:16].unsqueeze(2).to_broadcast([P, 8, 8]), ALU.add))
            link.wait()
            for t in range(TT):
                link(V.max(m8[:, :], rt[:, 2, t, :]))
                link(V.match_replace(rt[:, 3, t, :], m8[:, :], rt[:, 2, t, :], FOUND))
            link(V.tensor_scalar(e2(2), e2(3), FOUND, None, ALU.is_equal))
            dve.sem_inc(sem("route_v"), 1)
            link(V.tensor_tensor(e2(4), e2(2), e2(0), ALU.mult))
            for t in range(TT):
                link.mark(V.reduce_sum(mv[:, t, 0:1], rt[:, 4, t, :], AX_X))
            link.wait()
            link(V.reciprocal(mv[:, :, 1], mv[:, :, 0]))
            for t in range(TT):
                link(V.tensor_scalar(rt[:, 5, t, :], rt[:, 4, t, :], mv[:, t, 1:2], 0.5 * ROUTED_SCALE,
                                     ALU.mult, ALU.mult))

            for f in range(FE):
                dve.wait_ge(sem("sh_t"), f + 1)
                if f < FE - 1:
                    dve.wait_ge(sem("sh_gu"), 2 * f + 2)
                else:
                    dve.wait_ge(used[0], ring.free("shared", 0, 0) + 1)
                link(V.scalar_tensor_tensor(tg[:, f, :], tg[:, f, :], 1.0, ps[:, 4 + 2 * f, :], ALU.add, ALU.mult))
                link(V.scalar_tensor_tensor(hexp[:, f, :], tg[:, f, :], 0.5, ps[:, 5 + 2 * f, :], ALU.mult, ALU.mult))
                dve.sem_inc(sem("sh_h"), 1)

            dve.wait_ge(sem("route_p"), ROUTE_P["counts_p"])
            total = ps[:, 1, TT * N_EXPERTS:(TT + 1) * N_EXPERTS]
            for n in range(2):
                link.mark(V.memset(scan[n], 0.0))
            link(V.tensor_scalar(nblk, total, 0.0, None, ALU.is_gt))
            for m in range(1, TT):
                link(V.scalar_tensor_tensor(nblk, total, float(BLOCK * m), nblk, ALU.is_gt, ALU.add))
            link(V.tensor_copy(scan[0][:, 32:96], nblk))
            for m in range(6):
                src, dst, s = scan[m % 2], scan[1 - m % 2], 1 << m
                link(V.tensor_tensor(dst[:, 32:96], src[:, 32:96], src[:, 32 - s:96 - s], ALU.add))
            link(V.tensor_scalar(spare, scan[0][:, 95:96], -1.0, float(NBLK), ALU.mult, ALU.add))
            link.mark(V.tensor_scalar(pendc, spare, -2.0, 0.0, ALU.add, ALU.max))
            link(V.tensor_scalar(scan[0][:, 32:96], scan[0][:, 32:96], spare, None, ALU.add))
            link(V.tensor_scalar(idle_i.bitcast(I32), pendc, 0.5, -0.25, ALU.mult, ALU.add))
            dve.sem_inc(sem("route_v"), 1)
            link(V.tensor_tensor(first, scan[0][:, 32:96], nblk, ALU.subtract))
            link(V.tensor_scalar(first, first, float(BLOCK), None, ALU.mult))
            link(V.tensor_tensor(e3(1), ps[:, 1, 0:TT * N_EXPERTS].rearrange("p (t e) -> p t e", t=TT),
                                 first.unsqueeze(1).to_broadcast([P, TT, N_EXPERTS]), ALU.add))
            link(V.tensor_tensor(e2(1), e2(1), e2(2), ALU.mult))
            for t in range(TT):
                link.mark(V.max(key8[:, t, :], rt[:, 1, t, :]))
            link.wait()
            link(V.tensor_scalar(slot_i.bitcast(I32), key8, -1.0, None, ALU.add))
            dve.sem_inc(sem("route_v"), 1)
            dve.wait_ge(sem("route_p"), ROUTE_P["ends_p"])
            link(V.tensor_copy(pendc[0:N_EXPERTS, :], ps[0:N_EXPERTS, 2, 0:1]))
            dve.wait_ge(sem("count_in"), 32)
            V.tensor_scalar(past_e[0:N_EXPERTS, :], cnt_f[0:N_EXPERTS, :], pendc[0:N_EXPERTS, :], None,
                            ALU.is_ge).then_inc(sem("route_v"), 1)
            dve.wait_ge(sem("route_p"), ROUTE_P["blk_p"])
            V.tensor_scalar(blk_e.bitcast(I32), ps[:, 2, 0:NBLK], float(N_EXPERTS - 1), None,
                            ALU.min).then_inc(sem("route_v"), 1)
            for t in range(TT):
                for j in range(PER_TOKEN):
                    link.mark(V.scalar_tensor_tensor(mine[:, PER_TOKEN * t + j, :], rt[:, 1, t, :], key8[:, t, j:j + 1],
                                                     rt[:, 5, t, :], ALU.is_equal, ALU.mult))
            link.wait()
            link(V.reduce_sum(gate8.rearrange("p t j -> p (t j)"), mine, AX_X))
            dve.wait_ge(sem("route_p"), ROUTE_P["rows_p"])
            V.tensor_copy(row_i.bitcast(I32), ps[:, 2, 0:NBLK]).then_inc(sem("route_v"), 1)

            def block_h(u, turn):
                dve.wait_ge(sem("moe_t"), turn * 2 + (u + 1))
                link(V.scalar_tensor_tensor(tge, tge, 1.0, ps[:, 2, 0:FE * BLOCK], ALU.add, ALU.mult))
                dve.wait_ge(used[ring.slot("moe", 2 * u)], ring.free("moe", 2 * u, turn) + 1)
                V.tensor_tensor(he[u].rearrange("p f b -> p (f b)"), tge, ps[:, 3, 0:FE * BLOCK],
                                ALU.mult).then_inc(sem("moe_h"), 1)

            def block_y(u, turn):
                dve.wait_ge(sem(f"y_out{u}"), turn * 16 + 16)
                dve.wait_ge(used[ring.slot("moe", 2 * u + 1)], ring.free("moe", 2 * u + 1, turn) + 1)
                V.tensor_copy(ybuf[u][:, 512:1024], ps[:, 5 + 2 * u, :]).then_inc(sem("moe_y1"), 1)

            block_h(0, 0)
            idle = turns_without_rows(dve)
            with dve.Fori(0, LAST) as i:
                link.enter(i, 2)
                with dve.If(i >= idle):
                    block_y(0, i)
                    block_h(1, i)
                    block_y(1, i)
                    block_h(0, i + 1)
                link.k = 0
                with dve.Else():
                    dve.wait_ge(sem("moe_t"), i * 2 + 3)
                    dve.wait_ge(used[ring.slot("moe", 2)], ring.free("moe", 2, i) + 1)
                    dve.sem_inc(sem("dve_link"), 2)
                    link.k += 2
                    dve.sem_inc(sem("moe_h"), 2)
                    dve.sem_inc(sem("moe_y1"), 2)
                link.leave(LAST)
            block_y(0, LAST)
            block_h(1, LAST)
            block_y(1, LAST)
            dve.sem_inc(sem("moe_out"), 1)

            dve.wait_ge(sem("g2_moved"), 32)

            def combined(t):
                for j in range(PER_TOKEN):
                    n = t * PER_TOKEN + j
                    dve.wait_ge(sem(YG_IN[n % 4]), 16 * (n // 4 + 1))
                    if j == 0:
                        ins = V.tensor_scalar(routed[:, t, :], yg[n % 4], gate8[:, t, j:j + 1], None, ALU.mult)
                    else:
                        dve.wait_ge(sem("summed"), n)
                        ins = V.scalar_tensor_tensor(routed[:, t, :], yg[n % 4], gate8[:, t, j:j + 1],
                                                     routed[:, t, :], ALU.mult, ALU.add)
                    ins.then_inc(sem("summed"), 1)
                dve.wait_ge(sem("summed"), n + 1)
                link(V.tensor_tensor(routed[:, t, :], routed[:, t, :], g2row, ALU.mult))
                return routed[:, t, :]

            residual(1, ALPHA_1, combined)

            dve.wait_ge(sem("index_p"), INDEX_P["iw_p"])
            link(V.tensor_scalar(iws[:, :, :].rearrange("p t h -> p (t h)"), ps[:, 2, 0:TT * IDX_HEADS],
                                 IDX_HEADS ** -0.5 * IDX_DIM ** -0.5, None, ALU.mult))
            dve.wait_ge(sem("ckv_sq"), 1)
            link(V.tensor_scalar(rtmp[:, 0, :], stats[:, 0:TT, 0], 1.0 / KV_RANK, EPS, ALU.mult, ALU.add))
            root(rstd[:, :], rtmp[:, 0, :], rtmp[:, 1, :])
            dve.sem_inc(sem("ckv_rstd"), 1)
            link(V.memset(selm[:, 0, :], 0.0))
            n = 0
            dve.wait_ge(sem("cmaskq"), 1)
            for qb in range(1, TT):
                w = (qb + 1) * P
                score = selm[:, qb, 0:w]
                for h in range(IDX_HEADS):
                    dve.wait_ge(sem("idx_free"), 4 + n + 1)
                    if h == 0:
                        link(V.tensor_scalar(score, rl[:, n % 2, 0:w], iws[:, qb, h:h + 1], None, ALU.mult))
                    else:
                        link(V.scalar_tensor_tensor(score, rl[:, n % 2, 0:w], iws[:, qb, h:h + 1], score,
                                                    ALU.mult, ALU.add))
                    dve.sem_inc(sem("idx_s"), 1)
                    n += 1
            for qb in range(1, TT):
                w = (qb + 1) * P
                score = selm[:, qb, 0:w]
                link(V.tensor_tensor(score[:, qb * P:w], score[:, qb * P:w], cmaskq[:, :], ALU.add))
                for _ in range(TOPK // 8):
                    link(V.max(m8[:, :], score))
                    link(V.match_replace(score, m8[:, :], score, GONE))
                link(V.tensor_scalar(score, score, GONE, NEG, ALU.not_equal, ALU.mult))

            def attention(tag):
                dsa = tag == "dsa"
                past = NO_PAST if dsa else DSA_PAST

                def proj(k, g, par, turn):
                    pass

                def norm(n, g):
                    qb, m = n // 2, n % 2
                    v = lbuf[:, n % 4, 0:(qb + 1) * P]
                    dve.wait_ge(sem("att_p"), g * 8 + (n + 1) + past["p"])
                    link(V.reciprocal(rsum[:, n:n + 1], rsum[:, n:n + 1]))
                    if dsa:
                        V.tensor_scalar(v, v, rsum[:, n:n + 1], None, ALU.mult).then_inc(sem("att_pn"), 1)
                    elif m == 0:
                        link(V.tensor_scalar(v, v, rsum[:, n:n + 1], None, ALU.mult))
                    else:
                        link(V.tensor_scalar(rsum[:, n:n + 1], rsum[:, n:n + 1], lamv[:, 3:4], None, ALU.mult))
                        V.scalar_tensor_tensor(v, v, rsum[:, n:n + 1], lbuf[:, (n - 1) % 4, 0:(qb + 1) * P],
                                               ALU.mult, ALU.add).then_inc(sem("att_pn"), 1)

                def core(k, g, par):
                    if k < 8:
                        qb, m = k // 2, k % 2
                        w = (qb + 1) * P
                        v = lbuf[:, k % 4, 0:w]
                        dve.wait_ge(sem("att_s"), g * 8 + (k + 1) + past["s"])
                        if k == 0:
                            dve.wait_ge(sem(f"strip_in{par}"), (g >> 1) * 16 + 16 + past["strip_in"])
                        if dsa:
                            dve.wait_ge(sem("att_tr"), g * 8 + (k + 1) + past["tr"])
                        elif m:
                            dve.wait_ge(sem("att_tr"), g * 4 + (k + 1) // 2 + past["tr"])
                        link(V.scalar_tensor_tensor(v, ps[:, k % 2, 0:w], HEAD ** -0.5,
                                                    strip[par][:, m, T - w:T], ALU.mult, ALU.add))
                        dve.sem_inc(sem("att_s_free"), 1)
                        if dsa and qb:
                            link(V.tensor_tensor(v, v, selm[:, qb, 0:w], ALU.add))
                        V.tensor_reduce(nmax[:, k:k + 1], v, AX_X, ALU.max, negate=True).then_inc(sem("att_l"), 1)
                        if k == 7:
                            dve.sem_inc(sem("att_strip_free"), 1)
                    if 1 <= k < 9:
                        norm(k - 1, g)
                    if k == 11 and not dsa:
                        dve.wait_ge(sem("diff_osq"), g + 1)
                        link(V.tensor_scalar(ortmp[:, 0, :], osq[:, :], 1.0 / P, EPS, ALU.mult, ALU.add))
                        root(ortmp[:, 2, :], ortmp[:, 0, :], ortmp[:, 1, :])
                        dve.sem_inc(sem("diff_rstd"), 1)

                slots(dve, proj, core, 12, (link, 22 if dsa else 35))

            attention("dsa")
            residual(2, ALPHA_2)

            def mlp(layer):
                with dve.Fori(0, 2) as i:
                    for n in range(16):
                        dve.wait_ge(sem("up_free"), i * 16 + (32 * layer + n + 1 + 8))
                        v = h1T[:, bass.ds(i * 16 + n, 1), :]
                        V.tensor_tensor(v, v, v, ALU.mult).then_inc(sem("up_squared"), 1)
                residual(3 + 2 * layer, ALPHA_2)

            mlp(0)
            attention("diff")
            residual(4, ALPHA_2)
            mlp(1)


def kernel(**inputs):
    import concourse.bacc as bacc
    from concourse.bass_utils import run_bass_kernel_spmd

    nc = bacc.Bacc("TRN2", target_bir_lowering=False, num_devices=1)
    arrays, aps = {}, {}
    for name in INPUTS:
        v = np.ascontiguousarray(inputs[name])
        arrays["in_" + name] = v
        aps[name] = nc.dram_tensor("in_" + name, v.shape, F32, kind="ExternalInput").ap()
    arrays["bucket_onehot"] = bucket_onehot()
    onehot = nc.dram_tensor("bucket_onehot", arrays["bucket_onehot"].shape, F32, kind="ExternalInput").ap()
    arrays["counting"] = counting_rows()
    counting = nc.dram_tensor("counting", (P, TT + NBLK), F32, kind="ExternalInput").ap()
    out = nc.dram_tensor("out", (1, T, D), F32, kind="ExternalOutput").ap()
    program(nc, aps, onehot, counting, out)
    r = run_bass_kernel_spmd(nc, [arrays], core_ids=[0])
    return r.results[0]["out"]
```
